# Optimizing a Trainium2 kernel written in Bass

```python
import jax, jax.numpy as jnp
from jax import lax
import numpy as np

D_MODEL = 1024
BATCH = 1
SEQ = 2048
DEPTH = 2
DEC_BATCH = 8
DEC_SEQ = 8
PAST_LEN = 8192
PAGE_SIZE = 128

N_EVEN = (DEPTH + 1) // 2
N_ODD = DEPTH // 2
A_WIDTH = D_MODEL // 2
A_HEAD_DIM = 64
A_HEADS = A_WIDTH // A_HEAD_DIM
A_DECAY_RANK = 64
A_ICLR_RANK = 64
A_SHIFT_W = 3 * A_WIDTH + A_DECAY_RANK + A_ICLR_RANK
GN_EPS = 64e-5
B_WIDTH = D_MODEL // 2
CONV_W = 3
EVEN_IN_W = A_SHIFT_W + A_WIDTH + 4 * B_WIDTH
EVEN_MIX_W = A_WIDTH + B_WIDTH
C_GROUPS = ((128, 1), (512, 4), (2048, 16))
N_C_GROUPS = len(C_GROUPS)
C_HEADS = 8
C_HEAD_DIM = 64
C_WIDTH = C_HEADS * C_HEAD_DIM
C_QKV_W = 3 * N_C_GROUPS * C_WIDTH
ODD_IN_W = C_QKV_W + C_WIDTH
ATTN_BLOCK = 128
LN_EPS = 1e-5
DEEPNORM_ALPHA = (2 * DEPTH) ** 0.25
DEEPNORM_BETA = (8 * DEPTH) ** -0.25

kernel_name = 'hybrid_rwkv7_shortconv_dilated_swa_step'

def layer_norm(x, g, b):
    xf = x.astype(jnp.float32)
    mu = jnp.mean(xf, -1, keepdims=True)
    var = jnp.mean(jnp.square(xf - mu), -1, keepdims=True)
    return ((xf - mu) * lax.rsqrt(var + LN_EPS) * g + b).astype(x.dtype)

def wkv7_scan(r, decay, k, v, kk, a, s0):
    def step(S, inp):
        r_t, w_t, k_t, v_t, kk_t, a_t = inp
        sa = jnp.einsum('bhij,bhj->bhi', S, -kk_t)
        S = (S * w_t[:, :, None, :] + sa[..., None] * (kk_t * a_t)[:, :, None, :]
             + v_t[..., None] * k_t[:, :, None, :])
        return S, jnp.einsum('bhij,bhj->bhi', S, r_t)
    xs = tuple(jnp.moveaxis(t, 1, 0) for t in (r, decay, k, v, kk, a))
    s_final, ys = lax.scan(step, s0, xs)
    return jnp.moveaxis(ys, 0, 1), s_final

def rwkv7_mix(p, shift_prev, s0, mu, w0, w2, a0, a2, k_k, k_a, r_k, gn_g, gn_b):
    Bn, T, _ = p.shape
    prev = jnp.concatenate([shift_prev[:, None, :], p[:, :-1]], axis=1)
    ps = (p + (prev - p) * mu).astype(jnp.float32)
    r, k, v, wl, al = jnp.split(ps, [A_WIDTH, 2 * A_WIDTH, 3 * A_WIDTH, 3 * A_WIDTH + A_DECAY_RANK], axis=-1)
    w = -jax.nn.softplus(-(w0 + jnp.tanh(wl) @ w2)) - 0.5
    decay = jnp.exp(-jnp.exp(w))
    a = jax.nn.sigmoid(a0 + al @ a2)
    heads = lambda t: t.reshape(Bn, T, A_HEADS, A_HEAD_DIM)
    kk = heads(k * k_k)
    kk = kk * lax.rsqrt(jnp.maximum(jnp.sum(jnp.square(kk), -1, keepdims=True), 1e-24))
    k = k * (1.0 + (a - 1.0) * k_a)
    r, k, v, decay, a = heads(r), heads(k), heads(v), heads(decay), heads(a)
    y, s_new = wkv7_scan(r, decay, k, v, kk, a, s0.astype(jnp.float32))
    mean = jnp.mean(y, -1, keepdims=True)
    var = jnp.mean(jnp.square(y - mean), -1, keepdims=True)
    y = (y - mean) * lax.rsqrt(var + GN_EPS)
    y = y * gn_g.reshape(A_HEADS, A_HEAD_DIM) + gn_b.reshape(A_HEADS, A_HEAD_DIM)
    y = y + jnp.sum(r * k * r_k, -1, keepdims=True) * v
    return y.reshape(Bn, T, A_WIDTH), p[:, -1], s_new

def short_conv_mix(p, conv_prev, conv_w):
    b, c, h = jnp.split(p, 3, axis=-1)
    u = c * h
    T = u.shape[1]
    ucat = jnp.concatenate([conv_prev.astype(u.dtype), u], axis=1)
    y = sum(conv_w[j] * ucat[:, j:j + T] for j in range(CONV_W))
    return b * y, ucat[:, -(CONV_W - 1):]

def even_mix(x, shift_prev, s0, conv_prev, w_in, w_out, rw, conv_w):
    p = x @ w_in
    pA, zA, pB, zB = jnp.split(p, [A_SHIFT_W, A_SHIFT_W + A_WIDTH, A_SHIFT_W + A_WIDTH + 3 * B_WIDTH], axis=-1)
    yA, shift_new, s_new = rwkv7_mix(pA, shift_prev, s0, *rw)
    yB, conv_new = short_conv_mix(pB, conv_prev, conv_w)
    y = jnp.concatenate([yA.astype(x.dtype) * jax.nn.silu(zA), yB * jax.nn.silu(zB)], axis=-1) @ w_out
    return y, shift_new, s_new, conv_new

def dilated_window_attn_prompt(q, k, v, window, dilation):
    Bn, S, H, hd = q.shape
    nj = window // dilation
    L = S // dilation
    nb = -(-L // ATTN_BLOCK)
    Lp = nb * ATTN_BLOCK
    N = Bn * dilation
    def to_sub(t):
        t = t.reshape(Bn, L, dilation, H, hd).transpose(0, 2, 1, 3, 4).reshape(N, L, H, hd)
        return jnp.pad(t, ((0, 0), (0, Lp - L), (0, 0), (0, 0)))
    def band(t):
        tb = jnp.pad(t, ((0, 0), (ATTN_BLOCK, 0), (0, 0), (0, 0))).reshape(N, nb + 1, ATTN_BLOCK, H, hd)
        return jnp.concatenate([tb[:, :-1], tb[:, 1:]], axis=2)
    qb = to_sub(q).reshape(N, nb, ATTN_BLOCK, H, hd)
    kb, vb = band(to_sub(k)), band(to_sub(v))
    s = jnp.einsum('ncqhd,nckhd->nchqk', qb, kb, preferred_element_type=jnp.float32) * (hd ** -0.5)
    qi = jnp.arange(ATTN_BLOCK)[:, None]
    ki = jnp.arange(2 * ATTN_BLOCK)[None, :]
    dist = qi + ATTN_BLOCK - ki
    kpos = (jnp.arange(nb)[:, None, None] - 1) * ATTN_BLOCK + ki[None]
    mask = (dist >= 0) & (dist <= nj) & (kpos >= 0)
    s = jnp.where(mask[None, :, None], s, -jnp.inf)
    m = jnp.max(s, -1, keepdims=True)
    e = jnp.exp(s - m)
    den = jnp.sum(e, -1, keepdims=True)
    o = jnp.einsum('nchqk,nckhd->ncqhd', e / den, vb.astype(jnp.float32))
    lse = (m + jnp.log(den))[..., 0].transpose(0, 1, 3, 2)
    o = o.reshape(N, Lp, H, hd)[:, :L].reshape(Bn, dilation, L, H, hd).transpose(0, 2, 1, 3, 4).reshape(Bn, S, H, hd)
    lse = lse.reshape(N, Lp, H)[:, :L].reshape(Bn, dilation, L, H).transpose(0, 2, 1, 3).reshape(Bn, S, H)
    return o, lse

def dilated_window_attn_sample(q, k, v, kv_buf, window, dilation):
    Bn, T, H, hd = q.shape
    Wb = kv_buf.shape[1]
    nj = window // dilation
    kcat = jnp.concatenate([kv_buf[:, :, 0].astype(k.dtype), k], axis=1)
    vcat = jnp.concatenate([kv_buf[:, :, 1].astype(v.dtype), v], axis=1)
    idx = Wb + jnp.arange(T)[:, None] - dilation * jnp.arange(nj + 1)[None, :]
    valid = idx >= 0
    idxc = jnp.maximum(idx, 0)
    kg, vg = kcat[:, idxc], vcat[:, idxc]
    s = jnp.einsum('bthd,btjhd->bthj', q, kg, preferred_element_type=jnp.float32) * (hd ** -0.5)
    s = jnp.where(valid[None, :, None, :], s, -jnp.inf)
    m = jnp.max(s, -1, keepdims=True)
    e = jnp.exp(s - m)
    den = jnp.sum(e, -1, keepdims=True)
    o = jnp.einsum('bthj,btjhd->bthd', e / den, vg.astype(jnp.float32))
    lse = (m + jnp.log(den))[..., 0]
    keep = min(window, Wb + T)
    new_buf = jnp.stack([kcat, vcat], axis=2)[:, Wb + T - keep:]
    return o, lse, new_buf

def odd_mix(x, kv_bufs, w_in, w_out):
    Bn, T, _ = x.shape
    p = x @ w_in
    qkv = p[..., :C_QKV_W].reshape(Bn, T, 3, N_C_GROUPS, C_HEADS, C_HEAD_DIM)
    z = p[..., C_QKV_W:]
    outs, lses, new_bufs = [], [], []
    for g, (window, dilation) in enumerate(C_GROUPS):
        q, k, v = qkv[:, :, 0, g], qkv[:, :, 1, g], qkv[:, :, 2, g]
        if kv_bufs is None:
            o, lse = dilated_window_attn_prompt(q, k, v, window, dilation)
            keep = min(window, T)
            nbuf = jnp.stack([k, v], axis=2)[:, T - keep:]
        else:
            o, lse, nbuf = dilated_window_attn_sample(q, k, v, kv_bufs[g], window, dilation)
        outs.append(o)
        lses.append(lse)
        new_bufs.append(nbuf)
    alpha = jax.nn.softmax(jnp.stack(lses, axis=2), axis=2)
    o = jnp.sum(alpha[..., None] * jnp.stack(outs, axis=2), axis=2)
    y = o.reshape(Bn, T, C_WIDTH).astype(x.dtype) * jax.nn.silu(z)
    return y @ w_out, new_bufs

def setup_inputs(seed: int = 0) -> dict:
    key = jax.random.key(seed)
    ks = jax.random.split(key, 32)
    nrm = lambda k, shape, s: jax.random.normal(k, shape, jnp.float32) * s
    kv_shape = lambda w: (N_ODD, DEC_BATCH, min(w, PAST_LEN), 2, C_HEADS, C_HEAD_DIM)
    return {
        'x_prompt': nrm(ks[0], (BATCH, SEQ, D_MODEL), 1.0),
        'x_sample': nrm(ks[1], (DEC_BATCH, DEC_SEQ, D_MODEL), 1.0),
        'state_rwkv': nrm(ks[2], (N_EVEN, DEC_BATCH, A_HEADS, A_HEAD_DIM, A_HEAD_DIM), 0.1),
        'state_shift': nrm(ks[3], (N_EVEN, DEC_BATCH, A_SHIFT_W), 1.0),
        'state_conv': nrm(ks[4], (N_EVEN, DEC_BATCH, CONV_W - 1, B_WIDTH), 1.0),
        'cache_kv_w128': nrm(ks[5], kv_shape(128), 1.0),
        'cache_kv_w512': nrm(ks[6], kv_shape(512), 1.0),
        'cache_kv_w2048': nrm(ks[7], kv_shape(2048), 1.0),
        'even_w_in': nrm(ks[8], (N_EVEN, D_MODEL, EVEN_IN_W), D_MODEL ** -0.5),
        'even_w_out': nrm(ks[9], (N_EVEN, EVEN_MIX_W, D_MODEL), EVEN_MIX_W ** -0.5 * DEEPNORM_BETA),
        'rwkv_mu': jax.random.uniform(ks[10], (N_EVEN, A_SHIFT_W), jnp.float32),
        'rwkv_w0': -1.0 + nrm(ks[11], (N_EVEN, A_WIDTH), 0.5),
        'rwkv_w2': nrm(ks[12], (N_EVEN, A_DECAY_RANK, A_WIDTH), 0.1),
        'rwkv_a0': nrm(ks[13], (N_EVEN, A_WIDTH), 0.1),
        'rwkv_a2': nrm(ks[14], (N_EVEN, A_ICLR_RANK, A_WIDTH), 0.1),
        'rwkv_k_k': 0.85 + nrm(ks[15], (N_EVEN, A_WIDTH), 0.02),
        'rwkv_k_a': 1.0 + nrm(ks[16], (N_EVEN, A_WIDTH), 0.02),
        'rwkv_r_k': nrm(ks[17], (N_EVEN, A_HEADS, A_HEAD_DIM), 0.1),
        'rwkv_gn_g': 1.0 + nrm(ks[18], (N_EVEN, A_WIDTH), 0.02),
        'rwkv_gn_b': nrm(ks[19], (N_EVEN, A_WIDTH), 0.02),
        'conv_w': nrm(ks[20], (N_EVEN, CONV_W, B_WIDTH), CONV_W ** -0.5),
        'odd_w_in': nrm(ks[21], (N_ODD, D_MODEL, ODD_IN_W), D_MODEL ** -0.5),
        'odd_w_out': nrm(ks[22], (N_ODD, C_WIDTH, D_MODEL), C_WIDTH ** -0.5 * DEEPNORM_BETA),
        'ln_g': 1.0 + nrm(ks[23], (DEPTH, D_MODEL), 0.02),
        'ln_b': nrm(ks[24], (DEPTH, D_MODEL), 0.02),
    }

def reference(x_prompt, x_sample, state_rwkv, state_shift, state_conv, cache_kv_w128, cache_kv_w512,
              cache_kv_w2048, even_w_in, even_w_out, rwkv_mu, rwkv_w0, rwkv_w2, rwkv_a0, rwkv_a2,
              rwkv_k_k, rwkv_k_a, rwkv_r_k, rwkv_gn_g, rwkv_gn_b, conv_w, odd_w_in, odd_w_out, ln_g, ln_b):
    xp, xs = x_prompt, x_sample
    Bp = xp.shape[0]
    caches = (cache_kv_w128, cache_kv_w512, cache_kv_w2048)
    rwkv_p, rwkv_s, shift_p, shift_s, conv_p, conv_s = [], [], [], [], [], []
    kv_p = [[] for _ in range(N_C_GROUPS)]
    kv_s = [[] for _ in range(N_C_GROUPS)]
    for li in range(DEPTH):
        j = li // 2
        if li % 2 == 0:
            rw = (rwkv_mu[j], rwkv_w0[j], rwkv_w2[j], rwkv_a0[j], rwkv_a2[j], rwkv_k_k[j],
                  rwkv_k_a[j], rwkv_r_k[j], rwkv_gn_g[j], rwkv_gn_b[j])
            yp, sh_new, s_new, cv_new = even_mix(
                xp, jnp.zeros((Bp, A_SHIFT_W), xp.dtype),
                jnp.zeros((Bp, A_HEADS, A_HEAD_DIM, A_HEAD_DIM), jnp.float32),
                jnp.zeros((Bp, CONV_W - 1, B_WIDTH), xp.dtype),
                even_w_in[j], even_w_out[j], rw, conv_w[j])
            rwkv_p.append(s_new); shift_p.append(sh_new); conv_p.append(cv_new)
            ys, sh_new, s_new, cv_new = even_mix(
                xs, state_shift[j], state_rwkv[j], state_conv[j],
                even_w_in[j], even_w_out[j], rw, conv_w[j])
            rwkv_s.append(s_new); shift_s.append(sh_new); conv_s.append(cv_new)
        else:
            yp, bufs_p = odd_mix(xp, None, odd_w_in[j], odd_w_out[j])
            ys, bufs_s = odd_mix(xs, tuple(c[j] for c in caches), odd_w_in[j], odd_w_out[j])
            for g in range(N_C_GROUPS):
                kv_p[g].append(bufs_p[g])
                kv_s[g].append(bufs_s[g])
        xp = layer_norm(DEEPNORM_ALPHA * xp + yp, ln_g[li], ln_b[li])
        xs = layer_norm(DEEPNORM_ALPHA * xs + ys, ln_g[li], ln_b[li])
    return (xp, xs,
            jnp.stack(rwkv_p), jnp.stack(rwkv_s),
            jnp.stack(shift_p), jnp.stack(shift_s),
            jnp.stack(conv_p), jnp.stack(conv_s),
            jnp.stack(kv_p[0]), jnp.stack(kv_s[0]),
            jnp.stack(kv_p[1]), jnp.stack(kv_s[1]),
            jnp.stack(kv_p[2]), jnp.stack(kv_s[2]))


_drawn_inputs = setup_inputs


def setup_inputs(seed=0):
    import zlib

    import numpy as np

    out = dict(_drawn_inputs(seed))
    spreads = {}
    factors = {}
    for name, (base, spread) in spreads.items():
        noise = np.random.default_rng([zlib.crc32(name.encode()), seed]).standard_normal(out[name].shape)
        drawn = base * np.exp(spread * noise) if base else spread * noise
        out[name] = __import__('jax').numpy.asarray(drawn.astype(out[name].dtype))
    for name, factor in factors.items():
        out[name] = (out[name] * factor).astype(out[name].dtype)
    return out
```

```python
import concourse.bass as bass
from concourse import mybir
from contextlib import ExitStack

FP32 = mybir.dt.float32
ALU = mybir.AluOpType
ACT = mybir.ActivationFunctionType
AX = mybir.AxisListType

P = 128
D = 1024
KD = D // P
SEQ = 2048
NPT = SEQ // P
DB, DT = 8, 8
NS = DB * DT
NTOK = SEQ + NS
NTILE = NPT + 1
PAIRS = NPT // 2
H, HD = 8, 64
AW = H * HD
SHIFT_W = 3 * AW + 2 * HD
EVEN_W = SHIFT_W + AW + 4 * AW
NG = 3
ODD_W = 3 * NG * AW + AW
PAD = 2
R0, K0, V0, L0, ZA0, B0, C0, HH0, ZB0 = 0, AW, 2 * AW, 3 * AW, SHIFT_W, SHIFT_W + AW, SHIFT_W + 2 * AW, \
    SHIFT_W + 3 * AW, SHIFT_W + 4 * AW
SLOTS = 2


def each_tile(eng, body, tail=True):
    with eng.Fori(0, PAIRS) as i:
        for s in range(SLOTS):
            body(2 * i + s, s, i)
    if tail:
        body(NPT, 0, PAIRS)


class Sems(dict):

    def __init__(self, nc, ctx, phase, names, own={}):
        self.nc, self.own = nc, own
        self.update(own)
        for n in names.split():
            self[n] = ctx.enter_context(nc.semaphore(f"{phase}_{n}"))
        ctx.callback(self.clear)

    def clear(self):
        with self.nc.Block() as block:
            @block.sync
            def _(sp):
                for n, sem in self.items():
                    if n not in self.own:
                        sp.sem_clear(sem)


def transpose_in(nc, x_prompt, x_sample, xT, ident, p_pad, ps_pad, state_shift, state_conv, sw):
    with ExitStack() as ctx:
        xin = ctx.enter_context(nc.sbuf_tensor("ti_x", [P, SLOTS, D], FP32))
        tp = [ctx.enter_context(nc.psum_tensor(f"ti_p{i}", [P, 4, P], FP32)) for i in range(2 * SLOTS)]
        zeros = ctx.enter_context(nc.sbuf_tensor("ti_zero", [PAD, SHIFT_W], FP32))
        ones = ctx.enter_context(nc.sbuf_tensor("ti_one", [DB, PAD, AW], FP32))
        s = Sems(nc, ctx, "ti", "ident_zero ident x_loaded0 x_loaded1 transposed half0 half1 filled", {"padded": sw["padded"]})
        block = ctx.enter_context(nc.Block())

        @block.gpsimd
        def _(pool):
            nc.gpsimd.memset(ident[:], 0.0).then_inc(s["ident_zero"], 1)
            pool.wait_ge(s["ident_zero"], 1)
            nc.gpsimd.affine_select(out=ident[:], in_=ident[:], compare_op=ALU.not_equal, fill=1.0, base=0,
                                    pattern=[[-1, P]], channel_multiplier=1).then_inc(s["ident"], 1)
            nc.gpsimd.memset(zeros[:], 0.0).then_inc(s["filled"], 1)
            nc.gpsimd.memset(ones[:].rearrange("b a n -> b (a n)"), 1.0).then_inc(s["filled"], 1)
            pool.wait_ge(s["filled"], 2)
            for dst, src in ((p_pad[0:PAD, C0:C0 + 2 * AW], zeros[:, 0:2 * AW]), (p_pad[PAD - 1:PAD, 0:SHIFT_W], zeros[0:1, :]),
                             (ps_pad[:, 0:PAD, HH0:HH0 + AW], ones[:]), (ps_pad[:, 0:PAD, C0:HH0], state_conv),
                             (ps_pad[:, PAD - 1, 0:SHIFT_W], state_shift)):
                pool.dma_start(dst, src).then_inc(s["padded"], 16)
            pool.wait_ge(s["padded"], 16 * 5)

        @block.sync
        def _(sp):
            def load(t, b, u):
                sp.wait_ge(s["transposed"], t + 1)
                src = x_prompt[0, bass.ds(t * P, P), :] if u is not PAIRS else x_sample.rearrange("b t d -> (b t) d")
                rows = P if u is not PAIRS else NS
                sp.dma_start(xin[0:rows, b, :], src).then_inc(s[f"x_loaded{b}"], 16)
            each_tile(sp, load)

        @block.tensor
        def _(pe):
            pe.sem_inc(s["transposed"], SLOTS)
            pe.wait_ge(s["ident"], 1)

            def turn(t, b, u):
                rows = P if u is not PAIRS else NS
                pe.wait_ge(s[f"x_loaded{b}"], 16 * (u + 1))
                pe.wait_ge(s["half0"], t + 1)
                pe.wait_ge(s["half1"], t + 1)
                for k in range(KD):
                    mm = nc.tensor.transpose(tp[2 * b + k // 4][:, k % 4, 0:rows], xin[0:rows, b, k * P:(k + 1) * P],
                                             ident[0:rows, 0:rows])
                mm.then_inc(s["transposed"], 1)
            each_tile(pe, turn)

        def copy_out(eng, copy, half):
            eng.sem_inc(s[f"half{half}"], SLOTS)

            def body(t, b, u):
                rows = P if u is not PAIRS else NS
                eng.wait_ge(s["transposed"], t + 1 + SLOTS)
                copy(xT[:, 4 * half:4 * half + 4, bass.ds(t * P, rows)], tp[2 * b + half][:, :, 0:rows])\
                    .then_inc(s[f"half{half}"], 1)
            each_tile(eng, body)

        @block.vector
        def _(dve):
            copy_out(dve, nc.vector.tensor_copy, 0)

        @block.scalar
        def _(act):
            copy_out(act, nc.scalar.copy, 1)


def project_in(nc, ph, xT, w, cw, n_chunks, p_prompt, p_sample, sw, beside=None):
    NB = 4
    PER = NPT // NB
    with ExitStack() as ctx:
        wc = ctx.enter_context(nc.sbuf_tensor(f"{ph}_w", [P, SLOTS, KD, cw], FP32))
        stage = ctx.enter_context(nc.sbuf_tensor(f"{ph}_stage", [P, NB + 1, cw], FP32))
        ps = [ctx.enter_context(nc.psum_tensor(f"{ph}_ps{i}", [P, 512], FP32)) for i in range(NB + 1)]
        s = Sems(nc, ctx, ph, "chunk_done tile_done even_out odd_out stored0 stored1 stored2 stored3 stored4",
                 {f"w_loaded{b}": sw[f"{ph}_w_loaded{b}"] for b in range(SLOTS)})
        n_even, n_odd = NPT // 2 + 1, NPT // 2
        turns = n_chunks // 2

        def each_chunk(eng, body):
            with eng.Fori(0, turns) as i:
                for b in range(SLOTS):
                    body(2 * i + b, b, i)
            if n_chunks % 2:
                body(n_chunks - 1, 0, turns)

        block = ctx.enter_context(nc.Block())

        @block.gpsimd
        def _(pool):
            def load(c, b, u):
                pool.wait_ge(s["chunk_done"], c + 1)
                pool.dma_start(wc[:, b, :, :], w[:, bass.ds(c * cw, cw)].rearrange("(k p) n -> p k n", p=P))\
                    .then_inc(s[f"w_loaded{b}"], 16)
            each_chunk(pool, load)

        @block.tensor
        def _(pe):
            pe.sem_inc(s["chunk_done"], SLOTS)

            def chunk(c, b, u):
                pe.wait_ge(s[f"w_loaded{b}"], 16 * (u + 1))
                for t in range(NTILE):
                    bank, rows = (t % NB, P) if t < NPT else (NB, NS)
                    if t % 2 == 0:
                        pe.wait_ge(s["even_out"], c * n_even + 1 + (max(t - NB + 2, 0) // 2))
                    else:
                        pe.wait_ge(s["odd_out"], c * n_odd + 1 + (max(t - NB + 1, 0) // 2))
                    for k in range(KD):
                        mm = nc.tensor.matmul(ps[bank][0:rows, 0:cw], xT[:, k, t * P:t * P + rows], wc[:, b, k, :],
                                              start=(k == 0), stop=(k == KD - 1))
                    if t < NPT:
                        mm.then_inc(s["tile_done"], 1)
                    else:
                        mm.then_inc(s["chunk_done"], 1)
            each_chunk(pe, chunk)

        def copy_out(eng, copy, parity, n_mine, out_sem):
            eng.sem_inc(out_sem, 1)

            def chunk(c, b, u):
                if parity and beside:
                    beside(eng, c, u is turns)
                for t in range(parity, NTILE, 2):
                    bank, rows = (t % NB, P) if t < NPT else (NB, NS)
                    if t < NPT:
                        eng.wait_ge(s["tile_done"], c * NPT + t + 1)
                        eng.wait_ge(s[f"stored{bank}"], 16 * (c * PER + t // NB) + 1)
                    else:
                        eng.wait_ge(s["chunk_done"], c + 1 + SLOTS)
                        eng.wait_ge(s[f"stored{bank}"], 16 * c + 1)
                    copy(stage[0:rows, bank, :], ps[bank][0:rows, 0:cw]).then_inc(out_sem, 1)
            each_chunk(eng, chunk)

        @block.vector
        def _(dve):
            copy_out(dve, nc.vector.tensor_copy, 0, n_even, s["even_out"])

        @block.scalar
        def _(act):
            copy_out(act, nc.scalar.copy, 1, n_odd, s["odd_out"])

        @block.sync
        def _(sp):
            for b in range(NB + 1):
                sp.sem_inc(s[f"stored{b}"], 1)

            def chunk(c, b, u):
                for t in range(NTILE):
                    bank, rows = (t % NB, P) if t < NPT else (NB, NS)
                    if t % 2 == 0:
                        sp.wait_ge(s["even_out"], c * n_even + t // 2 + 2)
                    else:
                        sp.wait_ge(s["odd_out"], c * n_odd + t // 2 + 2)
                    cols = bass.ds(c * cw, cw)
                    dst = p_prompt[t * P:t * P + rows, cols] if t < NPT else p_sample[:, :, cols]
                    sp.dma_start(dst, stage[0:rows, bank, :]).then_inc(s[f"stored{bank}"], 16)
            each_chunk(sp, chunk)
            for b in range(NB):
                sp.wait_ge(s[f"stored{b}"], 16 * n_chunks * PER + 1)
            sp.wait_ge(s[f"stored{NB}"], 16 * n_chunks + 1)


CHUNK = 64
NCH = P // CHUNK
HP = H // 2
LEVELS = 6
LD_SCALE = -0.6065306597126334
GN_EPS = 64e-5
LN_EPS = 1e-5
ALPHA = 4 ** 0.25


def rwkv_constants():
    import numpy as np
    i = np.arange(P)
    same = (i[:, None] // CHUNK) == (i[None, :] // CHUNK)
    upto = same & (i[:, None] <= i[None, :])
    before = same & (i[:, None] < i[None, :])
    off = [(i[:, None] // (2 * m) == i[None, :] // (2 * m)) & (i[:, None] // m > i[None, :] // m)
           for m in (1, 2, 4, 8, 16, 32)]
    eye64 = (i[:, None] % HD) == np.arange(HD)[None, :]
    chunk = (i[:, None] // CHUNK) == np.arange(NCH)[None, :]
    cols = [upto, before, upto, before, upto, off[0].T, *off[1:], eye64, chunk]
    return np.ascontiguousarray(np.concatenate([c.astype(np.float32) for c in cols], axis=1))


CONST_W = 5 * P + LEVELS * P + HD + NCH


class Chain:

    def __init__(self, eng, sem, per_tile):
        self.eng, self.sem, self.per_tile = eng, sem, per_tile

    def start(self, t):
        self.t, self.n = t, 0

    def __call__(self, ins):
        self.n += 1
        ins.then_inc(self.sem, 1)
        self.eng.wait_ge(self.sem, self.t * self.per_tile + self.n)

    def end(self):
        assert self.n == self.per_tile, (self.n, self.per_tile)


def heads(ap):
    return ap.rearrange("p (h d) -> p h d", h=H)


def pairs(bank):
    return bank[:, 0:AW // 2].rearrange("p (h d) -> p h d", d=HD)


def over(ap, n):
    return ap.unsqueeze(2).broadcast_to([ap.shape[0], ap.shape[1], n])


def each(ap, n):
    return ap.unsqueeze(1).broadcast_to([ap.shape[0], n, ap.shape[1]])


def even_mix(nc, ident, p_pad, ps_pad, consts, state_rwkv, rw, conv_w, y_prompt, y_sample, scan_in, scan_y,
             state_p_out, state_s_out, shift_p_out, shift_s_out, conv_p_out, conv_s_out, sw):
    mu, w0, w2, a0, a2, k_k, k_a, r_k, gn_g, gn_b = rw
    with ExitStack() as ctx:
        def sb(name, shape):
            return ctx.enter_context(nc.sbuf_tensor(f"em_{name}", shape, FP32))

        cur = sb("cur", [P, SLOTS, EVEN_W])
        ps = sb("ps", [P, SLOTS, SHIFT_W])
        ch1 = sb("ch1", [P, SLOTS, 2 * AW])
        ch2 = sb("ch2", [P, SLOTS, 2 * AW])
        cst = sb("cst", [P, CONST_W])
        mu_b = sb("mu", [P, SHIFT_W])
        par = sb("par", [P, 10, AW])
        w2a2 = sb("w2a2", [P, AW])
        W0, A0, KK, KA, RK, GG, GB, CW = 0, 1, 2, 3, 4, 5, 6, 7
        lora = sb("lora", [P, P])
        wa = sb("wa", [P, 2 * AW])
        th = sb("th", [P, 2 * AW])
        cprev = th[:, 0:AW]
        pc_, pinv, pprev = sb("pc", [P, AW]), sb("pinv", [P, AW]), sb("pprev", [P, AW])
        pend = sb("pend", [P, HP, NCH])
        kk, sq = sb("kk", [P, AW]), sb("sq", [P, AW])
        kn = kk
        bv, kp = sb("bv", [P, AW]), sb("kp", [P, AW])
        zt, rt, bt, kt = sb("zt", [P, AW]), sb("rt", [P, AW]), sb("bt", [P, AW]), sb("kt", [P, AW])
        ss, rs, bonus = sb("ss", [P, H]), sb("rs", [P, H]), sb("bonus", [P, H])
        half = sb("half", [P, H])
        ZR = sb("ZR", [P, HP, 2, P])
        BT, KT = sb("BT", [P, HP, P]), sb("KT", [P, HP, P])
        AM = sb("AM", [P, H, 4, P])
        T, X = sb("T", [P, H, P]), sb("X", [P, H, P])
        Ym = sb("Ym", [P, H, P])
        AV, W1, U0 = sb("AV", [P, AW]), sb("W1", [P, AW]), sb("U0", [P, AW])
        QT = sb("QT", [P, HP, P])
        M1, G = sb("M1", [P, NCH, HP, HD]), sb("G", [P, NCH, HP, HD])
        M_BANK, G_BANK = (2, 7), (4, 0)
        S = sb("S", [P, NCH, HP, HD])
        yl, y = sb("yl", [P, AW]), sb("y", [P, AW])
        mean, var, rstd = sb("mean", [P, H]), sb("var", [P, H]), sb("rstd", [P, H])
        uw = sb("uw", [P, AW])
        u0, u1, u2 = sb("u0", [P, AW]), sb("u1", [P, AW]), sb("u2", [P, AW])
        rkv = sb("rkv", [P, AW])
        tz = sb("tz", [P, 2 * AW])
        gate = sb("gate", [P, 2 * AW])
        yout = sb("yout", [P, 2 * AW])
        s_vk = sb("s_vk", [HD, H * HD])
        bank = [ctx.enter_context(nc.psum_tensor(f"em_b{i}", [P, 512], FP32)) for i in range(8)]
        vec = ZR[:, :, :, :].rearrange("p a b c -> p (a b c)")
        sc_z, sc_b = [AM[:, i, :, :].rearrange("p a b -> p (a b)") for i in (0, 1)]
        sc_w, sc_k, sc_r = [AM[:, i, :, :].rearrange("p a b -> p (a b)") for i in (2, 3, 4)]
        sc_v = AM[:, 5, 0:2, :].rearrange("p a b -> p (a b)")
        sc_y = AM[:, 6, 0:2, :].rearrange("p a b -> p (a b)")
        sa = AM[:, 7, 0, 0:32]
        state = cur[:, 1, 0:2048].rearrange("p (i j) -> p i j", j=HD)
        outer = cur[:, 1, 2048:4096].rearrange("p (i j) -> p i j", j=HD)
        outer2 = ps[:, :, :].rearrange("p a b -> p (a b)")[:, 0:2048].rearrange("p (i j) -> p i j", j=HD)

        s = Sems(nc, ctx, "em",
                 "cst loaded0 loaded1 half shifted conv_read lora_T lora lora_mm wa_in tanh ld cum cprev exps "
                 "ss rs zrbk zrbk_T0 zrbk_T1 zrbk_T2 zrbk_T3 zrbk_out a_mm masked x1 t1_T t1 "
                 "y_mm ym d_mm t_add x_T x_out x_final av_mm av w1_mm u0_mm w1 u0 "
                 "q_mm yl_mm m_mm q m1 yl g_mm g_out s_mm s_new y_cross y_sum var rstd ynorm gates gated stored state_out y_back s_T s_vk "
                 "dve act pool scan_out scan_loaded vk vk_free scan_y bonus",
                 {n: sw[n] for n in ("conv_out", "conv_s_out")})
        block = ctx.enter_context(nc.Block())
        c_tri = cst[:, 0:P]
        c_zr = cst[:, P:5 * P]
        c_off = [cst[:, (5 + i) * P:(6 + i) * P] for i in range(LEVELS)]
        c_eye = cst[:, 11 * P:11 * P + HD]
        c_chunk = cst[:, 11 * P + HD:11 * P + HD + NCH]

        LOADS, CSTS = 4, 14
        STATE_OUTS = 2 + 2 + 1

        def rows_of(u):
            return NS if u is PAIRS else P

        @block.sync
        def _(sp):
            row = lambda a: a.rearrange("(o n) -> o n", o=1)
            for dst, src in ((mu_b[:], row(mu)), *[(par[:, j, :], row(a)) for j, a in
                             enumerate((w0, a0, k_k, k_a, r_k.rearrange("h d -> (h d)"), gn_g, gn_b,
                                        conv_w[0], conv_w[1], conv_w[2]))]):
                sp.dma_start(dst, src.broadcast_to([P, src.shape[1]])).then_inc(s["cst"], 16)
            sp.dma_start(cst[:], consts).then_inc(s["cst"], 16)
            sp.dma_start(w2a2[0:HD, :], w2).then_inc(s["cst"], 16)
            sp.dma_start(w2a2[HD:P, :], a2).then_inc(s["cst"], 16)

            def load(t, b, last=False):
                n = NS if last else P
                if last:
                    src = [ps_pad[:, PAD - j:PAD - j + DT, :] for j in range(3)]
                    cut = lambda a, lo, hi: a[:, :, lo:hi]
                else:
                    src = [p_pad[bass.ds(t * P + PAD - j, P), :] for j in range(3)]
                    cut = lambda a, lo, hi: a[:, lo:hi]
                for dst, a in ((cur[0:n, b, :], src[0]), (ps[0:n, b, :], cut(src[1], 0, SHIFT_W)),
                               (ch1[0:n, b, :], cut(src[1], C0, ZB0)), (ch2[0:n, b, :], cut(src[2], C0, ZB0))):
                    sp.dma_start(dst, a).then_inc(s[f"loaded{b}"], 16)

            def store(t, last=False):
                sp.wait_ge(s["gated"], t + 1)
                if last:
                    sp.dma_start(y_sample, yout[0:NS, :]).then_inc(s["stored"], 16)
                else:
                    sp.dma_start(y_prompt[bass.ds(t * P, P), :], yout[:]).then_inc(s["stored"], 16)

            sp.sem_inc(s["stored"], 1)
            for b in range(SLOTS):
                load(b, b)
            with sp.Fori(0, PAIRS - 1) as i:
                for b in range(SLOTS):
                    store(2 * i + b)
                    load(2 * i + b + SLOTS, b)
            store(NPT - 2)
            load(NPT, 0, last=True)
            store(NPT - 1)
            store(NPT, last=True)
            sp.dma_start(shift_p_out, p_pad[PAD + SEQ - 1:PAD + SEQ, 0:SHIFT_W]).then_inc(s["state_out"], 16)
            sp.dma_start(shift_s_out, ps_pad[:, PAD + DT - 1, 0:SHIFT_W]).then_inc(s["state_out"], 16)
            sp.wait_ge(s["stored"], 16 * NTILE + 1)
            sp.wait_ge(s["state_out"], 16 * STATE_OUTS)


        @block.gpsimd
        def _(pool):
            ch = Chain(pool, s["pool"], 18)
            g = nc.gpsimd
            g.memset(half[:], -0.5).then_inc(s["half"], 1)
            pool.wait_ge(s["half"], 1)
            pool.wait_ge(s["cst"], 16 * CSTS)

            def tile(t, b, u):
                n = rows_of(u)
                ch.start(t)
                pool.wait_ge(s[f"loaded{b}"], 16 * LOADS * (u + 1))
                c, x = cur[0:n, b, :], ps[0:n, b, :]
                ch(g.tensor_tensor(x, x, c[:, 0:SHIFT_W], ALU.subtract))
                ch(g.tensor_tensor(x, x, mu_b[0:n, :], ALU.mult))
                g.tensor_tensor(x, x, c[:, 0:SHIFT_W], ALU.add).then_inc(s["shifted"], 1)
                pool.wait_ge(s["shifted"], t + 1)
                ch(g.tensor_tensor(u0[0:n], c[:, C0:HH0], c[:, HH0:ZB0], ALU.mult))
                ch(g.tensor_tensor(u1[0:n], ch1[0:n, b, 0:AW], ch1[0:n, b, AW:], ALU.mult))
                ch(g.tensor_tensor(u2[0:n], ch2[0:n, b, 0:AW], ch2[0:n, b, AW:], ALU.mult))
                ch(g.tensor_tensor(u2[0:n], u2[0:n], par[0:n, CW, :], ALU.mult))
                ch(g.tensor_tensor(u1[0:n], u1[0:n], par[0:n, CW + 1, :], ALU.mult))
                ch(g.tensor_tensor(uw[0:n], u0[0:n], par[0:n, CW + 2, :], ALU.mult))
                ch(g.tensor_tensor(u1[0:n], u1[0:n], u2[0:n], ALU.add))
                ch(g.tensor_tensor(u1[0:n], u1[0:n], uw[0:n], ALU.add))
                ch(g.tensor_tensor(u1[0:n], u1[0:n], c[:, B0:C0], ALU.mult))
                pool.wait_ge(s["ss"], t + 1)
                g.tensor_tensor(rs[0:n], ss[0:n], half[0:n], ALU.pow).then_inc(s["rs"], 1)
                pool.wait_ge(s["half"], 1)
                pool.wait_ge(s["gates"], t + 1)
                ch(g.tensor_scalar(gate[0:n], tz[0:n], 0.5, 0.5, ALU.mult, ALU.add))
                ch(g.tensor_tensor(gate[0:n, 0:AW], gate[0:n, 0:AW], c[:, ZA0:B0], ALU.mult))
                ch(g.tensor_tensor(gate[0:n, AW:], gate[0:n, AW:], c[:, ZB0:], ALU.mult))
                pool.wait_ge(s["stored"], 16 * t + 1)
                ch(g.tensor_tensor(yout[0:n, AW:], u1[0:n], gate[0:n, AW:], ALU.mult))
                pool.wait_ge(s["bonus"], t + 1)
                ch(g.tensor_tensor(heads(rkv[0:n]), heads(x[:, V0:L0]), over(bonus[0:n], HD), ALU.mult))
                if u is PAIRS:
                    pool.wait_ge(s["scan_loaded"], 16 * 14)
                    for i in range(DT):
                        if i:
                            pool.wait_ge(s["vk_free"], i)
                        g.tensor_tensor(outer2, over(sc_v[:, 32 * i:32 * i + 32], HD),
                                        each(sc_k[:, HD * i:HD * i + HD], 32), ALU.mult).then_inc(s["vk"], 1)
                pool.wait_ge(s["var"], t + 1)
                g.tensor_tensor(rstd[0:n], var[0:n], half[0:n], ALU.pow).then_inc(s["rstd"], 1)
                pool.wait_ge(s["ynorm"], t + 1)
                ch(g.tensor_tensor(y[0:n], y[0:n], par[0:n, GB, :], ALU.add))
                ch(g.tensor_tensor(y[0:n], y[0:n], rkv[0:n], ALU.add))
                g.tensor_tensor(yout[0:n, 0:AW], y[0:n], gate[0:n, 0:AW], ALU.mult).then_inc(s["gated"], 1)
                pool.wait_ge(s["gated"], t + 1)
                ch.end()

            each_tile(pool, tile, tail=False)
            pool.dma_start(conv_p_out, u0[P - 2:P, :]).then_inc(s["conv_out"], 16)
            pool.wait_ge(s["conv_out"], 16)
            tile(NPT, 0, PAIRS)
            for q in range(DB):
                pool.dma_start(conv_s_out[q], u0[DT * q + DT - 2:DT * q + DT, :]).then_inc(s["conv_s_out"], 16)
            pool.wait_ge(s["conv_s_out"], 16 * DB)

        @block.vector
        def _(dve):
            ch = Chain(dve, s["dve"], 0)
            v = nc.vector
            ch.per_tile = 17
            dve.wait_ge(s["cst"], 16 * CSTS)
            v.memset(S[:, 0, :, :], 0.0).then_inc(s["s_new"], 1)
            dve.wait_ge(s["s_new"], 1)

            def prep(t, b, u):
                n = rows_of(u)
                x = ps[0:n, b, :]
                r, k = x[:, R0:K0], x[:, K0:V0]
                ch.start(t)
                dve.wait_ge(s["shifted"], t + 1)
                ch(v.tensor_tensor(kk[0:n], k, par[0:n, KK, :], ALU.mult))
                ch(v.tensor_tensor(sq[0:n], kk[0:n], kk[0:n], ALU.mult))
                ch(v.tensor_reduce(ss[0:n], heads(sq[0:n]), AX.X, ALU.add))
                v.tensor_scalar(ss[0:n], ss[0:n], 1e-24, None, ALU.max).then_inc(s["ss"], 1)
                dve.wait_ge(s["lora_mm"], t + 1)
                ch(v.tensor_tensor(wa[0:n, 0:AW], bank[1][0:n, :], par[0:n, W0, :], ALU.add))
                v.tensor_tensor(wa[0:n, AW:], bank[2][0:n, :], par[0:n, A0, :], ALU.add).then_inc(s["wa_in"], 1)
                dve.wait_ge(s["tanh"], t + 1)
                v.tensor_scalar(wa[0:n, 0:AW], th[0:n, 0:AW], LD_SCALE / 2, LD_SCALE / 2, ALU.mult, ALU.add)\
                    .then_inc(s["ld"], 1)
                ch(v.tensor_scalar(wa[0:n, AW:], th[0:n, AW:], 0.5, 0.5, ALU.mult, ALU.add))
                ld, a = wa[0:n, 0:AW], wa[0:n, AW:]
                dve.wait_ge(s["rs"], t + 1)
                ch(v.tensor_tensor(heads(kn[0:n]), heads(kk[0:n]), over(rs[0:n], HD), ALU.mult))
                ch(v.tensor_tensor(bv[0:n], kn[0:n], a, ALU.mult))
                ch(v.scalar_tensor_tensor(kp[0:n], a, -1.0, par[0:n, KA, :], ALU.add, ALU.mult))
                ch(v.scalar_tensor_tensor(kp[0:n], kp[0:n], 1.0, k, ALU.add, ALU.mult))
                ch(v.tensor_tensor(sq[0:n], r, kp[0:n], ALU.mult))
                ch(v.tensor_tensor(sq[0:n], sq[0:n], par[0:n, RK, :], ALU.mult))
                v.tensor_reduce(bonus[0:n], heads(sq[0:n]), AX.X, ALU.add).then_inc(s["bonus"], 1)

            def core(t, b, u):
                x = ps[:, b, :]
                r = x[:, R0:K0]
                ld = wa[:, 0:AW]
                dve.wait_ge(s["cum"], t + 1)
                v.tensor_tensor(cprev, bank[3][:], ld, ALU.subtract).then_inc(s["cprev"], 1)
                dve.wait_ge(s["exps"], t + 1)
                ch(v.tensor_tensor(bt[:], bv[:], pinv[:], ALU.mult))
                ch(v.tensor_tensor(kt[:], kp[:], pinv[:], ALU.mult))
                ch(v.scalar_tensor_tensor(zt[:], kn[:], -1.0, pprev[:], ALU.mult, ALU.mult))
                v.tensor_tensor(rt[:], r, pc_[:], ALU.mult).then_inc(s["zrbk"], 1)
                for h in range(H):
                    dve.wait_ge(s["a_mm"], H * t + h + 1)
                    v.tensor_tensor(AM[:, h, :, :].rearrange("p a b -> p (a b)"), bank[h % 4][:], c_zr, ALU.mult)\
                        .then_inc(s["masked"], 1)
                dve.wait_ge(s["masked"], H * (t + 1))
                ch(v.tensor_tensor(X[:], AM[:, :, 0, :], each(c_off[0], H), ALU.mult))
                v.tensor_tensor(X[:], X[:], each(ident[:], H), ALU.add).then_inc(s["x1"], 1)
                L = LEVELS - 2
                for lv in range(1, LEVELS):
                    for g in range(2):
                        hs = slice(4 * g, 4 * g + 4)
                        dve.wait_ge(s["y_mm"], 2 * ((L + 1) * t + lv - 1) + g + 1)
                        v.tensor_tensor(Ym[:, hs, :], bank[g][:].rearrange("p (h n) -> p h n", h=4),
                                        each(c_off[lv], 4), ALU.mult).then_inc(s["ym"], 1)
                    for g in range(2):
                        hs = slice(4 * g, 4 * g + 4)
                        dve.wait_ge(s["d_mm"], 2 * ((L + 1) * t + lv - 1) + g + 1)
                        M = T if lv < LEVELS - 1 else X
                        v.tensor_tensor(M[:, hs, :], M[:, hs, :], bank[2 + g][:].rearrange("p (h n) -> p h n", h=4),
                                        ALU.add).then_inc(s["t_add"], 1)
                dve.wait_ge(s["w1_mm"], t + 1)
                v.tensor_copy(W1[:], bank[7][:]).then_inc(s["w1"], 1)
                dve.wait_ge(s["q_mm"], t + 1)
                v.tensor_tensor(QT[:], bank[0][:].rearrange("p (h n) -> p h n", h=HP), ZR[:, :, 1, :], ALU.add)\
                    .then_inc(s["q"], 1)
                dve.wait_ge(s["m_mm"], t + 1)
                for c in range(NCH):
                    v.tensor_tensor(M1[:, c, :, :], pairs(bank[M_BANK[c]]), each(c_eye, HP), ALU.add)\
                        .then_inc(s["m1"], 1)
                for c in range(NCH):
                    dve.wait_ge(s["s_mm"], NCH * t + c + 1)
                    if c == NCH - 1:
                        dve.wait_ge(s["y_cross"], 2 * t + 1)
                    dve.wait_ge(s["g_out"], NCH * t + c + 1)
                    new = S[:, (c + 1) % NCH, :, :]
                    ch(v.tensor_tensor(new, pairs(bank[3]), G[:, c, :, :], ALU.add))
                    v.tensor_tensor(new, new, over(pend[:, :, c], HD), ALU.mult).then_inc(s["s_new"], 1)
                dve.wait_ge(s["y_cross"], 2 * t + 2)
                dve.wait_ge(s["yl"], t + 1)
                y4, yl4 = [a[:].rearrange("p (h e d) -> p h e d", e=2, d=HD) for a in (y, yl)]
                ch(v.tensor_tensor(y4[:, :, 0, :], yl4[:, :, 0, :], pairs(bank[5]), ALU.add))
                v.tensor_tensor(y4[:, :, 1, :], yl4[:, :, 1, :], pairs(bank[6]), ALU.add).then_inc(s["y_sum"], 1)
                dve.wait_ge(s["y_sum"], t + 1)

            def norm(t, b, u):
                n = rows_of(u)
                yh = heads(y[0:n])
                ch(v.tensor_reduce(mean[0:n], yh, AX.X, ALU.add))
                ch(v.tensor_scalar(mean[0:n], mean[0:n], 1.0 / HD, None, ALU.mult))
                ch(v.tensor_tensor(yh, yh, over(mean[0:n], HD), ALU.subtract))
                ch(v.tensor_tensor(sq[0:n], y[0:n], y[0:n], ALU.mult))
                ch(v.tensor_reduce(var[0:n], heads(sq[0:n]), AX.X, ALU.add))
                v.tensor_scalar(var[0:n], var[0:n], 1.0 / HD, GN_EPS, ALU.mult, ALU.add).then_inc(s["var"], 1)
                dve.wait_ge(s["rstd"], t + 1)
                ch(v.tensor_tensor(yh, yh, over(rstd[0:n], HD), ALU.mult))
                v.tensor_tensor(y[0:n], y[0:n], par[0:n, GG, :], ALU.mult).then_inc(s["ynorm"], 1)

            PREP, CORE, NORM = 11, 4 + NCH + 1, 6
            ch.per_tile = PREP + CORE + NORM

            def tile(t, b, u):
                prep(t, b, u)
                core(t, b, u)
                norm(t, b, u)
                ch.end()
                dve.wait_ge(s["gated"], t + 1)
            each_tile(dve, tile, tail=False)

            prep(NPT, 0, PAIRS)
            dve.wait_ge(s["scan_loaded"], 16 * 14)
            for i in range(DT):
                z, bb, w, rr = [a[:, HD * i:HD * i + HD] for a in (sc_z, sc_b, sc_w, sc_r)]
                ch(v.tensor_tensor(outer, state, each(z, 32), ALU.mult))
                ch(v.tensor_reduce(sa, outer, AX.X, ALU.add))
                ch(v.tensor_tensor(state, state, each(w, 32), ALU.mult))
                ch(v.tensor_tensor(outer, over(sa, HD), each(bb, 32), ALU.mult))
                ch(v.tensor_tensor(state, state, outer, ALU.add))
                dve.wait_ge(s["vk"], i + 1)
                v.tensor_tensor(state, state, outer2, ALU.add).then_inc(s["vk_free"], 1)
                dve.wait_ge(s["vk_free"], i + 1)
                ch(v.tensor_tensor(outer, state, each(rr, 32), ALU.mult))
                last = v.tensor_reduce(sc_y[:, 32 * i:32 * i + 32], outer, AX.X, ALU.add)
                if i < DT - 1:
                    ch(last)
                else:
                    last.then_inc(s["scan_y"], 1)
            dve.wait_ge(s["y_back"], 16 * DB)
            norm(NPT, 0, PAIRS)

        @block.scalar
        def _(act):
            a = nc.scalar

            def prep(t, b, u):
                n = rows_of(u)
                act.wait_ge(s["lora_T"], t + 1)
                a.activation(lora[0:HD, 0:n], bank[0][0:HD, 0:n], ACT.Tanh).then_inc(s["lora"], 1)
                a.copy(lora[HD:P, 0:n], bank[0][HD:P, 0:n]).then_inc(s["lora"], 1)
                act.wait_ge(s[f"loaded{b}"], 16 * LOADS * (u + 1))
                a.activation(tz[0:n, 0:AW], cur[0:n, b, ZA0:B0], ACT.Tanh, scale=0.5).then_inc(s["act"], 1)
                a.activation(tz[0:n, AW:], cur[0:n, b, ZB0:], ACT.Tanh, scale=0.5).then_inc(s["gates"], 1)
                act.wait_ge(s["wa_in"], t + 1)
                a.activation(th[0:n], wa[0:n], ACT.Tanh, scale=0.5).then_inc(s["tanh"], 1)

            def tile(t, b, u):
                prep(t, b, u)
                act.wait_ge(s["cprev"], t + 1)
                a.activation(pc_[:], bank[3][:], ACT.Exp).then_inc(s["act"], 1)
                a.activation(pinv[:], bank[3][:], ACT.Exp, scale=-1.0).then_inc(s["act"], 1)
                a.activation(pend[:].rearrange("p a b -> p (a b)"), bank[4][:, 0:HP * NCH], ACT.Exp).then_inc(s["act"], 1)
                a.activation(pprev[:], cprev, ACT.Exp).then_inc(s["exps"], 1)
                act.wait_ge(s["exps"], t + 1)
                for j, dst in enumerate((ZR[:, :, 0, :], ZR[:, :, 1, :], BT[:], KT[:])):
                    act.wait_ge(s[f"zrbk_T{j}"], t + 1)
                    a.copy(dst, bank[4 + j][:].rearrange("p (h n) -> p h n", h=HP)).then_inc(s["zrbk_out"], 1)
                act.wait_ge(s["t1_T"], 2 * t + 1)
                a.copy(T[:, 0:4, :], bank[4][:].rearrange("p (h n) -> p h n", h=4)).then_inc(s["t1"], 1)
                act.wait_ge(s["t1_T"], 2 * t + 2)
                a.copy(T[:, 4:8, :], bank[5][:].rearrange("p (h n) -> p h n", h=4)).then_inc(s["t1"], 1)
                act.wait_ge(s["av_mm"], t + 1)
                a.copy(AV[:], bank[6][:]).then_inc(s["av"], 1)
                for lv in range(1, LEVELS - 1):
                    for g in range(2):
                        act.wait_ge(s["x_T"], 2 * ((LEVELS - 2) * t + lv - 1) + g + 1)
                        a.copy(X[:, 4 * g:4 * g + 4, :], bank[4 + g][:].rearrange("p (h n) -> p h n", h=4))\
                            .then_inc(s["x_out"], 1)
                act.wait_ge(s["u0_mm"], t + 1)
                a.copy(U0[:], bank[6][:]).then_inc(s["u0"], 1)
                act.wait_ge(s["yl_mm"], t + 1)
                a.copy(yl[:], bank[1][:]).then_inc(s["yl"], 1)
                for c in range(NCH):
                    act.wait_ge(s["g_mm"], NCH * t + c + 1)
                    a.copy(G[:, c, :, :], pairs(bank[G_BANK[c]])).then_inc(s["g_out"], 1)
            each_tile(act, tile, tail=False)

            prep(NPT, 0, PAIRS)
            act.wait_ge(s["ld"], NPT + 1)
            a.activation(pc_[0:NS], wa[0:NS, 0:AW], ACT.Exp).then_inc(s["act"], 1)
            act.wait_ge(s["bonus"], NPT + 1)
            a.mul(zt[0:NS], kn[0:NS], -1.0).then_inc(s["act"], 1)
            act.wait_ge(s["act"], 4 * NPT + 3)
            for j, src in enumerate((zt[0:NS], bv[0:NS], pc_[0:NS], kp[0:NS], ps[0:NS, 0, R0:K0], ps[0:NS, 0, V0:L0])):
                for q in range(DB):
                    act.dma_start(scan_in[j, q].rearrange("h t d -> t h d"), heads(src[DT * q:DT * q + DT, :]))\
                        .then_inc(s["scan_out"], 16)
            act.wait_ge(s["scan_out"], 16 * 6 * DB)
            for j, dst in enumerate((sc_z, sc_b, sc_w, sc_k, sc_r)):
                for i in range(2):
                    act.dma_start(dst[64 * i:64 * i + 64, :],
                                  scan_in[j].rearrange("b h t d -> (b h) (t d)")).then_inc(s["scan_loaded"], 16)
            for i in range(2):
                act.dma_start(sc_v[64 * i:64 * i + 64, :].rearrange("p (t d) -> p t d", t=DT),
                              scan_in[5].rearrange("b h t (a d) -> a (b h) t d", a=2)[i])\
                    .then_inc(s["scan_loaded"], 16)
                act.dma_start(state[64 * i:64 * i + 64], state_rwkv.rearrange("b h (a i) j -> a (b h) i j", a=2)[i])\
                    .then_inc(s["scan_loaded"], 16)
            act.wait_ge(s["scan_y"], 1)
            for i in range(2):
                act.dma_start(scan_y.rearrange("b h t (a d) -> a (b h) t d", a=2)[i],
                              sc_y[64 * i:64 * i + 64, :].rearrange("p (t d) -> p t d", t=DT)).then_inc(s["scan_out"], 16)
                act.dma_start(state_s_out.rearrange("b h (a i) j -> a (b h) i j", a=2)[i], state[64 * i:64 * i + 64])\
                    .then_inc(s["state_out"], 16)
            act.wait_ge(s["scan_out"], 16 * (6 * DB + 2))
            for q in range(DB):
                act.dma_start(heads(y[DT * q:DT * q + DT, :]), scan_y[q].rearrange("h t d -> t h d"))\
                    .then_inc(s["y_back"], 16)
            act.wait_ge(s["s_T"], 1)
            a.copy(s_vk[:], bank[0][0:HD, :]).then_inc(s["s_vk"], 1)
            act.wait_ge(s["s_vk"], 1)
            act.dma_start(state_p_out.rearrange("h i j -> i h j"), s_vk[:].rearrange("p (h j) -> p h j", h=H))\
                .then_inc(s["state_out"], 16)

        @block.tensor
        def _(pe):
            mm, tr = nc.tensor.matmul, nc.tensor.transpose
            pe.wait_ge(s["cst"], 16 * CSTS)

            def prep(t, b, u):
                n = rows_of(u)
                pe.wait_ge(s["shifted"], t + 1)
                tr(bank[0][:, 0:n], ps[0:n, b, L0:], ident[0:n, 0:n]).then_inc(s["lora_T"], 1)
                pe.wait_ge(s["lora"], 2 * t + 2)
                mm(bank[1][0:n, :], lora[0:HD, 0:n], w2a2[0:HD, :], start=True, stop=True)
                mm(bank[2][0:n, :], lora[HD:P, 0:n], w2a2[HD:P, :], start=True, stop=True).then_inc(s["lora_mm"], 1)

            def tile(t, b, u):
                v = ps[:, b, V0:L0]
                prep(t, b, u)
                pe.wait_ge(s["ld"], t + 1)
                mm(bank[3][:], c_tri, wa[:, 0:AW], start=True, stop=True)
                for p in range(HP):
                    m = mm(bank[4][:, NCH * p:NCH * (p + 1)], wa[:, p * P:(p + 1) * P], c_chunk, start=True, stop=True)
                m.then_inc(s["cum"], 1)
                pe.wait_ge(s["zrbk"], t + 1)
                for j, src in enumerate((zt, rt, bt, kt)):
                    for p in range(HP):
                        m = tr(bank[4 + j][:, p * P:(p + 1) * P], src[:, p * P:(p + 1) * P], ident[:])
                    m.then_inc(s[f"zrbk_T{j}"], 1)
                pe.wait_ge(s["zrbk_out"], 4 * t + 4)
                for h in range(H):
                    e, p = HD * (h % 2), h // 2
                    if h >= 4:
                        pe.wait_ge(s["masked"], H * t + h - 3)
                    zr = ZR[e:e + HD, p, :, :].rearrange("p a b -> p (a b)")
                    mm(bank[h % 4][:, 0:2 * P], BT[e:e + HD, p, :], zr, start=True, stop=True)
                    mm(bank[h % 4][:, 2 * P:], KT[e:e + HD, p, :], zr, start=True, stop=True).then_inc(s["a_mm"], 1)
                pe.wait_ge(s["masked"], H * (t + 1))
                for h in range(H):
                    m = mm(bank[6][:, h * HD:(h + 1) * HD], AM[:, h, 2, :], v[:, h * HD:(h + 1) * HD], start=True, stop=True)
                m.then_inc(s["av_mm"], 1)
                pe.wait_ge(s["x1"], t + 1)
                for h in range(H):
                    m = tr(bank[4 + h // 4][:, (h % 4) * P:(h % 4 + 1) * P], X[:, h, :], ident[:])
                    if h % 4 == 3:
                        m.then_inc(s["t1_T"], 1)
                L = LEVELS - 1
                for lv in range(1, LEVELS):
                    for g in range(2):
                        if lv == 1:
                            pe.wait_ge(s["t1"], 2 * t + g + 1)
                        else:
                            pe.wait_ge(s["t_add"], 2 * (L * t + lv - 2) + g + 1)
                        for h in range(4 * g, 4 * g + 4):
                            m = mm(bank[g][:, (h % 4) * P:(h % 4 + 1) * P], AM[:, h, 0, :], T[:, h, :], start=True, stop=True)
                        m.then_inc(s["y_mm"], 1)
                    for g in range(2):
                        pe.wait_ge(s["ym"], 2 * (L * t + lv - 1) + g + 1)
                        if lv > 1:
                            pe.wait_ge(s["x_out"], 2 * ((L - 1) * t + lv - 2) + g + 1)
                        for h in range(4 * g, 4 * g + 4):
                            o = bank[2 + g][:, (h % 4) * P:(h % 4 + 1) * P]
                            if lv < LEVELS - 1:
                                m = mm(o, X[:, h, :], Ym[:, h, :], start=True, stop=True)
                            else:
                                m = mm(o, Ym[:, h, :], X[:, h, :], start=True, stop=True)
                        m.then_inc(s["d_mm"], 1)
                    if lv < LEVELS - 1:
                        for g in range(2):
                            pe.wait_ge(s["t_add"], 2 * (L * t + lv - 1) + g + 1)
                            for h in range(4 * g, 4 * g + 4):
                                m = tr(bank[4 + g][:, (h % 4) * P:(h % 4 + 1) * P], T[:, h, :], ident[:])
                            m.then_inc(s["x_T"], 1)
                pe.wait_ge(s["t_add"], 2 * L * (t + 1))
                pe.wait_ge(s["av"], t + 1)
                cols = [slice(h * HD, (h + 1) * HD) for h in range(H)]
                for h in range(H):
                    m = mm(bank[7][:, cols[h]], X[:, h, :], zt[:, cols[h]], start=True, stop=True)
                m.then_inc(s["w1_mm"], 1)
                for h in range(H):
                    m = mm(bank[6][:, cols[h]], X[:, h, :], AV[:, cols[h]], start=True, stop=True)
                m.then_inc(s["u0_mm"], 1)
                pe.wait_ge(s["w1"], t + 1)
                for h in range(H):
                    e, p = HD * (h % 2), h // 2
                    m = mm(bank[0][e:e + HD, p * P:(p + 1) * P], W1[:, cols[h]], AM[:, h, 1, :], start=True, stop=True)
                m.then_inc(s["q_mm"], 1)
                for c in range(NCH):
                    cs = slice(c * CHUNK, (c + 1) * CHUNK)
                    for h in range(H):
                        e, p = HD * (h % 2), h // 2
                        m = mm(bank[M_BANK[c]][e:e + HD, p * HD:(p + 1) * HD], W1[cs, cols[h]], bt[cs, cols[h]], start=True, stop=True)
                m.then_inc(s["m_mm"], 1)
                pe.wait_ge(s["u0"], t + 1)
                for h in range(H):
                    mm(bank[1][:, cols[h]], AM[:, h, 1, :], U0[:, cols[h]], start=True, stop=False)
                    m = mm(bank[1][:, cols[h]], AM[:, h, 3, :], v[:, cols[h]], start=False, stop=True)
                m.then_inc(s["yl_mm"], 1)
                pe.wait_ge(s["cst"], 16 * CSTS)
                pe.wait_ge(s["q"], t + 1)
                for c in range(NCH):
                    cs = slice(c * CHUNK, (c + 1) * CHUNK)
                    for h in range(H):
                        e, p = HD * (h % 2), h // 2
                        o = bank[G_BANK[c]][e:e + HD, p * HD:(p + 1) * HD]
                        mm(o, bt[cs, cols[h]], U0[cs, cols[h]], start=True, stop=False)
                        m = mm(o, kt[cs, cols[h]], v[cs, cols[h]], start=False, stop=True)
                    m.then_inc(s["g_mm"], 1)
                for c in range(NCH):
                    cs = slice(c * CHUNK, (c + 1) * CHUNK)
                    pe.wait_ge(s["cst"], 16 * CSTS)
                    pe.wait_ge(s["s_new"], NCH * t + c + 1)
                    pe.wait_ge(s["m1"], NCH * t + c + 1)
                    for h in range(H):
                        e, p = HD * (h % 2), h // 2
                        m = mm(bank[3][e:e + HD, p * HD:(p + 1) * HD], M1[e:e + HD, c, p, :], S[e:e + HD, c, p, :],
                               start=True, stop=True)
                    m.then_inc(s["s_mm"], 1)
                    for h in range(H):
                        e, p = HD * (h % 2), h // 2
                        m = mm(bank[5 + h % 2][cs, p * HD:(p + 1) * HD], QT[e:e + HD, p, cs], S[e:e + HD, c, p, :], start=True, stop=True)
                    m.then_inc(s["y_cross"], 1)
                pe.wait_ge(s["y_sum"], t + 1)
            each_tile(pe, tile, tail=False)
            prep(NPT, 0, PAIRS)
            pe.wait_ge(s["lora"], 2 * NPT + 2)
            pe.wait_ge(s["s_new"], NCH * NPT + 1)
            for p in range(HP):
                m = tr(bank[0][0:HD, p * P:(p + 1) * P], S[:, 0, p, :], ident[:])
            m.then_inc(s["s_T"], 1)


def project_out(nc, ph, ident, y_prompt, y_sample, width, w, x_prompt, x_sample, ln_g, ln_b, out_prompt, out_sample, xT):
    KW = width // P
    HALF = D // 2
    with ExitStack() as ctx:
        def sb(name, shape):
            return ctx.enter_context(nc.sbuf_tensor(f"{ph}_{name}", shape, FP32))

        ws = sb("w", [P, KW, D])
        g_b, b_b = sb("g", [P, D]), sb("b", [P, D])
        yin, xin = sb("yin", [P, SLOTS, width]), sb("xin", [P, SLOTS, D])
        yT = sb("yT", [P, KW, P])
        res = sb("res", [P, SLOTS, D])
        stats, mv, spare = sb("stats", [P, 2, 6]), sb("mv", [P, 2]), sb("spare", [P, 1])
        rstd, half = sb("rstd", [P, 1]), sb("half", [P, 1])
        bank = [ctx.enter_context(nc.psum_tensor(f"{ph}_b{i}", [P, 512], FP32)) for i in range(8)]
        s = Sems(nc, ctx, ph, "w half loaded0 loaded1 y_T yT0 yT1 products res var rstd scaled normed stored "
                              "x_T xT0 xT1 dve pool")
        block = ctx.enter_context(nc.Block())
        LOADS, WS = 2, 3

        def rows(last):
            return NS if last else P

        @block.sync
        def _(sp):
            def load(t, b, last=False):
                ys, xs = (y_sample, x_sample) if last else (y_prompt[bass.ds(t * P, P), :], x_prompt[bass.ds(t * P, P), :])
                sp.dma_start(yin[0:rows(last), b, :], ys).then_inc(s[f"loaded{b}"], 16)
                sp.dma_start(xin[0:rows(last), b, :], xs).then_inc(s[f"loaded{b}"], 16)

            def store(t, b, last=False):
                sp.wait_ge(s["normed"], t + 1)
                dst = out_sample if last else out_prompt[bass.ds(t * P, P), :]
                sp.dma_start(dst, res[0:rows(last), b, :]).then_inc(s["stored"], 16)

            for b in range(SLOTS):
                load(b, b)
            sp.dma_start(ws[:], w.rearrange("(k p) n -> p k n", p=P)).then_inc(s["w"], 16)
            for dst, a in ((g_b, ln_g), (b_b, ln_b)):
                sp.dma_start(dst[:], a.rearrange("(o n) -> o n", o=1).broadcast_to([P, D])).then_inc(s["w"], 16)
            sp.sem_inc(s["stored"], 32)
            with sp.Fori(0, PAIRS - 1) as i:
                for b in range(SLOTS):
                    store(2 * i + b, b)
                    load(2 * i + b + SLOTS, b)
            store(NPT - 2, 0)
            load(NPT, 0, last=True)
            store(NPT - 1, 1)
            store(NPT, 0, last=True)
            sp.wait_ge(s["stored"], 16 * (NTILE + 2))

        @block.tensor
        def _(pe):
            mm, tr = nc.tensor.matmul, nc.tensor.transpose
            pe.sem_inc(s["x_T"], 1)
            pe.sem_inc(s["products"], 1)
            pe.wait_ge(s["w"], 16 * WS)

            def products(t, b, u, last=False):
                n = rows(last)
                pe.wait_ge(s[f"loaded{b}"], 16 * LOADS * (u + 1))
                for k in range(KW):
                    m = tr(bank[k // 4][:, (k % 4) * P:(k % 4) * P + n], yin[0:n, b, k * P:(k + 1) * P], ident[0:n, 0:n])
                m.then_inc(s["y_T"], 1)
                pe.wait_ge(s["yT0"], t + 1)
                pe.wait_ge(s["yT1"], t + 1)
                pe.wait_ge(s["res"], t + 1)
                for j in range(2):
                    for k in range(KW):
                        m = mm(bank[2 + 2 * b + j][0:n, :], yT[:, k, 0:n], ws[:, k, j * HALF:(j + 1) * HALF],
                               start=(k == 0), stop=(k == KW - 1))
                m.then_inc(s["products"], 1)

            def transposes(t, b, last=False):
                if xT is None:
                    return
                n = rows(last)
                pe.wait_ge(s["normed"], t + 1)
                pe.wait_ge(s["xT0"], t + 1)
                pe.wait_ge(s["xT1"], t + 1)
                for k in range(KD):
                    m = tr(bank[6 + k // 4][:, (k % 4) * P:(k % 4) * P + n], res[0:n, b, k * P:(k + 1) * P], ident[0:n, 0:n])
                m.then_inc(s["x_T"], 1)

            products(0, 0, 0)
            with pe.Fori(0, PAIRS - 1) as i:
                products(2 * i + 1, 1, i)
                transposes(2 * i, 0)
                products(2 * i + 2, 0, i + 1)
                transposes(2 * i + 1, 1)
            products(NPT - 1, 1, PAIRS - 1)
            transposes(NPT - 2, 0)
            products(NPT, 0, PAIRS, last=True)
            transposes(NPT - 1, 1)
            transposes(NPT, 0, last=True)

        def copy_yT(eng, copy, t, j, n):
            eng.wait_ge(s["y_T"], t + 1)
            eng.wait_ge(s["products"], t + 1)
            k0 = 4 * j
            copy(yT[:, k0:k0 + 4, 0:n], bank[j][:].rearrange("p (k t) -> p k t", t=P)[:, :, 0:n])\
                .then_inc(s[f"yT{j}"], 1)

        def copy_xT(eng, copy, t, j, n):
            eng.wait_ge(s["x_T"], t + 2)
            copy(xT[:, 4 * j:4 * j + 4, bass.ds(t * P, n)], bank[6 + j][:].rearrange("p (k t) -> p k t", t=P)[:, :, 0:n])\
                .then_inc(s[f"xT{j}"], 1)

        def in_turn(eng, tile, behind):
            tile(0, 0, 0)
            with eng.Fori(0, PAIRS - 1) as i:
                tile(2 * i + 1, 1, i)
                behind(2 * i, 0)
                tile(2 * i + 2, 0, i + 1)
                behind(2 * i + 1, 1)
            tile(NPT - 1, 1, PAIRS - 1)
            behind(NPT - 2, 0)
            tile(NPT, 0, PAIRS, last=True)
            behind(NPT - 1, 1)
            behind(NPT, 0, last=True)

        @block.vector
        def _(dve):
            v = nc.vector
            ch = Chain(dve, s["dve"], 4)
            dve.sem_inc(s["res"], SLOTS)
            dve.sem_inc(s["xT0"], 1)

            def tile(t, b, u, last=False):
                n = rows(last)
                ch.start(t)
                copy_yT(dve, v.tensor_copy, t, 0, n)
                dve.wait_ge(s["products"], t + 2)
                dve.wait_ge(s["stored"], 16 * (t + 1))
                r = res[0:n, b, :]
                for j in range(2):
                    m = v.scalar_tensor_tensor(r[:, j * HALF:(j + 1) * HALF], xin[0:n, b, j * HALF:(j + 1) * HALF], ALPHA,
                                               bank[2 + 2 * b + j][0:n, :], ALU.mult, ALU.add)
                    if j:
                        m.then_inc(s["res"], 1)
                        dve.wait_ge(s["res"], t + 1 + SLOTS)
                    else:
                        ch(m)
                ch(v.bn_stats(stats[0:n, 0, :], r[:, 0:HALF]))
                ch(v.bn_stats(stats[0:n, 1, :], r[:, HALF:]))
                v.memset(spare[:], 0.0)
                ch(v.bn_aggr(mv[0:n], stats[0:n].rearrange("p a b -> p (a b)")))
                v.tensor_scalar(mv[0:n, 1:2], mv[0:n, 1:2], LN_EPS, None, ALU.add).then_inc(s["var"], 1)
                dve.wait_ge(s["rstd"], t + 1)
                v.tensor_scalar(r, r, mv[0:n, 0:1], rstd[0:n], ALU.subtract, ALU.mult).then_inc(s["scaled"], 1)
                dve.wait_ge(s["scaled"], t + 1)
                ch.end()

            def behind(t, b, last=False):
                if xT is not None:
                    copy_xT(dve, v.tensor_copy, t, 0, rows(last))
            in_turn(dve, tile, behind)

        @block.scalar
        def _(act):
            act.sem_inc(s["xT1"], 1)

            def tile(t, b, u, last=False):
                if KW > 4:
                    copy_yT(act, nc.scalar.copy, t, 1, rows(last))
                else:
                    act.wait_ge(s["y_T"], t + 1)
                    act.sem_inc(s["yT1"], 1)

            def behind(t, b, last=False):
                if xT is not None:
                    copy_xT(act, nc.scalar.copy, t, 1, rows(last))
            in_turn(act, tile, behind)

        @block.gpsimd
        def _(pool):
            g = nc.gpsimd
            g.memset(half[:], -0.5).then_inc(s["half"], 1)
            pool.wait_ge(s["half"], 1)
            pool.wait_ge(s["w"], 16 * WS)

            def tile(t, b, u, last=False):
                n = rows(last)
                r = res[0:n, b, :]
                pool.wait_ge(s["var"], t + 1)
                g.tensor_tensor(rstd[0:n], mv[0:n, 1:2], half[0:n], ALU.pow).then_inc(s["rstd"], 1)
                pool.wait_ge(s["scaled"], t + 1)
                g.tensor_tensor(r, r, g_b[0:n], ALU.mult).then_inc(s["pool"], 1)
                pool.wait_ge(s["pool"], t + 1)
                g.tensor_tensor(r, r, b_b[0:n], ALU.add).then_inc(s["normed"], 1)
            in_turn(pool, tile, lambda *a, **k: None)


C_QKV = 3 * NG * AW
DIL = (1, 4, 16)
SCALE = HD ** -0.5
NEG = -1e30
ST_W = AW + 2 * H


def window_constants():
    import numpy as np
    q, k = np.arange(P)[:, None], np.arange(2 * P)[None, :]
    dist = q + P - k
    return np.where((dist >= 0) & (dist <= P), 0.0, NEG).astype(np.float32)


def window_attention(nc, ident, p1, mask_in, stats_out, sw, beside):
    VS = 4
    HEADS = ((0, 2), (1, 3), (4, 6), (5, 7))

    with ExitStack() as ctx:
        def sb(name, shape):
            return ctx.enter_context(nc.sbuf_tensor(f"wa_{name}", shape, FP32))

        mask = sb("mask", [P, 2 * P])
        q_in, k_in = sb("q", [P, SLOTS, AW]), sb("k", [P, SLOTS, AW])
        v_in = sb("v", [P, VS, AW])
        qT, kT = sb("qT", [P, HP, P]), sb("kT", [P, SLOTS, HP, P])
        sm = sb("sm", [P, 2, H, 2 * P])
        ex = sb("ex", [P, 2, H, 2 * P])
        mx, spare = sb("mx", [P, H]), sb("spare", [P, len(HEADS)])
        eT = sb("eT", [P, 2, 2, 2 * P])
        out = sb("out", [P, SLOTS, ST_W])
        b_qk = ctx.enter_context(nc.psum_tensor("wa_qk", [P, 512], FP32))
        b_o = ctx.enter_context(nc.psum_tensor("wa_o", [P, 512], FP32))
        b_s = [ctx.enter_context(nc.psum_tensor(f"wa_s{i}", [P, 512], FP32)) for i in range(4)]
        b_e = [ctx.enter_context(nc.psum_tensor(f"wa_e{i}", [P, 512], FP32)) for i in range(2)]
        s = Sems(nc, ctx, "wa", "mask q_T k_T qT kT scores sm negmax ex e_T0 e_T1 eT0 eT1 values out "
                                "dve act loadqk0 loadqk1 loadv0 loadv1 loadv2 loadv3",
                 {f"stored{b}": sw[f"out_stored{b}"] for b in range(SLOTS)})
        block = ctx.enter_context(nc.Block())

        def walk(eng, step, last):
            def four(n0, u, rows, has, before):
                for j in range(4):
                    step(n0 + j, j, u, has[j], before if j == 0 else has[j - 1], *rows(j))
            G0, G1, G2 = NPT // 4, 4, 4
            yes, no = True, False
            four(0, 0, lambda j: (j * P, 1), (no, yes, yes, yes), None)
            with eng.Fori(1, G0) as i:
                four(4 * i, i, lambda j: (i * 4 * P + j * P, 1), (yes,) * 4, yes)
            with eng.Fori(0, G1) as i:
                four(4 * i + NPT, i + G0, lambda j: (i + j * 4 * P, 4), (no, yes, yes, yes), yes)
            four(2 * NPT, G0 + G1, lambda j: (j, 16), (no,) * 4, yes)
            with eng.Fori(1, G2) as i:
                four(4 * i + 2 * NPT, i + G0 + G1, lambda j: (4 * i + j, 16), (no,) * 4, no)
            last(3 * NPT)

        @block.sync
        def _(sp):
            sp.dma_start(mask[:], mask_in).then_inc(s["mask"], 16)

            def rows(tensor, j, row, d, c0, c1):
                if d == 4:
                    part = tensor[j * 4 * P:(j + 1) * 4 * P, c0:c1].rearrange("(i d) n -> d i n", d=d)
                    return part[bass.ds(row - j * 4 * P, 1)].rearrange("o i n -> (o i) n")
                if d == 16:
                    return tensor[:, c0:c1].rearrange("(i d) n -> d i n", d=d)[bass.ds(row, 1)].rearrange("o i n -> (o i) n")
                return tensor[bass.ds(row, P), c0:c1]

            def load(n, j, u, has, before, row, d):
                g = DIL.index(d)
                b = j % 2
                if before is not None:
                    if not isinstance(n, int) or n >= 2:
                        sp.wait_ge(s["k_T"], n - 1)
                for a, c in ((q_in, 0), (k_in, NG * AW)):
                    sp.dma_start(a[:, b, :], rows(p1, j, row, d, c + g * AW, c + (g + 1) * AW)).then_inc(s[f"loadqk{b}"], 16)
                if not isinstance(n, int) or n >= VS:
                    sp.wait_ge(s["values"], n - VS + 2)
                sp.dma_start(v_in[:, j, :], rows(p1, j, row, d, 2 * NG * AW + g * AW, 2 * NG * AW + (g + 1) * AW))\
                    .then_inc(s[f"loadv{j}"], 16)
            walk(sp, load, lambda n: None)

        @block.tensor
        def _(pe):
            mm, tr = nc.tensor.matmul, nc.tensor.transpose
            pe.wait_ge(s["mask"], 16)

            def scores(n, j, u, has, before, row, d):
                b = j % 2
                pe.wait_ge(s[f"loadqk{b}"], 32 * (2 * u + j // 2 + 1))
                if before is not None:
                    pe.wait_ge(s["kT"], n)
                for p in range(HP):
                    m = tr(b_qk[:, p * P:(p + 1) * P], q_in[:, b, p * P:(p + 1) * P], ident[:])
                m.then_inc(s["q_T"], 1)
                pe.wait_ge(s["qT"], n + 1)
                for p in range(HP):
                    m = tr(b_qk[:, p * P:(p + 1) * P], k_in[:, b, p * P:(p + 1) * P], ident[:])
                m.then_inc(s["k_T"], 1)
                pe.wait_ge(s["kT"], n + 1)
                for i, hs in enumerate(HEADS):
                    if before is not None:
                        pe.wait_ge(s["sm"], H * (n - 1) + 2 * i + 2)
                    for q, h in enumerate(hs):
                        e, p = HD * (h % 2), h // 2
                        o = b_s[i][:, q * 2 * P:(q + 1) * 2 * P]
                        if has:
                            mm(o[:, 0:P], qT[e:e + HD, p, :], kT[e:e + HD, 1 - b, p, :], start=True, stop=True)
                        m = mm(o[:, P:], qT[e:e + HD, p, :], kT[e:e + HD, b, p, :], start=True, stop=True)
                    m.then_inc(s["scores"], 1)

            def values(n, j, has):
                for i, hs in enumerate(HEADS):
                    pe.wait_ge(s["ex"], H * n + 2 * i + 2)
                    if not isinstance(n, int) or n:
                        pe.wait_ge(s[f"eT{i % 2}"], 2 * n + i // 2)
                    elif i // 2:
                        pe.wait_ge(s[f"eT{i % 2}"], 1)
                    for q, h in enumerate(hs):
                        for c in range(0 if has else 1, 2):
                            m = tr(b_e[i % 2][:, (2 * q + c) * P:(2 * q + c + 1) * P], ex[:, j % 2, h, c * P:(c + 1) * P], ident[:])
                    m.then_inc(s[f"e_T{i % 2}"], 1)
                    if i:
                        product(n, j, has, i - 1)
                product(n, j, has, 3)

            def product(n, j, has, i):
                pe.wait_ge(s[f"eT{i % 2}"], 2 * n + i // 2 + 1)
                if i == 0 and not (isinstance(n, int) and n == 0):
                    pe.wait_ge(s["out"], n)
                for q, h in enumerate(HEADS[i]):
                    for c in range(0 if has else 1, 2):
                        vb = j if c else (j - 1) % VS
                        m = mm(b_o[:, h * HD:(h + 1) * HD], eT[:, i % 2, q, c * P:(c + 1) * P], v_in[:, vb, h * HD:(h + 1) * HD],
                               start=(c == 0 or not has), stop=(c == 1))
                if i == 3:
                    m.then_inc(s["values"], 1)

            def step(n, j, u, has, before, row, d):
                scores(n, j, u, has, before, row, d)
                if before is not None:
                    values(n - 1, (j - 1) % 4, before)
                pe.wait_ge(s[f"loadv{j}"], 16 * (u + 1))
            walk(pe, step, lambda n: values(n - 1, 3, False))

        def copy_eT(eng, copy, n, j, has, i):
            eng.wait_ge(s[f"e_T{i % 2}"], 2 * n + i // 2 + 1)
            if i < 2:
                if not (isinstance(n, int) and n == 0):
                    eng.wait_ge(s["values"], n)
            src = b_e[i % 2][:].rearrange("p (q c t) -> p q c t", q=2, c=2)
            dst = eT[:, i % 2, :, :].rearrange("p q (c t) -> p q c t", c=2)
            lo = 0 if has else 1
            copy(dst[:, :, lo:, :], src[:, :, lo:, :]).then_inc(s[f"eT{i % 2}"], 1)

        @block.vector
        def _(dve):
            v = nc.vector
            dve.wait_ge(s["mask"], 16)

            def scores(n, j, u, has, before, row, d):
                dve.wait_ge(s["q_T"], n + 1)
                if before is not None:
                    dve.wait_ge(s["scores"], 4 * n)
                v.tensor_copy(qT[:].rearrange("p a b -> p (a b)"), b_qk[:]).then_inc(s["qT"], 1)
                dve.wait_ge(s["k_T"], n + 1)
                v.tensor_copy(kT[:, j % 2, :, :].rearrange("p a b -> p (a b)"), b_qk[:]).then_inc(s["kT"], 1)
                lo = 0 if has else P
                for i, hs in enumerate(HEADS):
                    dve.wait_ge(s["scores"], 4 * n + i + 1)
                    v.memset(spare[:, i:i + 1], 0.0)
                    for q, h in enumerate(hs):
                        v.tensor_tensor_reduce(out=sm[:, j % 2, h, lo:], in0=b_s[i][:, q * 2 * P + lo:(q + 1) * 2 * P],
                                               in1=mask[:, lo:], scale=SCALE, scalar=NEG, op0=ALU.add, op1=ALU.max,
                                               accum_out=mx[:, h:h + 1]).then_inc(s["sm"], 1)
                dve.wait_ge(s["sm"], H * (n + 1))
                if not isinstance(n, int) or n >= 2:
                    dve.wait_ge(s[f"stored{j % 2}"], 16 * (2 * u + j // 2))
                v.tensor_scalar(out[:, j % 2, AW:AW + H], mx[:], -1.0, None, ALU.mult).then_inc(s["negmax"], 1)

            def copies(n, j, has):
                for i in (0, 2):
                    copy_eT(dve, v.tensor_copy, n, j, has, i)

            def step(n, j, u, has, before, row, d):
                scores(n, j, u, has, before, row, d)
                if before is not None:
                    copies(n - 1, (j - 1) % 4, before)
            walk(dve, step, lambda n: copies(n - 1, 3, False))

        @block.scalar
        def _(act):
            a = nc.scalar
            beside(act)

            def scores(n, j, u, has, before, row, d):
                lo = 0 if has else P
                act.wait_ge(s["negmax"], n + 1)
                for i, hs in enumerate(HEADS):
                    for q, h in enumerate(hs):
                        a.activation(ex[:, j % 2, h, lo:], sm[:, j % 2, h, lo:], ACT.Exp, bias=out[:, j % 2, AW + h:AW + h + 1],
                                     scale=1.0, accum_out=out[:, j % 2, AW + H + h:AW + H + h + 1]).then_inc(s["ex"], 1)

            def copies(n, j, has):
                for i in (1, 3):
                    copy_eT(act, a.copy, n, j, has, i)
                act.wait_ge(s["values"], n + 1)
                a.copy(out[:, j % 2, 0:AW], b_o[:]).then_inc(s["out"], 1)

            def step(n, j, u, has, before, row, d):
                scores(n, j, u, has, before, row, d)
                if before is not None:
                    copies(n - 1, (j - 1) % 4, before)
            walk(act, step, lambda n: copies(n - 1, 3, False))

        @block.gpsimd
        def _(pool):
            def store(n, j, u, has, before, row, d):
                g = DIL.index(d)
                pool.wait_ge(s["out"], n + 1)
                if d == 1:
                    dst = stats_out[bass.ds(row, P), g, :]
                elif d == 4:
                    dst = stats_out[j * 4 * P:(j + 1) * 4 * P, g, :].rearrange("(i d) n -> d i n", d=d)
                    dst = dst[bass.ds(row - j * 4 * P, 1)].rearrange("o i n -> (o i) n")
                else:
                    dst = stats_out[:, g, :].rearrange("(i d) n -> d i n", d=d)[bass.ds(row, 1)].rearrange("o i n -> (o i) n")
                pool.dma_start(dst, out[:, j % 2, :]).then_inc(s[f"stored{j % 2}"], 16)
            walk(pool, store, lambda n: None)
            for b in range(2):
                pool.wait_ge(s[f"stored{b}"], 16 * 3 * NPT // 2)


def merge_windows(nc, stats, p1, p1_sample, o_sample, y_prompt, y_sample):
    Z0 = C_QKV
    with ExitStack() as ctx:
        def sb(name, shape):
            return ctx.enter_context(nc.sbuf_tensor(f"mw_{name}", shape, FP32))

        st = sb("st", [P, SLOTS, NG, ST_W])
        z, tz, zh, gate = sb("z", [P, SLOTS, AW]), sb("tz", [P, AW]), sb("zh", [P, AW]), sb("gate", [P, AW])
        low = sb("low", [P, H])
        w, wd = sb("w", [P, NG, H]), sb("wd", [P, NG, H])
        den = sb("den", [P, H])
        part, o = sb("part", [P, AW]), sb("o", [P, SLOTS, AW])
        s = Sems(nc, ctx, "mw", "loaded0 loaded1 tanh gate diff weights merged gated stored read dve pool")
        block = ctx.enter_context(nc.Block())

        @block.sync
        def _(sp):
            def load(t, b, last=False):
                if last:
                    sp.dma_start(o[0:NS, b, :], o_sample).then_inc(s[f"loaded{b}"], 16)
                    sp.dma_start(z[0:NS, b, :], p1_sample[:, :, Z0:].rearrange("b t n -> (b t) n")).then_inc(s[f"loaded{b}"], 16)
                else:
                    sp.dma_start(st[:, b, :, :], stats[bass.ds(t * P, P), :, :]).then_inc(s[f"loaded{b}"], 16)
                    sp.dma_start(z[:, b, :], p1[bass.ds(t * P, P), Z0:]).then_inc(s[f"loaded{b}"], 16)

            def store(t, b, last=False):
                sp.wait_ge(s["gated"], t + 1)
                if last:
                    sp.dma_start(y_sample, o[0:NS, b, :]).then_inc(s["stored"], 16)
                else:
                    sp.dma_start(y_prompt[bass.ds(t * P, P), :], o[:, b, :]).then_inc(s["stored"], 16)

            sp.sem_inc(s["stored"], 32)
            for b in range(SLOTS):
                load(b, b)
            with sp.Fori(0, PAIRS - 1) as i:
                for b in range(SLOTS):
                    store(2 * i + b, b)
                    load(2 * i + b + SLOTS, b)
            store(NPT - 2, 0)
            sp.wait_ge(s["stored"], 16 * (NPT - 1 + 2))
            load(NPT, 0, last=True)
            store(NPT - 1, 1)
            store(NPT, 0, last=True)
            sp.wait_ge(s["stored"], 16 * (NTILE + 2))

        @block.scalar
        def _(act):
            def gate_in(t, b, u):
                n = NS if u is PAIRS else P
                act.wait_ge(s[f"loaded{b}"], 32 * (u + 1))
                act.wait_ge(s["gate"], t + 1)
                nc.scalar.mul(zh[0:n], z[0:n, b, :], 0.5)
                nc.scalar.activation(tz[0:n], z[0:n, b, :], ACT.Tanh, scale=0.5).then_inc(s["tanh"], 1)

            def tile(t, b, u):
                gate_in(t, b, u)
                act.wait_ge(s["diff"], t + 1)
                nc.scalar.activation(w[:], w[:], ACT.Exp, scale=-1.0).then_inc(s["weights"], 1)
            each_tile(act, tile, tail=False)
            gate_in(NPT, 0, PAIRS)

        @block.vector
        def _(dve):
            v = nc.vector
            ch = Chain(dve, s["dve"], 10)

            def tile(t, b, u):
                ch.start(t)
                x = st[:, b, :, :]
                nm, dn = x[:, :, AW:AW + H], x[:, :, AW + H:]
                dve.wait_ge(s[f"loaded{b}"], 32 * (u + 1))
                ch(v.tensor_tensor(low[:], nm[:, 0, :], nm[:, 1, :], ALU.min))
                ch(v.tensor_tensor(low[:], low[:], nm[:, 2, :], ALU.min))
                v.tensor_tensor(w[:], nm, each(low[:], NG), ALU.subtract).then_inc(s["diff"], 1)
                dve.wait_ge(s["weights"], t + 1)
                ch(v.tensor_tensor(wd[:], w[:], dn, ALU.mult))
                ch(v.tensor_tensor(den[:], wd[:, 0, :], wd[:, 1, :], ALU.add))
                ch(v.tensor_tensor(den[:], den[:], wd[:, 2, :], ALU.add))
                ch(v.reciprocal(den[:], den[:]))
                ch(v.tensor_tensor(w[:], w[:], each(den[:], NG), ALU.mult))
                dve.wait_ge(s["stored"], 16 * (t + 1))
                for g in range(NG):
                    dst = part if g else o[:, b, :]
                    m = v.tensor_tensor(heads(dst if not g else part[:]), heads(x[:, g, 0:AW]), over(w[:, g, :], HD), ALU.mult)
                    if g < 2:
                        ch(m)
                    else:
                        m.then_inc(s["read"], 1)
                        dve.wait_ge(s["read"], t + 1)
                    if g == 1:
                        ch(v.tensor_tensor(o[:, b, :], o[:, b, :], part[:], ALU.add))
                v.tensor_tensor(o[:, b, :], o[:, b, :], part[:], ALU.add).then_inc(s["merged"], 1)
                dve.wait_ge(s["merged"], t + 1)
                ch.end()
            each_tile(dve, tile, tail=False)

        @block.gpsimd
        def _(pool):
            g = nc.gpsimd
            ch = Chain(pool, s["pool"], 1)
            pool.sem_inc(s["gate"], 1)

            def tile(t, b, u):
                n = NS if u is PAIRS else P
                ch.start(t)
                pool.wait_ge(s[f"loaded{b}"], 32 * (u + 1))
                pool.wait_ge(s["tanh"], t + 1)
                ch(g.tensor_tensor(tz[0:n], tz[0:n], zh[0:n], ALU.mult))
                g.tensor_tensor(gate[0:n], tz[0:n], zh[0:n], ALU.add).then_inc(s["gate"], 1)
                pool.wait_ge(s["gate"], t + 2)
                if u is not PAIRS:
                    pool.wait_ge(s["merged"], t + 1)
                ch.end()
                g.tensor_tensor(o[0:n, b, :], o[0:n, b, :], gate[0:n], ALU.mult).then_inc(s["gated"], 1)
            each_tile(pool, tile)


def sample_constants():
    import numpy as np
    t = np.tile(np.arange(DT), H)[:, None]
    m = np.arange(P)[None, :]
    add = lambda ok: np.where(ok, 0.0, NEG).astype(np.float32)
    old = [add((t % 4 == r) & (r + 4 * m >= t)) for r in range(4)]
    old += [add((t == r) & (m >= 0)) for r in range(8)]
    new = np.zeros((DB, H * DT, P + NG * NS), np.float32)
    col = np.arange(NS)[None, :]
    for b in range(DB):
        parts = [add(m >= t)]
        for d in DIL:
            parts.append(add((col // DT == b) & (col % DT <= t) & ((t - col % DT) % d == 0)))
        new[b] = np.concatenate(parts, axis=1)
    return np.concatenate(old, axis=1), new


def sample_attention(nc, ident, p1s, caches, old_mask, new_mask, o_out):
    R = H * DT
    NQ = 3
    QW = 4 * P
    NEW_W = P + NG * NS
    COLS = NQ * QW + NEW_W
    N_OLD = 13
    with ExitStack() as ctx:
        def sb(name, shape):
            return ctx.enter_context(nc.sbuf_tensor(f"sa_{name}", shape, FP32))

        K, V = sb("K", [P, SLOTS, N_OLD, AW]), sb("V", [P, N_OLD, AW])
        Vn = sb("Vn", [P, NG, AW])
        kqn = sb("kqn", [NS, NG, AW])
        Qall = sb("Qall", [P, DB, NG * HP * R])
        Q = sb("Q", [P, NG, HP, R])
        KnT = sb("KnT", [P, NG, HP, NS])
        KT = sb("KT", [P, HP, QW])
        om = sb("om", [R, NQ * QW])
        nm = sb("nm", [R, SLOTS, NEW_W])
        sm, ex = sb("sm", [R, COLS]), sb("ex", [R, COLS])
        mx, neg, den, rden = sb("mx", [R, 4]), sb("neg", [R, 1]), sb("den", [R, 1]), sb("rden", [R, 1])
        spare = sb("spare", [R, 1])
        ET = sb("ET", [P, 16, R])
        yT = sb("yT", [P, HP, NS])
        y = sb("y", [NS, AW])
        bank = [ctx.enter_context(nc.psum_tensor(f"sa_b{i}", [P, 512], FP32)) for i in range(8)]
        s = Sems(nc, ctx, "sa", "in zero q_T q_done kn_T kn_done ready K0 K1 V nm0 nm1 K_T kt0 kt1 q_copied scores sm "
                                "max ex rden scaled e_T e0 e1 out out0 y_T y stored dve act values k_read")
        block = ctx.enter_context(nc.Block())
        c0, c1, c2 = caches

        @block.sync
        def _(sp):
            for g in range(NG):
                sp.dma_start(kqn[:, g, :], p1s[:, :, g * AW:(g + 1) * AW].rearrange("b t n -> (b t) n")).then_inc(s["in"], 16)
            sp.dma_start(om[:], old_mask).then_inc(s["in"], 16)
            sp.wait_ge(s["zero"], 3)
            for g in range(NG):
                c = (2 * NG + g) * AW
                sp.dma_start(Vn[0:NS, g, :], p1s[:, :, c:c + AW].rearrange("b t n -> (b t) n")).then_inc(s["in"], 16)

            def rows(b, which):
                flat = lambda c: c[bass.ds(b, 1), :, which, :, :]
                x1 = flat(c1).rearrange("o (m r) h d -> m (o r) (h d)", r=4)
                x2 = flat(c2).rearrange("o (m r) h d -> m (o r) (h d)", r=16)[:, 0:8, :]
                x0 = flat(c0).rearrange("o m h d -> m o (h d)")
                return x1, x2, x0

            def load(b, slot, u):
                for (lo, hi), src in zip(((0, 4), (4, 12), (12, 13)), rows(b, 0)):
                    sp.dma_start(K[:, slot, lo:hi, :], src).then_inc(s[f"K{slot}"], 16)
                sp.dma_start(nm[:, slot, :], new_mask[bass.ds(b, 1), :, :].rearrange("o r n -> (o r) n")).then_inc(s[f"nm{slot}"], 16)

            def load_v(b):
                for (lo, hi), src in zip(((0, 4), (4, 12), (12, 13)), rows(b, 1)):
                    sp.dma_start(V[:, lo:hi, :], src).then_inc(s["V"], 16)

            sp.wait_ge(s["q_done"], 2 * NG)
            for g in range(NG):
                c = (NG + g) * AW
                sp.dma_start(kqn[:, g, :], p1s[:, :, c:c + AW].rearrange("b t n -> (b t) n")).then_inc(s["in"], 16)
            load(0, 0, 0)
            load(1, 1, 0)
            load_v(0)
            with sp.Fori(0, DB // 2 - 1) as i:
                for slot in range(2):
                    sp.wait_ge(s["zero"], 3)
                    sp.wait_ge(s["sm"], 4 * (2 * i + slot + 1))
                    load(2 * i + slot + 2, slot, i + 1)
                    sp.wait_ge(s["values"], 2 * i + slot + 1)
                    load_v(2 * i + slot + 1)
            sp.wait_ge(s["values"], DB - 1)
            load_v(DB - 1)
            sp.wait_ge(s["y"], 1)
            sp.dma_start(o_out, y[:]).then_inc(s["stored"], 16)
            sp.wait_ge(s["stored"], 16)

        @block.gpsimd
        def _(pool):
            nc.gpsimd.memset(Qall[:].rearrange("p a b -> p (a b)"), 0.0).then_inc(s["zero"], 1)
            nc.gpsimd.memset(Vn[:].rearrange("p a b -> p (a b)"), 0.0).then_inc(s["zero"], 1)
            nc.gpsimd.memset(ET[:].rearrange("p a b -> p (a b)"), 0.0).then_inc(s["zero"], 1)
            pool.wait_ge(s["zero"], 3)

            def own(b, slot, u):
                pool.wait_ge(s["scores"], 4 * b + 1)
                nc.gpsimd.tensor_copy(Q[:].rearrange("p g h r -> p (g h r)"),
                                      Qall[:, bass.ds(b, 1), :].rearrange("p o n -> p (o n)")).then_inc(s["q_copied"], 1)
            pool.wait_ge(s["q_done"], 2 * NG)
            with pool.Fori(0, DB // 2) as i:
                for slot in range(2):
                    own(2 * i + slot, slot, i)

        @block.tensor
        def _(pe):
            mm, tr = nc.tensor.matmul, nc.tensor.transpose
            pe.wait_ge(s["in"], 16 * (2 * NG + 1))
            for g in range(NG):
                for p in range(HP):
                    m = tr(bank[g][:, p * NS:(p + 1) * NS], kqn[:, g, p * P:(p + 1) * P], ident[0:NS, 0:NS])
                m.then_inc(s["q_T"], 1)
            pe.wait_ge(s["in"], 16 * (3 * NG + 1))
            for g in range(NG):
                for p in range(HP):
                    m = tr(bank[4 + g][:, p * NS:(p + 1) * NS], kqn[:, g, p * P:(p + 1) * P], ident[0:NS, 0:NS])
                m.then_inc(s["kn_T"], 1)
            pe.wait_ge(s["q_done"], 2 * NG)
            pe.wait_ge(s["kn_done"], NG)
            pe.sem_inc(s["scores"], 1)

            def sequence(b, slot, u):
                pe.wait_ge(s[f"K{slot}"], 48 * (u + 1))
                pe.wait_ge(s["q_copied"], b + 1)

                def score(q):
                    g = 1 if q == 0 else 2 if q < NQ else 0
                    pe.wait_ge(s["kt0"], 4 * b + q + 2)
                    pe.wait_ge(s["kt1"], 4 * b + q + 2)
                    width = QW if q < NQ else P
                    o = bank[4 + q % 2]
                    if q >= 2:
                        pe.wait_ge(s["sm"], 4 * b + q - 1)
                    for p in range(HP):
                        m = mm(o[0:R, 0:width], Q[:, g, p, :], KT[:, p, 0:width], start=(p == 0), stop=(p == HP - 1))
                    if q == NQ:
                        for g in range(NG):
                            for p in range(HP):
                                m = mm(o[0:R, P + g * NS:P + (g + 1) * NS], Q[:, g, p, :], KnT[:, g, p, :],
                                       start=(p == 0), stop=(p == HP - 1))
                    m.then_inc(s["scores"], 1)

                for q in range(NQ + 1):
                    n = 4 if q < NQ else 1
                    pe.wait_ge(s["kt0"], 4 * b + q + 1)
                    pe.wait_ge(s["kt1"], 4 * b + q + 1)
                    for p in range(HP):
                        for j in range(n):
                            m = tr(bank[p][:, j * P:(j + 1) * P], K[:, slot, 4 * q + j, p * P:(p + 1) * P], ident[:])
                    m.then_inc(s["K_T"] if q < NQ else s["k_read"], 1)
                    score(q)
                pe.wait_ge(s["zero"], 3)
                pe.wait_ge(s["scaled"], b + 1)
                for j in range(16):
                    o = bank[6 + j // 8][:, (j % 8) * R:(j % 8 + 1) * R]
                    if j < N_OLD:
                        m = tr(o, ex[:, j * P:(j + 1) * P], ident[0:R, 0:R])
                    else:
                        c = N_OLD * P + (j - N_OLD) * NS
                        m = tr(o[0:NS, :], ex[:, c:c + NS], ident[0:R, 0:R])
                    if j % 8 == 7:
                        m.then_inc(s["e_T"], 1)
                pe.wait_ge(s["V"], 48 * (b + 1))
                pe.wait_ge(s["e0"], b + 1)
                pe.wait_ge(s["e1"], b + 1)
                for p in range(HP):
                    for j in range(16):
                        w = V[:, j, p * P:(p + 1) * P] if j < N_OLD else Vn[:, j - N_OLD, p * P:(p + 1) * P]
                        m = mm(bank[4][:, p * 2 * DT:(p + 1) * 2 * DT], w, ET[:, j, 2 * p * DT:2 * (p + 1) * DT],
                               start=(j == 0), stop=(j == 15))
                m.then_inc(s["values"], 1)
                pe.wait_ge(s["out"], 2 * b + 2)
            with pe.Fori(0, DB // 2) as i:
                for slot in range(2):
                    sequence(2 * i + slot, slot, i)
            for p in range(HP):
                m = tr(bank[0][0:NS, p * P:(p + 1) * P], yT[:, p, :], ident[:])
            m.then_inc(s["y_T"], 1)

        def copy_kt(eng, copy, b, j):
            for q in range(NQ + 1):
                width = QW if q < NQ else P
                if q < NQ:
                    eng.wait_ge(s["K_T"], NQ * b + q + 1)
                else:
                    eng.wait_ge(s["k_read"], b + 1)
                eng.wait_ge(s["scores"], 4 * b + q + 1)
                for p in (2 * j, 2 * j + 1):
                    m = copy(KT[:, p, 0:width], bank[p][:, 0:width])
                m.then_inc(s[f"kt{j}"], 1)
                yield q

        @block.vector
        def _(dve):
            v = nc.vector
            ch = Chain(dve, s["dve"], 1)
            dve.wait_ge(s["zero"], 3)
            dve.wait_ge(s["in"], 16 * (2 * NG + 1))
            for g in range(NG):
                dve.wait_ge(s["q_T"], g + 1)
                for e in range(2):
                    for p in range(HP):
                        h = 2 * p + e
                        dst = Qall[HD * e:HD * e + HD].rearrange("p b (g h r) -> p g h b r", g=NG, h=HP)[:, g, p, :, h * DT:(h + 1) * DT]
                        m = v.tensor_copy(dst, bank[g][HD * e:HD * e + HD, p * NS:(p + 1) * NS].rearrange("p (b t) -> p b t", t=DT))
                    m.then_inc(s["q_done"], 1)
            dve.sem_inc(s["kt0"], 1)

            def sequence(b, slot, u):
                ch.start(b)
                copies = copy_kt(dve, v.tensor_copy, b, 0)
                for q in range(NQ + 1):
                    next(copies)
                    dve.wait_ge(s["scores"], 4 * b + q + 2)
                    if q == 0:
                        dve.wait_ge(s[f"nm{slot}"], 16 * (u + 1))
                    v.memset(spare[:], 0.0)
                    width = QW if q < NQ else NEW_W
                    mask = om[:, q * QW:q * QW + QW] if q < NQ else nm[:, slot, :]
                    v.tensor_tensor_reduce(out=sm[:, q * QW:q * QW + width], in0=bank[4 + q % 2][0:R, 0:width], in1=mask,
                                           scale=SCALE, scalar=NEG, op0=ALU.add, op1=ALU.max,
                                           accum_out=mx[:, q:q + 1]).then_inc(s["sm"], 1)
                for _ in copies:
                    pass
                dve.wait_ge(s["sm"], 4 * b + 4)
                v.tensor_reduce(neg[:], mx[:], AX.X, ALU.max, negate=True).then_inc(s["max"], 1)
                dve.wait_ge(s["ex"], b + 1)
                v.reciprocal(rden[:], den[:]).then_inc(s["rden"], 1)
                dve.wait_ge(s["rden"], b + 1)
                v.tensor_scalar(ex[:], ex[:], rden[:], None, ALU.mult).then_inc(s["scaled"], 1)
                dve.wait_ge(s["e_T"], 2 * b + 1)
                v.tensor_copy(ET[:, 0:8, :].rearrange("p a b -> p (a b)"), bank[6][:]).then_inc(s["e0"], 1)
                dve.wait_ge(s["values"], b + 1)
                for e in range(2):
                    src = bank[4][HD * e:HD * e + HD, 0:HP * 2 * DT].rearrange("p (h e t) -> p h e t", h=HP, e=2)[:, :, e, :]
                    v.tensor_copy(yT[HD * e:HD * e + HD, :, bass.ds(b * DT, DT)], src).then_inc(s["out"], 1)
            with dve.Fori(0, DB // 2) as i:
                for slot in range(2):
                    sequence(2 * i + slot, slot, i)
            dve.wait_ge(s["y_T"], 1)
            v.tensor_copy(y[:], bank[0][0:NS, :]).then_inc(s["y"], 1)

        @block.scalar
        def _(act):
            a = nc.scalar
            for g in range(NG):
                act.wait_ge(s["kn_T"], g + 1)
                a.copy(KnT[:, g, :, :].rearrange("p h r -> p (h r)"), bank[4 + g][:, 0:HP * NS]).then_inc(s["kn_done"], 1)
            act.sem_inc(s["kt1"], 1)
            act.wait_ge(s["zero"], 3)

            def sequence(b, slot, u):
                for _ in copy_kt(act, a.copy, b, 1):
                    pass
                act.wait_ge(s["max"], b + 1)
                a.activation(ex[:], sm[:], ACT.Exp, bias=neg[:], scale=1.0, accum_out=den[:]).then_inc(s["ex"], 1)
                act.wait_ge(s["e_T"], 2 * b + 2)
                a.copy(ET[:, 8:13, :].rearrange("p a b -> p (a b)"), bank[7][:, 0:5 * R])
                a.copy(ET[0:NS, 13:16, :].rearrange("p a b -> p (a b)"), bank[7][0:NS, 5 * R:]).then_inc(s["e1"], 1)
            with act.Fori(0, DB // 2) as i:
                for slot in range(2):
                    sequence(2 * i + slot, slot, i)


ARGS = ("x_prompt x_sample state_rwkv state_shift state_conv cache_kv_w128 cache_kv_w512 cache_kv_w2048 "
        "even_w_in even_w_out rwkv_mu rwkv_w0 rwkv_w2 rwkv_a0 rwkv_a2 rwkv_k_k rwkv_k_a rwkv_r_k rwkv_gn_g "
        "rwkv_gn_b conv_w odd_w_in odd_w_out ln_g ln_b").split()
WINDOWS = (128, 512, 2048)
OUTS = {
    "y_prompt": (1, SEQ, D), "y_sample": (DB, DT, D),
    "rwkv_prompt": (1, 1, H, HD, HD), "rwkv_sample": (1, DB, H, HD, HD),
    "shift_prompt": (1, 1, SHIFT_W), "shift_sample": (1, DB, SHIFT_W),
    "conv_prompt": (1, 1, 2, AW), "conv_sample": (1, DB, 2, AW),
}
for _w in WINDOWS:
    OUTS[f"kv{_w}_prompt"] = (1, 1, _w, 2, H, HD)
    OUTS[f"kv{_w}_sample"] = (1, DB, _w, 2, H, HD)


def decoder_step(nc, a, o, c):
    scratch = lambda name, *shape: nc.dram_tensor(f"s_{name}", shape, FP32, kind="Internal").ap()
    p_pad, ps_pad = scratch("p0", PAD + SEQ, EVEN_W), scratch("p0s", DB, PAD + DT, EVEN_W)
    y0, y0s = scratch("y0", SEQ, EVEN_MIX), scratch("y0s", NS, EVEN_MIX)
    scan_in, scan_y = scratch("scan_in", 6, DB, H, DT, HD), scratch("scan_y", DB, H, DT, HD)
    x1, x1s = scratch("x1", SEQ, D), scratch("x1s", NS, D)
    p1, p1s = scratch("p1", SEQ, ODD_W), scratch("p1s", DB, DT, ODD_W)
    stats, o1s = scratch("stats", SEQ, NG, ST_W), scratch("o1s", NS, AW)
    y1, y1s = scratch("y1", SEQ, AW), scratch("y1s", NS, AW)
    caches = [a[f"cache_kv_w{w}"][0] for w in WINDOWS]
    kv_s = [o[f"kv{w}_sample"][0] for w in WINDOWS]
    kv_p = [o[f"kv{w}_prompt"][0, 0] for w in WINDOWS]
    PIECES = 10

    with ExitStack() as ctx:
        ident = ctx.enter_context(nc.sbuf_tensor("ident", [P, P], FP32))
        sw = {n: ctx.enter_context(nc.semaphore(n)) for n in
              "padded ei_w_loaded0 ei_w_loaded1 oi_w_loaded0 oi_w_loaded1 conv_out conv_s_out out_stored0 out_stored1".split()}
        kv_stored = ctx.enter_context(nc.semaphore("kv_stored"))

        def shift_caches(eng, chunk, odd_one):
            for w, cache, out in zip(WINDOWS, caches, kv_s):
                n = (w - DT) // PIECES
                lo, rows = (PIECES * n, w - DT - PIECES * n) if odd_one else (chunk * n, n)
                if rows:
                    eng.dma_start(out[:, bass.ds(lo, rows)].rearrange("b r k h d -> b r (k h d)"),
                                  cache[:, bass.ds(lo + DT, rows)].rearrange("b r k h d -> b r (k h d)"))\
                       .then_inc(kv_stored, 16)

        def new_keys(eng):
            for g, w in enumerate(WINDOWS):
                for kv in range(2):
                    cols = slice(((1 + kv) * NG + g) * AW, ((1 + kv) * NG + g + 1) * AW)
                    eng.dma_start(kv_p[g][:, kv].rearrange("r h d -> r (h d)"), p1[SEQ - w:, cols]).then_inc(kv_stored, 16)
                    eng.dma_start(kv_s[g][:, w - DT:, kv].rearrange("b r h d -> b r (h d)"), p1s[:, :, cols])\
                       .then_inc(kv_stored, 16)

        KV_STORES = 3 * PIECES + 1 + 4 * NG
        with nc.sbuf_tensor("xT", [P, KD, NTOK], FP32) as xT:
            transpose_in(nc, a["x_prompt"], a["x_sample"], xT, ident, p_pad, ps_pad, a["state_shift"][0], a["state_conv"][0], sw)
            project_in(nc, "ei", xT, a["even_w_in"][0], 384, 11, p_pad[PAD:], ps_pad[:, PAD:], sw, shift_caches)
        rw = [a[f"rwkv_{n}"][0] for n in "mu w0 w2 a0 a2 k_k k_a r_k gn_g gn_b".split()]
        even_mix(nc, ident, p_pad, ps_pad, c["rwkv"], a["state_rwkv"][0], rw, a["conv_w"][0], y0, y0s, scan_in, scan_y,
                 o["rwkv_prompt"][0, 0], o["rwkv_sample"][0], o["shift_prompt"][0], o["shift_sample"][0],
                 o["conv_prompt"][0, 0], o["conv_sample"][0], sw)
        with nc.sbuf_tensor("x1T", [P, KD, NTOK], FP32) as xT:
            project_out(nc, "eo", ident, y0, y0s, EVEN_MIX, a["even_w_out"][0], a["x_prompt"][0],
                        a["x_sample"].rearrange("b t d -> (b t) d"), a["ln_g"][0], a["ln_b"][0], x1, x1s, xT)
            project_in(nc, "oi", xT, a["odd_w_in"][0], 512, 10, p1, p1s, sw)
        window_attention(nc, ident, p1, c["window"], stats, sw, new_keys)
        sample_attention(nc, ident, p1s, caches, c["sample_old"], c["sample_new"], o1s)
        merge_windows(nc, stats, p1, p1s, o1s, y1, y1s)
        project_out(nc, "oo", ident, y1, y1s, AW, a["odd_w_out"][0], x1, x1s, a["ln_g"][1], a["ln_b"][1],
                    o["y_prompt"][0], o["y_sample"].rearrange("b t d -> (b t) d"), None)
        with nc.Block() as block:
            @block.sync
            def _(sp):
                sp.wait_ge(kv_stored, 16 * KV_STORES)


EVEN_MIX = 2 * AW


def kernel(**inputs):
    import numpy as np
    import concourse.bacc as bacc
    from concourse.bass_utils import run_bass_kernel_spmd

    nc = bacc.Bacc("TRN2", target_bir_lowering=False, num_devices=1)
    sample_old, sample_new = sample_constants()
    constants = {"rwkv": rwkv_constants(), "window": window_constants(), "sample_old": sample_old, "sample_new": sample_new}
    arrays = {f"in_{n}": np.ascontiguousarray(inputs[n]) for n in ARGS}
    arrays.update({f"const_{n}": v for n, v in constants.items()})
    aps = {n: nc.dram_tensor(n, v.shape, FP32, kind="ExternalInput").ap() for n, v in arrays.items()}
    outs = {n: nc.dram_tensor(f"out_{n}", shape, FP32, kind="ExternalOutput").ap() for n, shape in OUTS.items()}
    decoder_step(nc, {n: aps[f"in_{n}"] for n in ARGS}, outs, {n: aps[f"const_{n}"] for n in constants})
    r = run_bass_kernel_spmd(nc, [arrays], core_ids=[0]).results[0]
    return tuple(r[f"out_{n}"] for n in OUTS)
```

```python
import concourse.bass as bass
from concourse import mybir
from contextlib import ExitStack

FP32 = mybir.dt.float32
FP32R = mybir.dt.float32r
ALU = mybir.AluOpType
ACT = mybir.ActivationFunctionType
AX = mybir.AxisListType

P = 128
D = 1024
KD = D // P
SEQ = 2048
NPT = SEQ // P
DB, DT = 8, 8
NS = DB * DT
NTOK = SEQ + NS
NTILE = NPT + 1
PAIRS = NPT // 2
H, HD = 8, 64
AW = H * HD
SHIFT_W = 3 * AW + 2 * HD
EVEN_W = SHIFT_W + AW + 4 * AW
NG = 3
ODD_W = 3 * NG * AW + AW
PAD = 2
R0, K0, V0, L0, ZA0, B0, C0, HH0, ZB0 = 0, AW, 2 * AW, 3 * AW, SHIFT_W, SHIFT_W + AW, SHIFT_W + 2 * AW, \
    SHIFT_W + 3 * AW, SHIFT_W + 4 * AW
SLOTS = 2


def each_tile(eng, body, tail=True):
    with eng.Fori(0, PAIRS) as i:
        for s in range(SLOTS):
            body(2 * i + s, s, i)
    if tail:
        body(NPT, 0, PAIRS)


class Sems(dict):

    def __init__(self, nc, ctx, phase, names, own={}):
        self.nc, self.own = nc, own
        self.update(own)
        for n in names.split():
            self[n] = ctx.enter_context(nc.semaphore(f"{phase}_{n}"))
        ctx.callback(self.clear)

    def clear(self):
        with self.nc.Block() as block:
            @block.sync
            def _(sp):
                for n, sem in self.items():
                    if n not in self.own:
                        sp.sem_clear(sem)


def transpose_in(nc, x_prompt, x_sample, x_high, x_low, ident, p_pad, ps_pad, state_shift, state_conv, sw):
    with ExitStack() as ctx:
        xin = ctx.enter_context(nc.sbuf_tensor("ti_x", [P, SLOTS, D], FP32))
        tp = [ctx.enter_context(nc.psum_tensor(f"ti_p{i}", [P, 4, P], FP32)) for i in range(2 * SLOTS)]
        zeros = ctx.enter_context(nc.sbuf_tensor("ti_zero", [PAD, SHIFT_W], FP32))
        ones = ctx.enter_context(nc.sbuf_tensor("ti_one", [DB, PAD, AW], FP32))
        s = Sems(nc, ctx, "ti", "ident_zero ident x_loaded0 x_loaded1 transposed high split filled", {"padded": sw["padded"]})
        block = ctx.enter_context(nc.Block())

        @block.gpsimd
        def _(pool):
            nc.gpsimd.memset(ident[:], 0.0).then_inc(s["ident_zero"], 1)
            pool.wait_ge(s["ident_zero"], 1)
            nc.gpsimd.affine_select(out=ident[:], in_=ident[:], compare_op=ALU.not_equal, fill=1.0, base=0,
                                    pattern=[[-1, P]], channel_multiplier=1).then_inc(s["ident"], 1)
            nc.gpsimd.memset(zeros[:], 0.0).then_inc(s["filled"], 1)
            nc.gpsimd.memset(ones[:].rearrange("b a n -> b (a n)"), 1.0).then_inc(s["filled"], 1)
            pool.wait_ge(s["filled"], 2)
            for dst, src in ((p_pad[0:PAD, C0:C0 + 2 * AW], zeros[:, 0:2 * AW]), (p_pad[PAD - 1:PAD, 0:SHIFT_W], zeros[0:1, :]),
                             (ps_pad[:, 0:PAD, HH0:HH0 + AW], ones[:]), (ps_pad[:, 0:PAD, C0:HH0], state_conv),
                             (ps_pad[:, PAD - 1, 0:SHIFT_W], state_shift)):
                pool.dma_start(dst, src).then_inc(s["padded"], 16)
            pool.wait_ge(s["padded"], 16 * 5)

        @block.sync
        def _(sp):
            def load(t, b, u):
                sp.wait_ge(s["transposed"], t + 1)
                src = x_prompt[0, bass.ds(t * P, P), :] if u is not PAIRS else x_sample.rearrange("b t d -> (b t) d")
                rows = P if u is not PAIRS else NS
                sp.dma_start(xin[0:rows, b, :], src).then_inc(s[f"x_loaded{b}"], 16)
            each_tile(sp, load)

        @block.tensor
        def _(pe):
            pe.sem_inc(s["transposed"], SLOTS)
            pe.wait_ge(s["ident"], 1)

            def turn(t, b, u):
                rows = P if u is not PAIRS else NS
                pe.wait_ge(s[f"x_loaded{b}"], 16 * (u + 1))
                pe.wait_ge(s["split"], 2 * t + 2)
                for k in range(KD):
                    mm = nc.tensor.transpose(tp[2 * b + k // 4][:, k % 4, 0:rows], xin[0:rows, b, k * P:(k + 1) * P],
                                             ident[0:rows, 0:rows])
                mm.then_inc(s["transposed"], 1)
            each_tile(pe, turn)

        def halves(t, b, rows):
            at = lambda x, i: x[:, 4 * i:4 * i + 4, bass.ds(t * P, rows)]
            return [(tp[2 * b + i][:, :, 0:rows], at(x_high, i), at(x_low, i)) for i in range(2)]

        @block.vector
        def _(dve):
            dve.sem_inc(s["split"], 2 * SLOTS)

            def low(t, b, u):
                for i, (src, high, dst) in enumerate(halves(t, b, P if u is not PAIRS else NS)):
                    dve.wait_ge(s["high"], 2 * t + i + 1)
                    nc.vector.tensor_tensor(dst, src, high.bitcast(FP32), ALU.subtract).then_inc(s["split"], 1)
            each_tile(dve, low)

        @block.scalar
        def _(act):
            def high(t, b, u):
                act.wait_ge(s["transposed"], t + 1 + SLOTS)
                for src, dst, _ in halves(t, b, P if u is not PAIRS else NS):
                    nc.scalar.copy(dst, src).then_inc(s["high"], 1)
            each_tile(act, high)


def project_in(nc, ph, x_high, x_low, w, cw, n_chunks, p_prompt, p_sample, sw, beside=None):
    NB = 4
    PER = NPT // NB
    with ExitStack() as ctx:
        wc = ctx.enter_context(nc.sbuf_tensor(f"{ph}_w", [P, KD, cw], FP32))
        one = ctx.enter_context(nc.sbuf_tensor(f"{ph}_one", [P, 1], FP32))
        w_high = ctx.enter_context(nc.sbuf_tensor(f"{ph}_w_high", [P, SLOTS, KD, cw], FP32R))
        w_low = ctx.enter_context(nc.sbuf_tensor(f"{ph}_w_low", [P, SLOTS, KD, cw], FP32R))
        stage = ctx.enter_context(nc.sbuf_tensor(f"{ph}_stage", [P, NB + 1, cw], FP32))
        ps = [ctx.enter_context(nc.psum_tensor(f"{ph}_ps{i}", [P, 512], FP32)) for i in range(NB + 1)]
        s = Sems(nc, ctx, ph, "one w_high w_split chunk_done tile_done even_out odd_out "
                              "stored0 stored1 stored2 stored3 stored4",
                 {f"w_loaded{b}": sw[f"{ph}_w_loaded{b}"] for b in range(SLOTS)})
        n_even, n_odd = NPT // 2 + 1, NPT // 2

        def each_chunk(eng, body):
            with eng.Fori(0, n_chunks // 2) as i:
                for b in range(SLOTS):
                    body(2 * i + b, b, i)

        block = ctx.enter_context(nc.Block())

        @block.gpsimd
        def _(pool):
            def load(c, b, u):
                pool.wait_ge(s["w_split"], c + 1)
                pool.wait_ge(s["chunk_done"], c + 1)
                pool.dma_start(wc[:], w[:, bass.ds(c * cw, cw)].rearrange("(k p) n -> p k n", p=P))\
                    .then_inc(s[f"w_loaded{b}"], 16)
                pool.wait_ge(s[f"w_loaded{b}"], 16 * (u + 1))
                nc.gpsimd.tensor_tensor(w_high[:, b, :, :].rearrange("p k n -> p (k n)"), wc[:].rearrange("p k n -> p (k n)"),
                                        one[:].broadcast_to([P, KD * cw]), ALU.mult).then_inc(s["w_high"], 1)
                pool.wait_ge(s["w_high"], c + 1)
                nc.gpsimd.tensor_tensor(w_low[:, b, :, :], wc[:], w_high[:, b, :, :].bitcast(FP32), ALU.subtract)\
                    .then_inc(s["w_split"], 1)
            nc.gpsimd.memset(one[:], 1.0).then_inc(s["one"], 1)
            pool.wait_ge(s["one"], 1)
            pool.sem_inc(s["w_split"], 1)
            each_chunk(pool, load)

        @block.tensor
        def _(pe):
            pe.sem_inc(s["chunk_done"], SLOTS)

            def chunk(c, b, u):
                pe.wait_ge(s["w_split"], c + 2)
                for t in range(NTILE):
                    bank, rows = (t % NB, P) if t < NPT else (NB, NS)
                    if t % 2 == 0:
                        pe.wait_ge(s["even_out"], c * n_even + 1 + (max(t - NB + 2, 0) // 2))
                    else:
                        pe.wait_ge(s["odd_out"], c * n_odd + 1 + (max(t - NB + 1, 0) // 2))
                    for k in range(KD):
                        for i, (x, y) in enumerate(((x_high, w_high), (x_high, w_low), (x_low, w_high))):
                            mm = nc.tensor.matmul(ps[bank][0:rows, 0:cw], x[:, k, t * P:t * P + rows], y[:, b, k, :],
                                                  start=(k == 0 and i == 0), stop=(k == KD - 1 and i == 2))
                    if t < NPT:
                        mm.then_inc(s["tile_done"], 1)
                    else:
                        mm.then_inc(s["chunk_done"], 1)
            each_chunk(pe, chunk)

        def copy_out(eng, copy, parity, n_mine, out_sem):
            eng.sem_inc(out_sem, 1)

            def chunk(c, b, u):
                if parity and b == 0 and beside:
                    beside(eng, u)
                for t in range(parity, NTILE, 2):
                    bank, rows = (t % NB, P) if t < NPT else (NB, NS)
                    if t < NPT:
                        eng.wait_ge(s["tile_done"], c * NPT + t + 1)
                        eng.wait_ge(s[f"stored{bank}"], 16 * (c * PER + t // NB) + 1)
                    else:
                        eng.wait_ge(s["chunk_done"], c + 1 + SLOTS)
                        eng.wait_ge(s[f"stored{bank}"], 16 * c + 1)
                    copy(stage[0:rows, bank, :], ps[bank][0:rows, 0:cw]).then_inc(out_sem, 1)
            each_chunk(eng, chunk)

        @block.vector
        def _(dve):
            copy_out(dve, nc.vector.tensor_copy, 0, n_even, s["even_out"])

        @block.scalar
        def _(act):
            copy_out(act, nc.scalar.copy, 1, n_odd, s["odd_out"])

        @block.sync
        def _(sp):
            for b in range(NB + 1):
                sp.sem_inc(s[f"stored{b}"], 1)

            def chunk(c, b, u):
                for t in range(NTILE):
                    bank, rows = (t % NB, P) if t < NPT else (NB, NS)
                    if t % 2 == 0:
                        sp.wait_ge(s["even_out"], c * n_even + t // 2 + 2)
                    else:
                        sp.wait_ge(s["odd_out"], c * n_odd + t // 2 + 2)
                    cols = bass.ds(c * cw, cw)
                    dst = p_prompt[t * P:t * P + rows, cols] if t < NPT else p_sample[:, :, cols]
                    sp.dma_start(dst, stage[0:rows, bank, :]).then_inc(s[f"stored{bank}"], 16)
            each_chunk(sp, chunk)
            for b in range(NB):
                sp.wait_ge(s[f"stored{b}"], 16 * n_chunks * PER + 1)
            sp.wait_ge(s[f"stored{NB}"], 16 * n_chunks + 1)


CHUNK = 64
NCH = P // CHUNK
HP = H // 2
LEVELS = 6
LD_SCALE = -0.6065306597126334
GN_EPS = 64e-5
LN_EPS = 1e-5
ALPHA = 4 ** 0.25


def rwkv_constants():
    import numpy as np
    i = np.arange(P)
    same = (i[:, None] // CHUNK) == (i[None, :] // CHUNK)
    upto = same & (i[:, None] <= i[None, :])
    before = same & (i[:, None] < i[None, :])
    off = [(i[:, None] // (2 * m) == i[None, :] // (2 * m)) & (i[:, None] // m > i[None, :] // m)
           for m in (1, 2, 4, 8, 16, 32)]
    eye64 = (i[:, None] % HD) == np.arange(HD)[None, :]
    chunk = (i[:, None] // CHUNK) == np.arange(NCH)[None, :]
    cols = [upto, before, upto, before, upto, off[0].T, *off[1:], eye64, chunk]
    return np.ascontiguousarray(np.concatenate([c.astype(np.float32) for c in cols], axis=1))


CONST_W = 5 * P + LEVELS * P + HD + NCH


class Chain:

    def __init__(self, eng, sem, per_tile):
        self.eng, self.sem, self.per_tile = eng, sem, per_tile

    def start(self, t, n=0):
        self.t, self.n = t, n

    def __call__(self, ins):
        self.n += 1
        ins.then_inc(self.sem, 1)
        self.eng.wait_ge(self.sem, self.t * self.per_tile + self.n)

    def end(self):
        assert self.n == self.per_tile, (self.n, self.per_tile)


def heads(ap):
    return ap.rearrange("p (h d) -> p h d", h=H)


def pairs(bank):
    return bank[:, 0:AW // 2].rearrange("p (h d) -> p h d", d=HD)


def over(ap, n):
    return ap.unsqueeze(2).broadcast_to([ap.shape[0], ap.shape[1], n])


def each(ap, n):
    return ap.unsqueeze(1).broadcast_to([ap.shape[0], n, ap.shape[1]])


def even_mix(nc, ident, p_pad, ps_pad, consts, state_rwkv, rw, conv_w, y_prompt, y_sample, scan_in, scan_y,
             state_p_out, state_s_out, shift_p_out, shift_s_out, conv_p_out, conv_s_out, sw):
    mu, w0, w2, a0, a2, k_k, k_a, r_k, gn_g, gn_b = rw
    with ExitStack() as ctx:
        def sb(name, shape):
            return ctx.enter_context(nc.sbuf_tensor(f"em_{name}", shape, FP32))

        cur = sb("cur", [P, SLOTS, EVEN_W])
        ps = sb("ps", [P, SLOTS, SHIFT_W])
        V = sb("V", [P, SLOTS, AW])
        ch1, ch2 = sb("ch1", [P, 2 * AW]), sb("ch2", [P, 2 * AW])
        cst = sb("cst", [P, CONST_W])
        mu_b = sb("mu", [P, SHIFT_W])
        par = sb("par", [P, 10, AW])
        w2a2 = sb("w2a2", [P, 2, AW])
        W0, A0, KK, KA, RK, GG, GB, CW = 0, 1, 2, 3, 4, 5, 6, 7
        lora = sb("lora", [P, P])
        wa = sb("wa", [P, 2 * AW])
        pc_, pinv, pprev = sb("pc", [P, AW]), sb("pinv", [P, AW]), sb("pprev", [P, AW])
        pend = sb("pend", [P, SLOTS, HP * NCH])
        kk, sq = sb("kk", [P, AW]), sb("sq", [P, AW])
        kn = kk
        bv, kp = sb("bv", [P, AW]), sb("kp", [P, AW])
        rt, bt, kt = sb("rt", [P, AW]), sb("bt", [P, SLOTS, AW]), sb("kt", [P, SLOTS, AW])
        za = sb("za", [P, SLOTS, 2, H, HD])
        ss, rs, bonus = sb("ss", [P, H]), sb("rs", [P, H]), sb("bonus", [P, H])
        half = sb("half", [P, H])
        ZR = sb("ZR", [P, 2, HP, 2, P])
        BT, KT = sb("BT", [P, HP, P]), sb("KT", [P, HP, P])
        AM = sb("AM", [P, H, 4, P])
        T, X = sb("T", [P, H, P]), sb("X", [P, H, P])
        Ym = sb("Ym", [P, H, P])
        WU = sb("WU", [P, H, 2, HD])
        QT = sb("QT", [P, HP, P])
        M1, G = sb("M1", [P, NCH, HP, HD]), sb("G", [P, NCH, HP, HD])
        M_BANK, G_BANK = (2, 7), (4, 0)
        S = sb("S", [P, NCH, HP, HD])
        yl = Ym[:, 0:4, :].rearrange("p h n -> p (h n)")
        y = sb("y", [P, AW])
        mean, var, rstd = sb("mean", [P, H]), sb("var", [P, H]), sb("rstd", [P, H])
        u0 = sb("u0", [P, AW])
        rkv = sb("rkv", [P, SLOTS, AW])
        tz = sb("tz", [P, 2 * AW])
        gate = sb("gate", [P, SLOTS, AW])
        yout = sb("yout", [P, SLOTS, 2 * AW])
        bank = [ctx.enter_context(nc.psum_tensor(f"em_b{i}", [P, 512], FP32)) for i in range(8)]
        sc_z, sc_b, sc_w, sc_k, sc_r = [AM[:, i, :, :].rearrange("p a b -> p (a b)") for i in range(5)]
        sc_v = AM[:, 5, 0:2, :].rearrange("p a b -> p (a b)")
        sc_y = AM[:, 6, 0:2, :].rearrange("p a b -> p (a b)")
        sa = AM[:, 7, 0, 0:32]
        state = cur[:, 1, 0:2048].rearrange("p (i j) -> p i j", j=HD)
        outer = cur[:, 1, 2048:4096].rearrange("p (i j) -> p i j", j=HD)
        outer2 = ps[:, :, :].rearrange("p a b -> p (a b)")[:, 0:2048].rearrange("p (i j) -> p i j", j=HD)
        s_vk = yout[0:HD, 1, 0:H * HD]

        s = Sems(nc, ctx, "em",
                 "cst loaded0 loaded1 ch_loaded half zero shifted conv lora_T lora lora_mm wa_in tanh ld kk sq "
                 "ss rs kp rk bonus cum cprev exps zbk rt zrbk_T0 zrbk_T1 zrbk_T2 zrbk_T3 zrbk_out a_mm masked x1 "
                 "t1_T t1 y_mm ym d_mm t_add x_T x_out av_mm av wu_mm wu q_mm yl_mm m_mm q m1 yl g_mm g_out s_mm "
                 "s_new y_cross y_sum centred ysq var rstd ynorm gates gated stored state_out y_back s_T s_vk rkv "
                 "dve_p dve_c dve_n act pool_s pool_c pool_f scan_out scan_loaded vk vk_free scan_y",
                 {n: sw[n] for n in ("conv_out", "conv_s_out")})
        block = ctx.enter_context(nc.Block())
        c_tri = cst[:, 0:P]
        c_zr = cst[:, P:5 * P]
        c_off = [cst[:, (5 + i) * P:(6 + i) * P] for i in range(LEVELS)]
        c_eye = cst[:, 11 * P:11 * P + HD]
        c_chunk = cst[:, 11 * P + HD:11 * P + HD + NCH]
        LOADS, CSTS = 2, 14
        STATE_OUTS = 2 + 2 + 1
        L = LEVELS - 1

        def rows_of(t):
            return NS if isinstance(t, int) and t == NPT else P

        def walk(eng, step, peeled=1):
            step(0, 0, 0)
            step(1, 1, 0)
            with eng.Fori(1, PAIRS - peeled) as i:
                step(2 * i, 0, i)
                step(2 * i + 1, 1, i)
            for t in range(NPT - 2 * peeled, NPT):
                step(t, t % 2, t // 2)

        def first(t):
            return isinstance(t, int) and t == 0

        def final(t):
            return isinstance(t, int) and t == NPT - 1

        @block.sync
        def _(sp):
            row = lambda a: a.rearrange("(o n) -> o n", o=1)
            sp.wait_ge(s["zero"], 2)

            def load(t, b):
                n = rows_of(t)
                for dst, j, lo, hi in ((cur, 0, 0, EVEN_W), (ps, 1, 0, SHIFT_W)):
                    src = (ps_pad[:, PAD - j:PAD - j + DT, lo:hi] if n == NS else p_pad[bass.ds(t * P + PAD - j, P), lo:hi])
                    sp.dma_start(dst[0:n, b, :], src).then_inc(s[f"loaded{b}"], 16)

            def load_ch(t):
                n = rows_of(t)
                for dst, j in ((ch1, 1), (ch2, 2)):
                    src = ps_pad[:, PAD - j:PAD - j + DT, C0:ZB0] if n == NS else p_pad[bass.ds(t * P + PAD - j, P), C0:ZB0]
                    sp.dma_start(dst[0:n, :], src).then_inc(s["ch_loaded"], 16)

            def store(t, b):
                sp.wait_ge(s["gated"], t + 1)
                n = rows_of(t)
                dst = y_sample if n == NS else y_prompt[bass.ds(t * P, P), :]
                sp.dma_start(dst, yout[0:n, b, :]).then_inc(s["stored"], 16)

            load(0, 0)
            load_ch(0)
            for dst, src in ((mu_b[:], row(mu)), *[(par[:, j, :], row(a)) for j, a in
                             enumerate((w0, a0, k_k, k_a, r_k.rearrange("h d -> (h d)"), gn_g, gn_b,
                                        conv_w[0], conv_w[1], conv_w[2]))]):
                sp.dma_start(dst, src.broadcast_to([P, src.shape[1]])).then_inc(s["cst"], 16)
            sp.dma_start(cst[:], consts).then_inc(s["cst"], 16)
            sp.dma_start(w2a2[0:HD, 0, :], w2).then_inc(s["cst"], 16)
            sp.dma_start(w2a2[HD:P, 1, :], a2).then_inc(s["cst"], 16)
            sp.sem_inc(s["stored"], 32)
            load(1, 1)

            def prepared(t):
                sp.wait_ge(s["conv"], t + 1)
                if not (isinstance(t, int) and t >= NPT):
                    load_ch(t + 1)
                sp.wait_ge(s["rt"], t + 1)
                sp.wait_ge(s["zbk"], t + 1)

            prepared(0)
            load(2, 0)

            def step(t, b, u):
                if not first(t):
                    store(t - 1, 1 - b)
                if final(t):
                    return
                prepared(t + 1)
                if not (isinstance(t, int) and t + 3 > NPT):
                    load(t + 3, 1 - b)
            walk(sp, step, peeled=2)
            store(NPT - 1, 1)
            store(NPT, 0)
            sp.dma_start(shift_p_out, p_pad[PAD + SEQ - 1:PAD + SEQ, 0:SHIFT_W]).then_inc(s["state_out"], 16)
            sp.dma_start(shift_s_out, ps_pad[:, PAD + DT - 1, 0:SHIFT_W]).then_inc(s["state_out"], 16)
            sp.wait_ge(s["stored"], 16 * (NTILE + 2))
            sp.wait_ge(s["state_out"], 16 * STATE_OUTS)

        @block.gpsimd
        def _(pool):
            g = nc.gpsimd
            ch_s, ch_c, ch_f = (Chain(pool, s[f"pool_{c}"], n) for c, n in (("s", 2), ("c", 11), ("f", 2)))
            g.memset(w2a2[:].rearrange("p a n -> p (a n)"), 0.0).then_inc(s["zero"], 1)
            g.memset(ZR[:].rearrange("p a b c d -> p (a b c d)"), 0.0).then_inc(s["zero"], 1)
            g.memset(half[:], -0.5).then_inc(s["half"], 1)
            pool.wait_ge(s["half"], 1)
            pool.wait_ge(s["zero"], 2)
            pool.wait_ge(s["cst"], 16 * CSTS)

            def shift(t, b, u):
                n = rows_of(t)
                ch_s.start(t)
                pool.wait_ge(s[f"loaded{b}"], 16 * LOADS * (u + 1))
                c, x = cur[0:n, b, 0:SHIFT_W], ps[0:n, b, :]
                ch_s(g.tensor_tensor(x, x, c, ALU.subtract))
                ch_s(g.tensor_tensor(x, x, mu_b[0:n, :], ALU.mult))
                if not (isinstance(t, int) and t < SLOTS):
                    pool.wait_ge(s["g_mm"], NCH * (t - 1))
                g.tensor_tensor(V[0:n, b, :], x[:, V0:L0], c[:, V0:L0], ALU.add)
                g.tensor_tensor(x[:, L0:], x[:, L0:], c[:, L0:], ALU.add)
                g.tensor_tensor(x[:, 0:V0], x[:, 0:V0], c[:, 0:V0], ALU.add).then_inc(s["shifted"], 1)
                pool.wait_ge(s["shifted"], t + 1)
                ch_s.end()

            def norm_k(t):
                n = rows_of(t)
                pool.wait_ge(s["ss"], t + 1)
                g.tensor_tensor(rs[0:n], ss[0:n], half[0:n], ALU.pow).then_inc(s["rs"], 1)

            def conv(t, b):
                n = rows_of(t)
                c = cur[0:n, b, :]
                ch_c.start(t)
                pool.wait_ge(s["ch_loaded"], 32 * (t + 1))
                a1, b1, a2_, b2 = ch1[0:n, 0:AW], ch1[0:n, AW:], ch2[0:n, 0:AW], ch2[0:n, AW:]
                ch_c(g.tensor_tensor(u0[0:n], c[:, C0:HH0], c[:, HH0:ZB0], ALU.mult))
                ch_c(g.tensor_tensor(a1, a1, b1, ALU.mult))
                ch_c(g.tensor_tensor(a2_, a2_, b2, ALU.mult))
                ch_c(g.tensor_tensor(a2_, a2_, par[0:n, CW, :], ALU.mult))
                ch_c(g.tensor_tensor(a1, a1, par[0:n, CW + 1, :], ALU.mult))
                ch_c(g.tensor_tensor(b1, u0[0:n], par[0:n, CW + 2, :], ALU.mult))
                ch_c(g.tensor_tensor(a1, a1, a2_, ALU.add))
                ch_c(g.tensor_tensor(a1, a1, b1, ALU.add))
                ch_c(g.tensor_tensor(a1, a1, c[:, B0:C0], ALU.mult))
                pool.wait_ge(s["gates"], t + 1)
                g.tensor_tensor(gate[0:n, b, :], tz[0:n, 0:AW], c[:, ZA0:B0], ALU.mult)
                ch_c(g.tensor_tensor(tz[0:n, AW:], tz[0:n, AW:], c[:, ZB0:], ALU.mult))
                pool.wait_ge(s["stored"], 16 * (t + 1))
                ch_c(g.tensor_tensor(yout[0:n, b, AW:], a1, tz[0:n, AW:], ALU.mult))
                pool.sem_inc(s["conv"], 1)
                ch_c.end()

            def bonus_in(t, b):
                n = rows_of(t)
                r = ps[0:n, b, R0:K0]
                pool.wait_ge(s["kp"], t + 1)
                g.tensor_tensor(sq[0:n], r, kp[0:n], ALU.mult).then_inc(s["rk"], 1)
                pool.wait_ge(s["rk"], 2 * t + 1)
                g.tensor_tensor(sq[0:n], sq[0:n], par[0:n, RK, :], ALU.mult).then_inc(s["rk"], 1)
                if n == P:
                    pool.wait_ge(s["exps"], t + 1)
                    g.tensor_tensor(rt[0:n], r, pc_[0:n], ALU.mult).then_inc(s["rt"], 1)
                pool.wait_ge(s["bonus"], t + 1)
                g.tensor_tensor(heads(rkv[0:n, b, :]), heads(V[0:n, b, :]), over(bonus[0:n], HD), ALU.mult).then_inc(s["rkv"], 1)

            def finish_a(t):
                n = rows_of(t)
                pool.wait_ge(s["var"], t + 1)
                g.tensor_tensor(rstd[0:n], var[0:n], half[0:n], ALU.pow).then_inc(s["rstd"], 1)

            def finish(t, b):
                n = rows_of(t)
                ch_f.start(t)
                finish_a(t)
                pool.wait_ge(s["ynorm"], t + 1)
                ch_f(g.tensor_tensor(y[0:n], y[0:n], par[0:n, GB, :], ALU.add))
                ch_f(g.tensor_tensor(y[0:n], y[0:n], rkv[0:n, b, :], ALU.add))
                g.tensor_tensor(yout[0:n, b, 0:AW], y[0:n], gate[0:n, b, :], ALU.mult).then_inc(s["gated"], 1)
                pool.wait_ge(s["gated"], t + 1)
                ch_f.end()

            shift(0, 0, 0)
            norm_k(0)
            conv(0, 0)
            bonus_in(0, 0)
            shift(1, 1, 0)

            def step(t, b, u):
                if not first(t):
                    finish(t - 1, 1 - b)
                norm_k(t + 1)
                conv(t + 1, 1 - b)
                bonus_in(t + 1, 1 - b)
                if not final(t):
                    shift(t + 2, b, u + 1)
                if isinstance(t, int) and t == NPT - 2:
                    pool.dma_start(conv_p_out, u0[P - 2:P, :]).then_inc(s["conv_out"], 16)
                    pool.wait_ge(s["conv_out"], 16)
            walk(pool, step)
            for q in range(DB):
                pool.dma_start(conv_s_out[q], u0[DT * q + DT - 2:DT * q + DT, :]).then_inc(s["conv_s_out"], 16)
            finish(NPT - 1, 1)
            pool.wait_ge(s["scan_loaded"], 16 * 14)
            for i in range(DT):
                if i:
                    pool.wait_ge(s["vk_free"], i)
                g.tensor_tensor(outer2, over(sc_v[:, 32 * i:32 * i + 32], HD),
                                each(sc_k[:, HD * i:HD * i + HD], 32), ALU.mult).then_inc(s["vk"], 1)
            finish(NPT, 0)
            pool.wait_ge(s["conv_s_out"], 16 * DB)

        @block.vector
        def _(dve):
            v = nc.vector
            ch_p, ch_c, ch_n = (Chain(dve, s[f"dve_{c}"], n) for c, n in (("p", 6), ("c", 3 + NCH), ("n", 4)))
            dve.wait_ge(s["cst"], 16 * CSTS)
            v.memset(S[:, 0, :, :], 0.0).then_inc(s["s_new"], 1)
            dve.wait_ge(s["s_new"], 1)

            def prep_k(t, b):
                n = rows_of(t)
                ch_p.start(t)
                dve.wait_ge(s["shifted"], t + 1)
                v.tensor_tensor(kk[0:n], ps[0:n, b, K0:V0], par[0:n, KK, :], ALU.mult).then_inc(s["kk"], 1)

            def prep_ss(t):
                n = rows_of(t)
                dve.wait_ge(s["sq"], t + 1)
                ch_p(v.tensor_reduce(ss[0:n], heads(sq[0:n]), AX.X, ALU.add))
                v.tensor_scalar(ss[0:n], ss[0:n], 1e-24, None, ALU.max).then_inc(s["ss"], 1)

            def prep_wa(t):
                n = rows_of(t)
                dve.wait_ge(s["lora_mm"], t + 1)
                ch_p(v.tensor_tensor(wa[0:n, 0:AW], bank[7][0:n, :], par[0:n, W0, :], ALU.add))
                v.tensor_tensor(wa[0:n, AW:], bank[6][0:n, :], par[0:n, A0, :], ALU.add).then_inc(s["wa_in"], 1)

            def prep_kp(t, b):
                n = rows_of(t)
                k, a = ps[0:n, b, K0:V0], wa[0:n, AW:]
                dve.wait_ge(s["tanh"], t + 1)
                ch_p(v.tensor_scalar(a, a, 0.5, 0.5, ALU.mult, ALU.add))
                dve.wait_ge(s["rs"], t + 1)
                ch_p(v.tensor_tensor(heads(kn[0:n]), heads(kk[0:n]), over(rs[0:n], HD), ALU.mult))
                ch_p(v.tensor_tensor(bv[0:n], kn[0:n], a, ALU.mult))
                ch_p(v.scalar_tensor_tensor(kp[0:n], a, -1.0, par[0:n, KA, :], ALU.add, ALU.mult))
                v.scalar_tensor_tensor(kp[0:n], kp[0:n], 1.0, k, ALU.add, ALU.mult).then_inc(s["kp"], 1)

            def prep_ld(t):
                n = rows_of(t)
                dve.wait_ge(s["tanh"], t + 1)
                v.tensor_scalar(wa[0:n, 0:AW], wa[0:n, 0:AW], LD_SCALE / 2, LD_SCALE / 2, ALU.mult, ALU.add)\
                    .then_inc(s["ld"], 1)

            def prep_cprev(t):
                dve.wait_ge(s["cum"], t + 1)
                v.tensor_tensor(pprev[:], bank[4][:], wa[:, 0:AW], ALU.subtract).then_inc(s["cprev"], 1)

            def prep_end(t, b):
                n = rows_of(t)
                if n == P:
                    dve.wait_ge(s["exps"], t + 1)
                    v.tensor_tensor(bt[:, b, :], bv[:], pinv[:], ALU.mult)
                    v.tensor_tensor(kt[:, b, :], kp[:], pinv[:], ALU.mult)
                    v.scalar_tensor_tensor(za[:, b, 0, :, :], heads(kn[:]), -1.0, heads(pprev[:]), ALU.mult, ALU.mult)\
                        .then_inc(s["zbk"], 1)
                dve.wait_ge(s["rk"], 2 * t + 2)
                v.tensor_reduce(bonus[0:n], heads(sq[0:n]), AX.X, ALU.add).then_inc(s["bonus"], 1)
                dve.wait_ge(s["bonus"], t + 1)
                ch_p.end()

            def prep_all(t, b):
                prep_k(t, b)
                prep_ss(t)
                prep_wa(t)
                prep_ld(t)
                prep_kp(t, b)
                prep_cprev(t)
                prep_end(t, b)

            def norm_a(t):
                n = rows_of(t)
                yh = heads(y[0:n])
                ch_n.start(t)
                ch_n(v.tensor_reduce(mean[0:n], yh, AX.X, ALU.add))
                ch_n(v.tensor_scalar(mean[0:n], mean[0:n], 1.0 / HD, None, ALU.mult))
                v.tensor_tensor(yh, yh, over(mean[0:n], HD), ALU.subtract).then_inc(s["centred"], 1)

            def norm_b(t):
                n = rows_of(t)
                ch_n.start(t, 2)
                dve.wait_ge(s["ysq"], t + 1)
                ch_n(v.tensor_reduce(var[0:n], heads(sq[0:n]), AX.X, ALU.add))
                v.tensor_scalar(var[0:n], var[0:n], 1.0 / HD, GN_EPS, ALU.mult, ALU.add).then_inc(s["var"], 1)

            def norm_c(t):
                n = rows_of(t)
                yh = heads(y[0:n])
                ch_n.start(t, 3)
                dve.wait_ge(s["rstd"], t + 1)
                ch_n(v.tensor_tensor(yh, yh, over(rstd[0:n], HD), ALU.mult))
                v.tensor_tensor(y[0:n], y[0:n], par[0:n, GG, :], ALU.mult).then_inc(s["ynorm"], 1)

            def step(t, b, u):
                sample_next = final(t)
                ch_c.start(t)
                for h in range(H):
                    dve.wait_ge(s["a_mm"], H * t + h + 1)
                    v.tensor_tensor(AM[:, h, :, :].rearrange("p a b -> p (a b)"), bank[h % 4][:], c_zr, ALU.mult)\
                        .then_inc(s["masked"], 1)
                dve.wait_ge(s["masked"], H * (t + 1))
                for g in range(2):
                    hs = slice(4 * g, 4 * g + 4)
                    ch_c(v.tensor_tensor(X[:, hs, :], AM[:, hs, 0, :], each(c_off[0], 4), ALU.mult))
                    v.tensor_tensor(X[:, hs, :], X[:, hs, :], each(ident[:], 4), ALU.add).then_inc(s["x1"], 1)
                for lv in range(1, LEVELS):
                    for g in range(2):
                        hs = slice(4 * g, 4 * g + 4)
                        dve.wait_ge(s["y_mm"], 2 * (L * t + lv - 1) + g + 1)
                        v.tensor_tensor(Ym[:, hs, :], bank[g][:].rearrange("p (h n) -> p h n", h=4),
                                        each(c_off[lv], 4), ALU.mult).then_inc(s["ym"], 1)
                    for g in range(2):
                        hs = slice(4 * g, 4 * g + 4)
                        dve.wait_ge(s["d_mm"], 2 * (L * t + lv - 1) + g + 1)
                        M = T if lv < LEVELS - 1 else X
                        v.tensor_tensor(M[:, hs, :], M[:, hs, :], bank[2 + g][:].rearrange("p (h n) -> p h n", h=4),
                                        ALU.add).then_inc(s["t_add"], 1)
                    if lv == 1:
                        if not first(t):
                            norm_b(t - 1)
                        prep_k(t + 1, 1 - b)
                    elif lv == 2:
                        if not first(t):
                            norm_c(t - 1)
                        prep_ss(t + 1)
                    elif lv == 3:
                        prep_wa(t + 1)
                    elif lv == 4:
                        prep_ld(t + 1)
                        prep_kp(t + 1, 1 - b)
                if not sample_next:
                    prep_cprev(t + 1)
                dve.wait_ge(s["q_mm"], t + 1)
                for e in range(2):
                    r_ = slice(HD * e, HD * e + HD)
                    m = v.tensor_tensor(QT[r_], bank[0][r_].rearrange("p (h n) -> p h n", h=HP), ZR[r_, e, :, 1, :], ALU.add)
                m.then_inc(s["q"], 1)
                dve.wait_ge(s["m_mm"], t + 1)
                for c in range(NCH):
                    v.tensor_tensor(M1[:, c, :, :], pairs(bank[M_BANK[c]]), each(c_eye, HP), ALU.add)\
                        .then_inc(s["m1"], 1)
                prep_end(t + 1, 1 - b)
                for c in range(NCH):
                    dve.wait_ge(s["s_mm"], NCH * t + c + 1)
                    if c == NCH - 1:
                        dve.wait_ge(s["y_cross"], 2 * t + 1)
                    dve.wait_ge(s["g_out"], NCH * t + c + 1)
                    new = S[:, (c + 1) % NCH, :, :]
                    ch_c(v.tensor_tensor(new, pairs(bank[3]), G[:, c, :, :], ALU.add))
                    v.tensor_tensor(new, new, over(pend[:, b, c::NCH], HD), ALU.mult).then_inc(s["s_new"], 1)
                dve.wait_ge(s["y_cross"], 2 * t + 2)
                dve.wait_ge(s["yl"], t + 1)
                if not first(t):
                    dve.wait_ge(s["gated"], t)
                y4, yl4 = [a.rearrange("p (h e d) -> p h e d", e=2, d=HD) for a in (y[:], yl)]
                ch_c(v.tensor_tensor(y4[:, :, 0, :], yl4[:, :, 0, :], pairs(bank[5]), ALU.add))
                v.tensor_tensor(y4[:, :, 1, :], yl4[:, :, 1, :], pairs(bank[6]), ALU.add).then_inc(s["y_sum"], 1)
                dve.wait_ge(s["y_sum"], t + 1)
                ch_c.end()
                norm_a(t)

            prep_all(0, 0)
            walk(dve, step)
            norm_b(NPT - 1)
            norm_c(NPT - 1)

            steps = Chain(dve, s["dve_c"], 0)
            steps.t, steps.n = 0, NPT * ch_c.per_tile
            dve.wait_ge(s["scan_loaded"], 16 * 14)
            for i in range(DT):
                z, bb, w, rr = [a[:, HD * i:HD * i + HD] for a in (sc_z, sc_b, sc_w, sc_r)]
                steps(v.tensor_tensor(outer, state, each(z, 32), ALU.mult))
                steps(v.tensor_reduce(sa, outer, AX.X, ALU.add))
                steps(v.tensor_tensor(state, state, each(w, 32), ALU.mult))
                steps(v.tensor_tensor(outer, over(sa, HD), each(bb, 32), ALU.mult))
                steps(v.tensor_tensor(state, state, outer, ALU.add))
                dve.wait_ge(s["vk"], i + 1)
                v.tensor_tensor(state, state, outer2, ALU.add).then_inc(s["vk_free"], 1)
                dve.wait_ge(s["vk_free"], i + 1)
                steps(v.tensor_tensor(outer, state, each(rr, 32), ALU.mult))
                last = v.tensor_reduce(sc_y[:, 32 * i:32 * i + 32], outer, AX.X, ALU.add)
                if i < DT - 1:
                    steps(last)
                else:
                    last.then_inc(s["scan_y"], 1)
            dve.wait_ge(s["y_back"], 16 * DB)
            norm_a(NPT)
            norm_b(NPT)
            norm_c(NPT)

        @block.scalar
        def _(act):
            a = nc.scalar
            act.wait_ge(s["zero"], 2)

            def prep_lora(t, b, u):
                n = rows_of(t)
                act.wait_ge(s["lora_T"], t + 1)
                a.activation(lora[0:HD, 0:n], bank[7][0:HD, 0:n], ACT.Tanh).then_inc(s["lora"], 1)
                a.copy(lora[HD:P, 0:n], bank[7][HD:P, 0:n]).then_inc(s["lora"], 1)
                act.wait_ge(s[f"loaded{b}"], 16 * LOADS * (u + 1))
                if not first(t):
                    act.wait_ge(s["conv"], t)
                a.activation(tz[0:n, 0:AW], cur[0:n, b, ZA0:B0], ACT.Tanh, scale=0.5)
                a.activation(tz[0:n, AW:], cur[0:n, b, ZB0:], ACT.Tanh, scale=0.5).then_inc(s["act"], 1)
                act.wait_ge(s["act"], t + 1)
                a.activation(tz[0:n], tz[0:n], ACT.Copy, bias=0.5, scale=0.5).then_inc(s["gates"], 1)

            def prep_sq(t):
                n = rows_of(t)
                act.wait_ge(s["kk"], t + 1)
                a.activation(sq[0:n], kk[0:n], ACT.Square).then_inc(s["sq"], 1)

            def prep_tanh(t):
                n = rows_of(t)
                act.wait_ge(s["wa_in"], t + 1)
                a.activation(wa[0:n], wa[0:n], ACT.Tanh, scale=0.5).then_inc(s["tanh"], 1)

            def prep_exps(t, b):
                act.wait_ge(s["cprev"], t + 1)
                a.activation(pinv[:], bank[4][:], ACT.Exp, scale=-1.0)
                a.activation(pc_[:], bank[4][:], ACT.Exp)
                a.activation(pend[:, b, :], bank[5][:, 0:HP * NCH], ACT.Exp)
                a.activation(pprev[:], pprev[:], ACT.Exp).then_inc(s["exps"], 1)

            def step(t, b, u):
                for j, dst in enumerate((0, 1, BT, KT)):
                    act.wait_ge(s[f"zrbk_T{j}"], t + 1)
                    src = bank[4 + j][:].rearrange("p (h n) -> p h n", h=HP)
                    if j < 2:
                        for e in range(2):
                            r_ = slice(HD * e, HD * e + HD)
                            m = a.copy(ZR[r_, e, :, j, :], src[r_])
                        m.then_inc(s["zrbk_out"], 1)
                    else:
                        a.copy(dst[:], src).then_inc(s["zrbk_out"], 1)
                act.wait_ge(s["av_mm"], t + 1)
                a.copy(za[:, b, 1, :, :], heads(bank[6][:])).then_inc(s["av"], 1)
                act.wait_ge(s["t1_T"], 2 * t + 1)
                a.copy(T[:, 0:4, :], bank[4][:].rearrange("p (h n) -> p h n", h=4)).then_inc(s["t1"], 1)
                act.wait_ge(s["t1_T"], 2 * t + 2)
                a.copy(T[:, 4:8, :], bank[5][:].rearrange("p (h n) -> p h n", h=4)).then_inc(s["t1"], 1)
                for lv in range(1, LEVELS - 1):
                    for g in range(2):
                        act.wait_ge(s["x_T"], 2 * ((L - 1) * t + lv - 1) + g + 1)
                        a.copy(X[:, 4 * g:4 * g + 4, :], bank[4 + g][:].rearrange("p (h n) -> p h n", h=4))\
                            .then_inc(s["x_out"], 1)
                    if lv == 1:
                        prep_lora(t + 1, 1 - b, u + b)
                    elif lv == 2:
                        prep_sq(t + 1)
                    elif lv == 3:
                        prep_tanh(t + 1)
                if not final(t):
                    prep_exps(t + 1, 1 - b)
                for g in range(2):
                    act.wait_ge(s["wu_mm"], 2 * t + g + 1)
                    a.copy(WU[:, 4 * g:4 * g + 4, :, :].rearrange("p h a d -> p (h a d)"), bank[6 + g][:]).then_inc(s["wu"], 1)
                act.wait_ge(s["yl_mm"], t + 1)
                a.copy(yl, bank[1][:]).then_inc(s["yl"], 1)
                for c in range(NCH):
                    act.wait_ge(s["g_mm"], NCH * t + c + 1)
                    a.copy(G[:, c, :, :], pairs(bank[G_BANK[c]])).then_inc(s["g_out"], 1)
                centred_sq(t)

            def centred_sq(t):
                n = rows_of(t)
                act.wait_ge(s["centred"], t + 1)
                a.activation(sq[0:n], y[0:n], ACT.Square).then_inc(s["ysq"], 1)

            prep_lora(0, 0, 0)
            prep_sq(0)
            prep_tanh(0)
            prep_exps(0, 0)
            walk(act, step)

            act.wait_ge(s["bonus"], NPT + 1)
            act.wait_ge(s["rkv"], NPT + 1)
            a.activation(pc_[0:NS], wa[0:NS, 0:AW], ACT.Exp).then_inc(s["act"], 1)
            a.mul(pinv[0:NS], kn[0:NS], -1.0).then_inc(s["act"], 1)
            act.wait_ge(s["act"], NPT + 3)
            act.wait_ge(s["gated"], NPT)
            for j, src in enumerate((pinv[0:NS], bv[0:NS], pc_[0:NS], kp[0:NS], ps[0:NS, 0, R0:K0], V[0:NS, 0, :])):
                for q in range(DB):
                    act.dma_start(scan_in[j, q].rearrange("h t d -> t h d"), heads(src[DT * q:DT * q + DT, :]))\
                        .then_inc(s["scan_out"], 16)
            act.wait_ge(s["scan_out"], 16 * 6 * DB)
            for j, dst in enumerate((sc_z, sc_b, sc_w, sc_k, sc_r)):
                for i in range(2):
                    act.dma_start(dst[64 * i:64 * i + 64, :],
                                  scan_in[j].rearrange("b h t d -> (b h) (t d)")).then_inc(s["scan_loaded"], 16)
            for i in range(2):
                act.dma_start(sc_v[64 * i:64 * i + 64, :].rearrange("p (t d) -> p t d", t=DT),
                              scan_in[5].rearrange("b h t (a d) -> a (b h) t d", a=2)[i])\
                    .then_inc(s["scan_loaded"], 16)
                act.dma_start(state[64 * i:64 * i + 64], state_rwkv.rearrange("b h (a i) j -> a (b h) i j", a=2)[i])\
                    .then_inc(s["scan_loaded"], 16)
            act.wait_ge(s["scan_y"], 1)
            for i in range(2):
                act.dma_start(scan_y.rearrange("b h t (a d) -> a (b h) t d", a=2)[i],
                              sc_y[64 * i:64 * i + 64, :].rearrange("p (t d) -> p t d", t=DT)).then_inc(s["scan_out"], 16)
                act.dma_start(state_s_out.rearrange("b h (a i) j -> a (b h) i j", a=2)[i], state[64 * i:64 * i + 64])\
                    .then_inc(s["state_out"], 16)
            act.wait_ge(s["scan_out"], 16 * (6 * DB + 2))
            for q in range(DB):
                act.dma_start(heads(y[DT * q:DT * q + DT, :]), scan_y[q].rearrange("h t d -> t h d"))\
                    .then_inc(s["y_back"], 16)
            act.wait_ge(s["s_T"], 1)
            act.wait_ge(s["stored"], 16 * (NPT + 2))
            a.copy(s_vk, bank[0][0:HD, :]).then_inc(s["s_vk"], 1)
            act.wait_ge(s["s_vk"], 1)
            act.dma_start(state_p_out.rearrange("h i j -> i h j"), s_vk.rearrange("p (h j) -> p h j", h=H))\
                .then_inc(s["state_out"], 16)
            centred_sq(NPT)

        @block.tensor
        def _(pe):
            mm, tr = nc.tensor.matmul, nc.tensor.transpose
            pe.wait_ge(s["cst"], 16 * CSTS)
            pe.wait_ge(s["zero"], 2)
            cols = [slice(h * HD, (h + 1) * HD) for h in range(H)]

            def prep_lora_T(t, b):
                n = rows_of(t)
                pe.wait_ge(s["shifted"], t + 1)
                tr(bank[7][:, 0:n], ps[0:n, b, L0:], ident[0:n, 0:n]).then_inc(s["lora_T"], 1)

            def prep_lora(t):
                n = rows_of(t)
                pe.wait_ge(s["lora"], 2 * t + 2)
                mm(bank[7][0:n, :], lora[:, 0:n], w2a2[:, 0, :], start=True, stop=True)
                mm(bank[6][0:n, :], lora[:, 0:n], w2a2[:, 1, :], start=True, stop=True).then_inc(s["lora_mm"], 1)

            def prep_cum(t):
                pe.wait_ge(s["ld"], t + 1)
                mm(bank[4][:], c_tri, wa[:, 0:AW], start=True, stop=True)
                for p in range(HP):
                    m = mm(bank[5][:, NCH * p:NCH * (p + 1)], wa[:, p * P:(p + 1) * P], c_chunk, start=True, stop=True)
                m.then_inc(s["cum"], 1)

            def step(t, b, u):
                v = V[:, b, :]
                z = za[:, b, 0, :, :].rearrange("p h d -> p (h d)")
                pe.wait_ge(s["zbk"], t + 1)
                pe.wait_ge(s["rt"], t + 1)
                if not first(t):
                    pe.wait_ge(s["y_sum"], t)
                pair = lambda src, p: src[:, p * P:(p + 1) * P]
                for j, src in enumerate((z, rt[:], bt[:, b, :], kt[:, b, :])):
                    for p in range(HP):
                        m = tr(bank[4 + j][:, p * P:(p + 1) * P], pair(src, p), ident[:])
                    m.then_inc(s[f"zrbk_T{j}"], 1)
                pe.wait_ge(s["zrbk_out"], 4 * t + 4)
                for h in range(H):
                    e, p = h % 2, h // 2
                    if h >= 4:
                        pe.wait_ge(s["masked"], H * t + h - 3)
                    zr = ZR[:, e, p, :, :].rearrange("p a b -> p (a b)")
                    mm(bank[h % 4][:, 0:2 * P], BT[:, p, :], zr, start=True, stop=True)
                    mm(bank[h % 4][:, 2 * P:], KT[:, p, :], zr, start=True, stop=True).then_inc(s["a_mm"], 1)
                pe.wait_ge(s["masked"], H * (t + 1))
                for h in range(H):
                    m = mm(bank[6][:, cols[h]], AM[:, h, 2, :], v[:, cols[h]], start=True, stop=True)
                m.then_inc(s["av_mm"], 1)
                for g in range(2):
                    pe.wait_ge(s["x1"], 2 * t + g + 1)
                    for h in range(4 * g, 4 * g + 4):
                        m = tr(bank[4 + g][:, (h % 4) * P:(h % 4 + 1) * P], X[:, h, :], ident[:])
                    m.then_inc(s["t1_T"], 1)
                for lv in range(1, LEVELS):
                    for g in range(2):
                        if lv == 1:
                            pe.wait_ge(s["t1"], 2 * t + g + 1)
                        else:
                            pe.wait_ge(s["t_add"], 2 * (L * t + lv - 2) + g + 1)
                        for h in range(4 * g, 4 * g + 4):
                            m = mm(bank[g][:, (h % 4) * P:(h % 4 + 1) * P], AM[:, h, 0, :], T[:, h, :], start=True, stop=True)
                        m.then_inc(s["y_mm"], 1)
                    if lv == 1:
                        pe.wait_ge(s["av"], t + 1)
                    for g in range(2):
                        pe.wait_ge(s["ym"], 2 * (L * t + lv - 1) + g + 1)
                        if lv > 1:
                            pe.wait_ge(s["x_out"], 2 * ((L - 1) * t + lv - 2) + g + 1)
                        for h in range(4 * g, 4 * g + 4):
                            o = bank[2 + g][:, (h % 4) * P:(h % 4 + 1) * P]
                            if lv < LEVELS - 1:
                                m = mm(o, X[:, h, :], Ym[:, h, :], start=True, stop=True)
                            else:
                                m = mm(o, Ym[:, h, :], X[:, h, :], start=True, stop=True)
                        m.then_inc(s["d_mm"], 1)
                    if lv < LEVELS - 1:
                        if lv == 1:
                            prep_lora_T(t + 1, 1 - b)
                        elif lv == 2:
                            prep_lora(t + 1)
                        for g in range(2):
                            pe.wait_ge(s["t_add"], 2 * (L * t + lv - 1) + g + 1)
                            for h in range(4 * g, 4 * g + 4):
                                m = tr(bank[4 + g][:, (h % 4) * P:(h % 4 + 1) * P], T[:, h, :], ident[:])
                            m.then_inc(s["x_T"], 1)
                    elif not final(t):
                        prep_cum(t + 1)
                pe.wait_ge(s["t_add"], 2 * L * (t + 1))
                pe.wait_ge(s["wa_in"], t + 2)
                for g in range(2):
                    for h in range(4 * g, 4 * g + 4):
                        m = mm(bank[6 + g][:, (h % 4) * P:(h % 4 + 1) * P], X[:, h, :],
                               za[:, b, :, h, :], start=True, stop=True)
                    m.then_inc(s["wu_mm"], 1)
                pe.wait_ge(s["wu"], 2 * t + 2)
                for h in range(H):
                    e, p = HD * (h % 2), h // 2
                    m = mm(bank[0][e:e + HD, p * P:(p + 1) * P], WU[:, h, 0, :], AM[:, h, 1, :], start=True, stop=True)
                m.then_inc(s["q_mm"], 1)
                for c in range(NCH):
                    cs = slice(c * CHUNK, (c + 1) * CHUNK)
                    for h in range(H):
                        e, p = HD * (h % 2), h // 2
                        m = mm(bank[M_BANK[c]][e:e + HD, p * HD:(p + 1) * HD], WU[cs, h, 0, :], bt[cs, b, cols[h]], start=True, stop=True)
                m.then_inc(s["m_mm"], 1)
                for h in range(H):
                    mm(bank[1][:, cols[h]], AM[:, h, 1, :], WU[:, h, 1, :], start=True, stop=False)
                    m = mm(bank[1][:, cols[h]], AM[:, h, 3, :], v[:, cols[h]], start=False, stop=True)
                m.then_inc(s["yl_mm"], 1)
                pe.wait_ge(s["cst"], 16 * CSTS)
                pe.wait_ge(s["q"], t + 1)
                if not final(t):
                    pe.wait_ge(s["exps"], t + 2)
                for c in range(NCH):
                    cs = slice(c * CHUNK, (c + 1) * CHUNK)
                    for h in range(H):
                        e, p = HD * (h % 2), h // 2
                        o = bank[G_BANK[c]][e:e + HD, p * HD:(p + 1) * HD]
                        mm(o, bt[cs, b, cols[h]], WU[cs, h, 1, :], start=True, stop=False)
                        m = mm(o, kt[cs, b, cols[h]], v[cs, cols[h]], start=False, stop=True)
                    m.then_inc(s["g_mm"], 1)
                for c in range(NCH):
                    cs = slice(c * CHUNK, (c + 1) * CHUNK)
                    pe.wait_ge(s["cst"], 16 * CSTS)
                    pe.wait_ge(s["s_new"], NCH * t + c + 1)
                    pe.wait_ge(s["m1"], NCH * t + c + 1)
                    for h in range(H):
                        e, p = HD * (h % 2), h // 2
                        m = mm(bank[3][e:e + HD, p * HD:(p + 1) * HD], M1[e:e + HD, c, p, :], S[e:e + HD, c, p, :],
                               start=True, stop=True)
                    m.then_inc(s["s_mm"], 1)
                    for h in range(H):
                        e, p = HD * (h % 2), h // 2
                        m = mm(bank[5 + h % 2][cs, p * HD:(p + 1) * HD], QT[e:e + HD, p, cs], S[e:e + HD, c, p, :], start=True, stop=True)
                    m.then_inc(s["y_cross"], 1)

            prep_lora_T(0, 0)
            prep_lora(0)
            prep_cum(0)
            walk(pe, step)
            pe.wait_ge(s["s_new"], NCH * NPT + 1)
            for p in range(HP):
                m = tr(bank[0][0:HD, p * P:(p + 1) * P], S[:, 0, p, :], ident[:])
            m.then_inc(s["s_T"], 1)


def project_out(nc, ph, ident, y_prompt, y_sample, width, w, x_prompt, x_sample, ln_g, ln_b, out_prompt, out_sample, xT=None):
    KW = width // P
    HALF = D // 2
    with ExitStack() as ctx:
        def sb(name, shape):
            return ctx.enter_context(nc.sbuf_tensor(f"{ph}_{name}", shape, FP32))

        ws = sb("w", [P, KW, D])
        g_b, b_b = sb("g", [P, D]), sb("b", [P, D])
        yin = sb("yin", [P, width])
        yT = sb("yT", [P, KW, P])
        res = sb("res", [P, SLOTS, D])
        stats, mv, spare = sb("stats", [P, 2, 6]), sb("mv", [P, 2]), sb("spare", [P, 1])
        rstd, half = sb("rstd", [P, 1]), sb("half", [P, 1])
        bank = [ctx.enter_context(nc.psum_tensor(f"{ph}_b{i}", [P, 512], FP32)) for i in range(8)]
        s = Sems(nc, ctx, ph, "w half y_loaded x_loaded0 x_loaded1 y_T yT0 yT1 products res var rstd scaled normed stored "
                              "x_T x_high x_split dve pool")
        block = ctx.enter_context(nc.Block())
        WS = 3

        def rows(last):
            return NS if last else P

        @block.sync
        def _(sp):
            def load_y(t, last=False):
                sp.wait_ge(s["y_T"], t + 1)
                sp.dma_start(yin[0:rows(last), :], y_sample if last else y_prompt[bass.ds(t * P, P), :])\
                    .then_inc(s["y_loaded"], 16)

            def load_x(t, b, last=False):
                sp.wait_ge(s["stored"], 16 * (t + 1))
                if xT is not None:
                    sp.wait_ge(s["x_T"], t + 1)
                xs = x_sample if last else x_prompt[bass.ds(t * P, P), :]
                sp.dma_start(res[0:rows(last), b, :], xs).then_inc(s[f"x_loaded{b}"], 16)

            def store(t, b, last=False):
                sp.wait_ge(s["normed"], t + 1)
                dst = out_sample if last else out_prompt[bass.ds(t * P, P), :]
                sp.dma_start(dst, res[0:rows(last), b, :]).then_inc(s["stored"], 16)

            sp.sem_inc(s["stored"], 16 * SLOTS)
            load_y(0)
            load_x(0, 0)
            sp.dma_start(ws[:], w.rearrange("(k p) n -> p k n", p=P)).then_inc(s["w"], 16)
            for dst, a in ((g_b, ln_g), (b_b, ln_b)):
                sp.dma_start(dst[:], a.rearrange("(o n) -> o n", o=1).broadcast_to([P, D])).then_inc(s["w"], 16)
            load_y(1)
            load_x(1, 1)

            def ahead(t, b, last=False):
                load_y(t + SLOTS, last)
                store(t, b)
                load_x(t + SLOTS, b, last)

            with sp.Fori(0, PAIRS - 1) as i:
                for b in range(SLOTS):
                    ahead(2 * i + b, b)
            ahead(NPT - 2, 0, last=True)
            store(NPT - 1, 1)
            store(NPT, 0, last=True)
            sp.wait_ge(s["stored"], 16 * (NTILE + 2))

        @block.tensor
        def _(pe):
            mm, tr = nc.tensor.matmul, nc.tensor.transpose
            pe.sem_inc(s["x_T"], SLOTS)
            pe.sem_inc(s["y_T"], 1)
            pe.sem_inc(s["products"], 1)
            pe.wait_ge(s["w"], 16 * WS)

            def products(t, b, u, last=False):
                n = rows(last)
                pe.wait_ge(s["y_loaded"], 16 * (t + 1))
                for k in range(KW):
                    m = tr(bank[k // 4][:, (k % 4) * P:(k % 4) * P + n], yin[0:n, k * P:(k + 1) * P], ident[0:n, 0:n])
                m.then_inc(s["y_T"], 1)
                pe.wait_ge(s["yT0"], t + 1)
                pe.wait_ge(s["yT1"], t + 1)
                pe.wait_ge(s["res"], t + 1)
                for j in range(2):
                    for k in range(KW):
                        m = mm(bank[2 + 2 * b + j][0:n, :], yT[:, k, 0:n], ws[:, k, j * HALF:(j + 1) * HALF],
                               start=(k == 0), stop=(k == KW - 1))
                m.then_inc(s["products"], 1)

            def transposes(t, b, last=False):
                if xT is None:
                    return
                n = rows(last)
                pe.wait_ge(s["normed"], t + 1)
                pe.wait_ge(s["x_split"], 2 * t + 2)
                for k in range(KD):
                    m = tr(bank[6 + k // 4][:, (k % 4) * P:(k % 4) * P + n], res[0:n, b, k * P:(k + 1) * P], ident[0:n, 0:n])
                m.then_inc(s["x_T"], 1)

            products(0, 0, 0)
            with pe.Fori(0, PAIRS - 1) as i:
                products(2 * i + 1, 1, i)
                transposes(2 * i, 0)
                products(2 * i + 2, 0, i + 1)
                transposes(2 * i + 1, 1)
            products(NPT - 1, 1, PAIRS - 1)
            transposes(NPT - 2, 0)
            products(NPT, 0, PAIRS, last=True)
            transposes(NPT - 1, 1)
            transposes(NPT, 0, last=True)

        def copy_yT(eng, copy, t, j, n):
            eng.wait_ge(s["y_T"], t + 2)
            eng.wait_ge(s["products"], t + 1)
            k0 = 4 * j
            copy(yT[:, k0:k0 + 4, 0:n], bank[j][:].rearrange("p (k t) -> p k t", t=P)[:, :, 0:n])\
                .then_inc(s[f"yT{j}"], 1)

        def halves(t, n):
            at = lambda x, j: x[:, 4 * j:4 * j + 4, bass.ds(t * P, n)]
            src = lambda j: bank[6 + j][:].rearrange("p (k t) -> p k t", t=P)[:, :, 0:n]
            return [(src(j), at(xT[0], j), at(xT[1], j)) for j in range(2)]

        def in_turn(eng, tile, behind):
            tile(0, 0, 0)
            with eng.Fori(0, PAIRS - 1) as i:
                tile(2 * i + 1, 1, i)
                behind(2 * i, 0)
                tile(2 * i + 2, 0, i + 1)
                behind(2 * i + 1, 1)
            tile(NPT - 1, 1, PAIRS - 1)
            behind(NPT - 2, 0)
            tile(NPT, 0, PAIRS, last=True)
            behind(NPT - 1, 1)
            behind(NPT, 0, last=True)

        @block.vector
        def _(dve):
            v = nc.vector
            ch = Chain(dve, s["dve"], 4)
            dve.sem_inc(s["res"], SLOTS)
            dve.sem_inc(s["x_split"], 2)

            def tile(t, b, u, last=False):
                n = rows(last)
                ch.start(t)
                copy_yT(dve, v.tensor_copy, t, 0, n)
                dve.wait_ge(s["products"], t + 2)
                dve.wait_ge(s[f"x_loaded{b}"], 16 * (u + 1))
                r = res[0:n, b, :]
                for j in range(2):
                    m = v.scalar_tensor_tensor(r[:, j * HALF:(j + 1) * HALF], r[:, j * HALF:(j + 1) * HALF], ALPHA,
                                               bank[2 + 2 * b + j][0:n, :], ALU.mult, ALU.add)
                    if j:
                        m.then_inc(s["res"], 1)
                        dve.wait_ge(s["res"], t + 1 + SLOTS)
                    else:
                        ch(m)
                ch(v.bn_stats(stats[0:n, 0, :], r[:, 0:HALF]))
                ch(v.bn_stats(stats[0:n, 1, :], r[:, HALF:]))
                v.memset(spare[:], 0.0)
                ch(v.bn_aggr(mv[0:n], stats[0:n].rearrange("p a b -> p (a b)")))
                v.tensor_scalar(mv[0:n, 1:2], mv[0:n, 1:2], LN_EPS, None, ALU.add).then_inc(s["var"], 1)
                dve.wait_ge(s["rstd"], t + 1)
                v.tensor_scalar(r, r, mv[0:n, 0:1], rstd[0:n], ALU.subtract, ALU.mult).then_inc(s["scaled"], 1)
                dve.wait_ge(s["scaled"], t + 1)
                ch.end()

            def behind(t, b, last=False):
                if xT is not None:
                    for j, (src, high, low) in enumerate(halves(t, rows(last))):
                        dve.wait_ge(s["x_high"], 2 * t + j + 1)
                        v.tensor_tensor(low, src, high.bitcast(FP32), ALU.subtract).then_inc(s["x_split"], 1)
            in_turn(dve, tile, behind)

        @block.scalar
        def _(act):
            def tile(t, b, u, last=False):
                if KW > 4:
                    copy_yT(act, nc.scalar.copy, t, 1, rows(last))
                else:
                    act.wait_ge(s["y_T"], t + 2)
                    act.sem_inc(s["yT1"], 1)

            def behind(t, b, last=False):
                if xT is not None:
                    act.wait_ge(s["x_T"], t + 1 + SLOTS)
                    for src, high, _ in halves(t, rows(last)):
                        nc.scalar.copy(high, src).then_inc(s["x_high"], 1)
            in_turn(act, tile, behind)

        @block.gpsimd
        def _(pool):
            g = nc.gpsimd
            g.memset(half[:], -0.5).then_inc(s["half"], 1)
            pool.wait_ge(s["half"], 1)
            pool.wait_ge(s["w"], 16 * WS)

            def tile(t, b, u, last=False):
                n = rows(last)
                r = res[0:n, b, :]
                pool.wait_ge(s["var"], t + 1)
                g.tensor_tensor(rstd[0:n], mv[0:n, 1:2], half[0:n], ALU.pow).then_inc(s["rstd"], 1)
                pool.wait_ge(s["scaled"], t + 1)
                g.tensor_tensor(r, r, g_b[0:n], ALU.mult).then_inc(s["pool"], 1)
                pool.wait_ge(s["pool"], t + 1)
                g.tensor_tensor(r, r, b_b[0:n], ALU.add).then_inc(s["normed"], 1)
            in_turn(pool, tile, lambda *a, **k: None)


C_QKV = 3 * NG * AW
DIL = (1, 4, 16)
SCALE = HD ** -0.5
NEG = -1e30
ST_W = AW + 2 * H


def window_constants():
    import numpy as np
    q, k = np.arange(P)[:, None], np.arange(2 * P)[None, :]
    dist = q + P - k
    return np.where((dist >= 0) & (dist <= P), 0.0, NEG).astype(np.float32)


def window_attention(nc, ident, p1, mask_in, stats_out, sw, beside):
    VS = 4
    HEADS = ((0, 2), (1, 3), (4, 6), (5, 7))

    with ExitStack() as ctx:
        def sb(name, shape):
            return ctx.enter_context(nc.sbuf_tensor(f"wa_{name}", shape, FP32))

        mask = sb("mask", [P, 2 * P])
        q_in, k_in = sb("q", [P, SLOTS, AW]), sb("k", [P, SLOTS, AW])
        v_in = sb("v", [P, VS, AW])
        qT, kT = sb("qT", [P, HP, P]), sb("kT", [P, SLOTS, HP, P])
        sm = sb("sm", [P, 2, H, 2 * P])
        ex = sb("ex", [P, 2, H, 2 * P])
        mx, spare = sb("mx", [P, H]), sb("spare", [P, len(HEADS)])
        eT = sb("eT", [P, 2, 2, 2 * P])
        out = sb("out", [P, SLOTS, ST_W])
        b_qk = ctx.enter_context(nc.psum_tensor("wa_qk", [P, 512], FP32))
        b_o = ctx.enter_context(nc.psum_tensor("wa_o", [P, 512], FP32))
        b_s = [ctx.enter_context(nc.psum_tensor(f"wa_s{i}", [P, 512], FP32)) for i in range(4)]
        b_e = [ctx.enter_context(nc.psum_tensor(f"wa_e{i}", [P, 512], FP32)) for i in range(2)]
        s = Sems(nc, ctx, "wa", "mask q_T k_T qT kT scores sm negmax ex e_T0 e_T1 eT0 eT1 values out "
                                "dve act loadqk0 loadqk1 loadv0 loadv1 loadv2 loadv3",
                 {f"stored{b}": sw[f"out_stored{b}"] for b in range(SLOTS)})
        block = ctx.enter_context(nc.Block())

        def walk(eng, step, last):
            def four(n0, u, rows, has, before):
                for j in range(4):
                    step(n0 + j, j, u, has[j], before if j == 0 else has[j - 1], *rows(j))
            G0, G1, G2 = NPT // 4, 4, 4
            yes, no = True, False
            four(0, 0, lambda j: (j * P, 1), (no, yes, yes, yes), None)
            with eng.Fori(1, G0) as i:
                four(4 * i, i, lambda j: (i * 4 * P + j * P, 1), (yes,) * 4, yes)
            with eng.Fori(0, G1) as i:
                four(4 * i + NPT, i + G0, lambda j: (i + j * 4 * P, 4), (no, yes, yes, yes), yes)
            four(2 * NPT, G0 + G1, lambda j: (j, 16), (no,) * 4, yes)
            with eng.Fori(1, G2) as i:
                four(4 * i + 2 * NPT, i + G0 + G1, lambda j: (4 * i + j, 16), (no,) * 4, no)
            last(3 * NPT)

        @block.sync
        def _(sp):
            sp.dma_start(mask[:], mask_in).then_inc(s["mask"], 16)

            def rows(tensor, j, row, d, c0, c1):
                if d == 4:
                    part = tensor[j * 4 * P:(j + 1) * 4 * P, c0:c1].rearrange("(i d) n -> d i n", d=d)
                    return part[bass.ds(row - j * 4 * P, 1)].rearrange("o i n -> (o i) n")
                if d == 16:
                    return tensor[:, c0:c1].rearrange("(i d) n -> d i n", d=d)[bass.ds(row, 1)].rearrange("o i n -> (o i) n")
                return tensor[bass.ds(row, P), c0:c1]

            def load(n, j, u, has, before, row, d):
                g = DIL.index(d)
                b = j % 2
                if before is not None:
                    if not isinstance(n, int) or n >= 2:
                        sp.wait_ge(s["k_T"], n - 1)
                for a, c in ((q_in, 0), (k_in, NG * AW)):
                    sp.dma_start(a[:, b, :], rows(p1, j, row, d, c + g * AW, c + (g + 1) * AW)).then_inc(s[f"loadqk{b}"], 16)
                if not isinstance(n, int) or n >= VS:
                    sp.wait_ge(s["values"], n - VS + 2)
                sp.dma_start(v_in[:, j, :], rows(p1, j, row, d, 2 * NG * AW + g * AW, 2 * NG * AW + (g + 1) * AW))\
                    .then_inc(s[f"loadv{j}"], 16)
            walk(sp, load, lambda n: None)

        @block.tensor
        def _(pe):
            mm, tr = nc.tensor.matmul, nc.tensor.transpose
            pe.wait_ge(s["mask"], 16)

            def scores(n, j, u, has, before, row, d):
                b = j % 2
                pe.wait_ge(s[f"loadqk{b}"], 32 * (2 * u + j // 2 + 1))
                if before is not None:
                    pe.wait_ge(s["kT"], n)
                for p in range(HP):
                    m = tr(b_qk[:, p * P:(p + 1) * P], q_in[:, b, p * P:(p + 1) * P], ident[:])
                m.then_inc(s["q_T"], 1)
                pe.wait_ge(s["qT"], n + 1)
                for p in range(HP):
                    m = tr(b_qk[:, p * P:(p + 1) * P], k_in[:, b, p * P:(p + 1) * P], ident[:])
                m.then_inc(s["k_T"], 1)
                pe.wait_ge(s["kT"], n + 1)
                for i, hs in enumerate(HEADS):
                    if before is not None:
                        pe.wait_ge(s["sm"], H * (n - 1) + 2 * i + 2)
                    for q, h in enumerate(hs):
                        e, p = HD * (h % 2), h // 2
                        o = b_s[i][:, q * 2 * P:(q + 1) * 2 * P]
                        if has:
                            mm(o[:, 0:P], qT[e:e + HD, p, :], kT[e:e + HD, 1 - b, p, :], start=True, stop=True)
                        m = mm(o[:, P:], qT[e:e + HD, p, :], kT[e:e + HD, b, p, :], start=True, stop=True)
                    m.then_inc(s["scores"], 1)

            def values(n, j, has):
                for i, hs in enumerate(HEADS):
                    pe.wait_ge(s["ex"], H * n + 2 * i + 2)
                    if not isinstance(n, int) or n:
                        pe.wait_ge(s[f"eT{i % 2}"], 2 * n + i // 2)
                    elif i // 2:
                        pe.wait_ge(s[f"eT{i % 2}"], 1)
                    for q, h in enumerate(hs):
                        for c in range(0 if has else 1, 2):
                            m = tr(b_e[i % 2][:, (2 * q + c) * P:(2 * q + c + 1) * P], ex[:, j % 2, h, c * P:(c + 1) * P], ident[:])
                    m.then_inc(s[f"e_T{i % 2}"], 1)
                    if i:
                        product(n, j, has, i - 1)
                product(n, j, has, 3)

            def product(n, j, has, i):
                pe.wait_ge(s[f"eT{i % 2}"], 2 * n + i // 2 + 1)
                if i == 0 and not (isinstance(n, int) and n == 0):
                    pe.wait_ge(s["out"], n)
                for q, h in enumerate(HEADS[i]):
                    for c in range(0 if has else 1, 2):
                        vb = j if c else (j - 1) % VS
                        m = mm(b_o[:, h * HD:(h + 1) * HD], eT[:, i % 2, q, c * P:(c + 1) * P], v_in[:, vb, h * HD:(h + 1) * HD],
                               start=(c == 0 or not has), stop=(c == 1))
                if i == 3:
                    m.then_inc(s["values"], 1)

            def step(n, j, u, has, before, row, d):
                scores(n, j, u, has, before, row, d)
                if before is not None:
                    values(n - 1, (j - 1) % 4, before)
                pe.wait_ge(s[f"loadv{j}"], 16 * (u + 1))
            walk(pe, step, lambda n: values(n - 1, 3, False))

        def copy_eT(eng, copy, n, j, has, i):
            eng.wait_ge(s[f"e_T{i % 2}"], 2 * n + i // 2 + 1)
            if i < 2:
                if not (isinstance(n, int) and n == 0):
                    eng.wait_ge(s["values"], n)
            src = b_e[i % 2][:].rearrange("p (q c t) -> p q c t", q=2, c=2)
            dst = eT[:, i % 2, :, :].rearrange("p q (c t) -> p q c t", c=2)
            lo = 0 if has else 1
            copy(dst[:, :, lo:, :], src[:, :, lo:, :]).then_inc(s[f"eT{i % 2}"], 1)

        @block.vector
        def _(dve):
            v = nc.vector
            dve.wait_ge(s["mask"], 16)

            def scores(n, j, u, has, before, row, d):
                dve.wait_ge(s["q_T"], n + 1)
                if before is not None:
                    dve.wait_ge(s["scores"], 4 * n)
                v.tensor_copy(qT[:].rearrange("p a b -> p (a b)"), b_qk[:]).then_inc(s["qT"], 1)
                dve.wait_ge(s["k_T"], n + 1)
                v.tensor_copy(kT[:, j % 2, :, :].rearrange("p a b -> p (a b)"), b_qk[:]).then_inc(s["kT"], 1)
                lo = 0 if has else P
                for i, hs in enumerate(HEADS):
                    dve.wait_ge(s["scores"], 4 * n + i + 1)
                    v.memset(spare[:, i:i + 1], 0.0)
                    for q, h in enumerate(hs):
                        v.tensor_tensor_reduce(out=sm[:, j % 2, h, lo:], in0=b_s[i][:, q * 2 * P + lo:(q + 1) * 2 * P],
                                               in1=mask[:, lo:], scale=SCALE, scalar=NEG, op0=ALU.add, op1=ALU.max,
                                               accum_out=mx[:, h:h + 1]).then_inc(s["sm"], 1)
                dve.wait_ge(s["sm"], H * (n + 1))
                if not isinstance(n, int) or n >= 2:
                    dve.wait_ge(s[f"stored{j % 2}"], 16 * (2 * u + j // 2))
                v.tensor_scalar(out[:, j % 2, AW:AW + H], mx[:], -1.0, None, ALU.mult).then_inc(s["negmax"], 1)

            def copies(n, j, has):
                for i in (0, 2):
                    copy_eT(dve, v.tensor_copy, n, j, has, i)

            def step(n, j, u, has, before, row, d):
                scores(n, j, u, has, before, row, d)
                if before is not None:
                    copies(n - 1, (j - 1) % 4, before)
            walk(dve, step, lambda n: copies(n - 1, 3, False))

        @block.scalar
        def _(act):
            a = nc.scalar
            beside(act)

            def scores(n, j, u, has, before, row, d):
                lo = 0 if has else P
                act.wait_ge(s["negmax"], n + 1)
                for i, hs in enumerate(HEADS):
                    for q, h in enumerate(hs):
                        a.activation(ex[:, j % 2, h, lo:], sm[:, j % 2, h, lo:], ACT.Exp, bias=out[:, j % 2, AW + h:AW + h + 1],
                                     scale=1.0, accum_out=out[:, j % 2, AW + H + h:AW + H + h + 1]).then_inc(s["ex"], 1)

            def copies(n, j, has):
                for i in (1, 3):
                    copy_eT(act, a.copy, n, j, has, i)
                act.wait_ge(s["values"], n + 1)
                a.copy(out[:, j % 2, 0:AW], b_o[:]).then_inc(s["out"], 1)

            def step(n, j, u, has, before, row, d):
                scores(n, j, u, has, before, row, d)
                if before is not None:
                    copies(n - 1, (j - 1) % 4, before)
            walk(act, step, lambda n: copies(n - 1, 3, False))

        @block.gpsimd
        def _(pool):
            def store(n, j, u, has, before, row, d):
                g = DIL.index(d)
                pool.wait_ge(s["out"], n + 1)
                if d == 1:
                    dst = stats_out[bass.ds(row, P), g, :]
                elif d == 4:
                    dst = stats_out[j * 4 * P:(j + 1) * 4 * P, g, :].rearrange("(i d) n -> d i n", d=d)
                    dst = dst[bass.ds(row - j * 4 * P, 1)].rearrange("o i n -> (o i) n")
                else:
                    dst = stats_out[:, g, :].rearrange("(i d) n -> d i n", d=d)[bass.ds(row, 1)].rearrange("o i n -> (o i) n")
                pool.dma_start(dst, out[:, j % 2, :]).then_inc(s[f"stored{j % 2}"], 16)
            walk(pool, store, lambda n: None)
            for b in range(2):
                pool.wait_ge(s[f"stored{b}"], 16 * 3 * NPT // 2)


def merge_windows(nc, stats, p1, p1_sample, o_sample, y_prompt, y_sample):
    Z0 = C_QKV
    with ExitStack() as ctx:
        def sb(name, shape):
            return ctx.enter_context(nc.sbuf_tensor(f"mw_{name}", shape, FP32))

        st = sb("st", [P, SLOTS, NG, ST_W])
        z, tz, zh, gate = sb("z", [P, SLOTS, AW]), sb("tz", [P, AW]), sb("zh", [P, AW]), sb("gate", [P, AW])
        low = sb("low", [P, H])
        w, wd = sb("w", [P, NG, H]), sb("wd", [P, NG, H])
        den = sb("den", [P, H])
        part, o = sb("part", [P, AW]), sb("o", [P, SLOTS, AW])
        s = Sems(nc, ctx, "mw", "loaded0 loaded1 tanh gate diff weights merged gated stored read dve pool")
        block = ctx.enter_context(nc.Block())

        @block.sync
        def _(sp):
            def load(t, b, last=False):
                if last:
                    sp.dma_start(o[0:NS, b, :], o_sample).then_inc(s[f"loaded{b}"], 16)
                    sp.dma_start(z[0:NS, b, :], p1_sample[:, :, Z0:].rearrange("b t n -> (b t) n")).then_inc(s[f"loaded{b}"], 16)
                else:
                    sp.dma_start(st[:, b, :, :], stats[bass.ds(t * P, P), :, :]).then_inc(s[f"loaded{b}"], 16)
                    sp.dma_start(z[:, b, :], p1[bass.ds(t * P, P), Z0:]).then_inc(s[f"loaded{b}"], 16)

            def store(t, b, last=False):
                sp.wait_ge(s["gated"], t + 1)
                if last:
                    sp.dma_start(y_sample, o[0:NS, b, :]).then_inc(s["stored"], 16)
                else:
                    sp.dma_start(y_prompt[bass.ds(t * P, P), :], o[:, b, :]).then_inc(s["stored"], 16)

            sp.sem_inc(s["stored"], 32)
            for b in range(SLOTS):
                load(b, b)
            with sp.Fori(0, PAIRS - 1) as i:
                for b in range(SLOTS):
                    store(2 * i + b, b)
                    load(2 * i + b + SLOTS, b)
            store(NPT - 2, 0)
            sp.wait_ge(s["stored"], 16 * (NPT - 1 + 2))
            load(NPT, 0, last=True)
            store(NPT - 1, 1)
            store(NPT, 0, last=True)
            sp.wait_ge(s["stored"], 16 * (NTILE + 2))

        @block.scalar
        def _(act):
            def gate_in(t, b, u):
                n = NS if u is PAIRS else P
                act.wait_ge(s[f"loaded{b}"], 32 * (u + 1))
                act.wait_ge(s["gate"], t + 1)
                nc.scalar.mul(zh[0:n], z[0:n, b, :], 0.5)
                nc.scalar.activation(tz[0:n], z[0:n, b, :], ACT.Tanh, scale=0.5).then_inc(s["tanh"], 1)

            def tile(t, b, u):
                gate_in(t, b, u)
                act.wait_ge(s["diff"], t + 1)
                nc.scalar.activation(w[:], w[:], ACT.Exp, scale=-1.0).then_inc(s["weights"], 1)
            each_tile(act, tile, tail=False)
            gate_in(NPT, 0, PAIRS)

        @block.vector
        def _(dve):
            v = nc.vector
            ch = Chain(dve, s["dve"], 10)

            def tile(t, b, u):
                ch.start(t)
                x = st[:, b, :, :]
                nm, dn = x[:, :, AW:AW + H], x[:, :, AW + H:]
                dve.wait_ge(s[f"loaded{b}"], 32 * (u + 1))
                ch(v.tensor_tensor(low[:], nm[:, 0, :], nm[:, 1, :], ALU.min))
                ch(v.tensor_tensor(low[:], low[:], nm[:, 2, :], ALU.min))
                v.tensor_tensor(w[:], nm, each(low[:], NG), ALU.subtract).then_inc(s["diff"], 1)
                dve.wait_ge(s["weights"], t + 1)
                ch(v.tensor_tensor(wd[:], w[:], dn, ALU.mult))
                ch(v.tensor_tensor(den[:], wd[:, 0, :], wd[:, 1, :], ALU.add))
                ch(v.tensor_tensor(den[:], den[:], wd[:, 2, :], ALU.add))
                ch(v.reciprocal(den[:], den[:]))
                ch(v.tensor_tensor(w[:], w[:], each(den[:], NG), ALU.mult))
                dve.wait_ge(s["stored"], 16 * (t + 1))
                for g in range(NG):
                    dst = part if g else o[:, b, :]
                    m = v.tensor_tensor(heads(dst if not g else part[:]), heads(x[:, g, 0:AW]), over(w[:, g, :], HD), ALU.mult)
                    if g < 2:
                        ch(m)
                    else:
                        m.then_inc(s["read"], 1)
                        dve.wait_ge(s["read"], t + 1)
                    if g == 1:
                        ch(v.tensor_tensor(o[:, b, :], o[:, b, :], part[:], ALU.add))
                v.tensor_tensor(o[:, b, :], o[:, b, :], part[:], ALU.add).then_inc(s["merged"], 1)
                dve.wait_ge(s["merged"], t + 1)
                ch.end()
            each_tile(dve, tile, tail=False)

        @block.gpsimd
        def _(pool):
            g = nc.gpsimd
            ch = Chain(pool, s["pool"], 1)
            pool.sem_inc(s["gate"], 1)

            def tile(t, b, u):
                n = NS if u is PAIRS else P
                ch.start(t)
                pool.wait_ge(s[f"loaded{b}"], 32 * (u + 1))
                pool.wait_ge(s["tanh"], t + 1)
                ch(g.tensor_tensor(tz[0:n], tz[0:n], zh[0:n], ALU.mult))
                g.tensor_tensor(gate[0:n], tz[0:n], zh[0:n], ALU.add).then_inc(s["gate"], 1)
                pool.wait_ge(s["gate"], t + 2)
                if u is not PAIRS:
                    pool.wait_ge(s["merged"], t + 1)
                ch.end()
                g.tensor_tensor(o[0:n, b, :], o[0:n, b, :], gate[0:n], ALU.mult).then_inc(s["gated"], 1)
            each_tile(pool, tile)


def sample_constants():
    import numpy as np
    t = np.tile(np.arange(DT), H)[:, None]
    m = np.arange(P)[None, :]
    add = lambda ok: np.where(ok, 0.0, NEG).astype(np.float32)
    old = [add((t % 4 == r) & (r + 4 * m >= t)) for r in range(4)]
    old += [add((t == r) & (m >= 0)) for r in range(8)]
    new = np.zeros((DB, H * DT, P + NG * NS), np.float32)
    col = np.arange(NS)[None, :]
    for b in range(DB):
        parts = [add(m >= t)]
        for d in DIL:
            parts.append(add((col // DT == b) & (col % DT <= t) & ((t - col % DT) % d == 0)))
        new[b] = np.concatenate(parts, axis=1)
    return np.concatenate(old, axis=1), new


def sample_attention(nc, ident, p1s, caches, old_mask, new_mask, o_out):
    R = H * DT
    NQ = 3
    QW = 4 * P
    NEW_W = P + NG * NS
    COLS = NQ * QW + NEW_W
    N_OLD = 13
    with ExitStack() as ctx:
        def sb(name, shape):
            return ctx.enter_context(nc.sbuf_tensor(f"sa_{name}", shape, FP32))

        K, V = sb("K", [P, SLOTS, N_OLD, AW]), sb("V", [P, N_OLD, AW])
        Vn = sb("Vn", [P, NG, AW])
        kqn = sb("kqn", [NS, NG, AW])
        Qall = sb("Qall", [P, DB, NG * HP * R])
        Q = sb("Q", [P, NG, HP, R])
        KnT = sb("KnT", [P, NG, HP, NS])
        KT = sb("KT", [P, HP, QW])
        om = sb("om", [R, NQ * QW])
        nm = sb("nm", [R, SLOTS, NEW_W])
        sm, ex = sb("sm", [R, COLS]), sb("ex", [R, COLS])
        mx, neg, den, rden = sb("mx", [R, 4]), sb("neg", [R, 1]), sb("den", [R, 1]), sb("rden", [R, 1])
        spare = sb("spare", [R, 1])
        ET = sb("ET", [P, 16, R])
        yT = sb("yT", [P, HP, NS])
        y = sb("y", [NS, AW])
        bank = [ctx.enter_context(nc.psum_tensor(f"sa_b{i}", [P, 512], FP32)) for i in range(8)]
        s = Sems(nc, ctx, "sa", "in zero q_T q_done kn_T kn_done ready K0 K1 V nm0 nm1 K_T kt0 kt1 q_copied scores sm "
                                "max ex rden scaled e_T e0 e1 out out0 y_T y stored dve act values k_read")
        block = ctx.enter_context(nc.Block())
        c0, c1, c2 = caches

        @block.sync
        def _(sp):
            for g in range(NG):
                sp.dma_start(kqn[:, g, :], p1s[:, :, g * AW:(g + 1) * AW].rearrange("b t n -> (b t) n")).then_inc(s["in"], 16)
            sp.dma_start(om[:], old_mask).then_inc(s["in"], 16)
            sp.wait_ge(s["zero"], 3)
            for g in range(NG):
                c = (2 * NG + g) * AW
                sp.dma_start(Vn[0:NS, g, :], p1s[:, :, c:c + AW].rearrange("b t n -> (b t) n")).then_inc(s["in"], 16)

            def rows(b, which):
                flat = lambda c: c[bass.ds(b, 1), :, which, :, :]
                x1 = flat(c1).rearrange("o (m r) h d -> m (o r) (h d)", r=4)
                x2 = flat(c2).rearrange("o (m r) h d -> m (o r) (h d)", r=16)[:, 0:8, :]
                x0 = flat(c0).rearrange("o m h d -> m o (h d)")
                return x1, x2, x0

            def load(b, slot, u):
                for (lo, hi), src in zip(((0, 4), (4, 12), (12, 13)), rows(b, 0)):
                    sp.dma_start(K[:, slot, lo:hi, :], src).then_inc(s[f"K{slot}"], 16)
                sp.dma_start(nm[:, slot, :], new_mask[bass.ds(b, 1), :, :].rearrange("o r n -> (o r) n")).then_inc(s[f"nm{slot}"], 16)

            def load_v(b):
                for (lo, hi), src in zip(((0, 4), (4, 12), (12, 13)), rows(b, 1)):
                    sp.dma_start(V[:, lo:hi, :], src).then_inc(s["V"], 16)

            sp.wait_ge(s["q_done"], 2 * NG)
            for g in range(NG):
                c = (NG + g) * AW
                sp.dma_start(kqn[:, g, :], p1s[:, :, c:c + AW].rearrange("b t n -> (b t) n")).then_inc(s["in"], 16)
            load(0, 0, 0)
            load(1, 1, 0)
            load_v(0)
            with sp.Fori(0, DB // 2 - 1) as i:
                for slot in range(2):
                    sp.wait_ge(s["zero"], 3)
                    sp.wait_ge(s["sm"], 4 * (2 * i + slot + 1))
                    load(2 * i + slot + 2, slot, i + 1)
                    sp.wait_ge(s["values"], 2 * i + slot + 1)
                    load_v(2 * i + slot + 1)
            sp.wait_ge(s["values"], DB - 1)
            load_v(DB - 1)
            sp.wait_ge(s["y"], 1)
            sp.dma_start(o_out, y[:]).then_inc(s["stored"], 16)
            sp.wait_ge(s["stored"], 16)

        @block.gpsimd
        def _(pool):
            nc.gpsimd.memset(Qall[:].rearrange("p a b -> p (a b)"), 0.0).then_inc(s["zero"], 1)
            nc.gpsimd.memset(Vn[:].rearrange("p a b -> p (a b)"), 0.0).then_inc(s["zero"], 1)
            nc.gpsimd.memset(ET[:].rearrange("p a b -> p (a b)"), 0.0).then_inc(s["zero"], 1)
            pool.wait_ge(s["zero"], 3)

            def own(b, slot, u):
                pool.wait_ge(s["scores"], 4 * b + 1)
                nc.gpsimd.tensor_copy(Q[:].rearrange("p g h r -> p (g h r)"),
                                      Qall[:, bass.ds(b, 1), :].rearrange("p o n -> p (o n)")).then_inc(s["q_copied"], 1)
            pool.wait_ge(s["q_done"], 2 * NG)
            with pool.Fori(0, DB // 2) as i:
                for slot in range(2):
                    own(2 * i + slot, slot, i)

        @block.tensor
        def _(pe):
            mm, tr = nc.tensor.matmul, nc.tensor.transpose
            pe.wait_ge(s["in"], 16 * (2 * NG + 1))
            for g in range(NG):
                for p in range(HP):
                    m = tr(bank[g][:, p * NS:(p + 1) * NS], kqn[:, g, p * P:(p + 1) * P], ident[0:NS, 0:NS])
                m.then_inc(s["q_T"], 1)
            pe.wait_ge(s["in"], 16 * (3 * NG + 1))
            for g in range(NG):
                for p in range(HP):
                    m = tr(bank[4 + g][:, p * NS:(p + 1) * NS], kqn[:, g, p * P:(p + 1) * P], ident[0:NS, 0:NS])
                m.then_inc(s["kn_T"], 1)
            pe.wait_ge(s["q_done"], 2 * NG)
            pe.wait_ge(s["kn_done"], NG)
            pe.sem_inc(s["scores"], 1)

            def sequence(b, slot, u):
                pe.wait_ge(s[f"K{slot}"], 48 * (u + 1))
                pe.wait_ge(s["q_copied"], b + 1)

                def score(q):
                    g = 1 if q == 0 else 2 if q < NQ else 0
                    pe.wait_ge(s["kt0"], 4 * b + q + 2)
                    pe.wait_ge(s["kt1"], 4 * b + q + 2)
                    width = QW if q < NQ else P
                    o = bank[4 + q % 2]
                    if q >= 2:
                        pe.wait_ge(s["sm"], 4 * b + q - 1)
                    for p in range(HP):
                        m = mm(o[0:R, 0:width], Q[:, g, p, :], KT[:, p, 0:width], start=(p == 0), stop=(p == HP - 1))
                    if q == NQ:
                        for g in range(NG):
                            for p in range(HP):
                                m = mm(o[0:R, P + g * NS:P + (g + 1) * NS], Q[:, g, p, :], KnT[:, g, p, :],
                                       start=(p == 0), stop=(p == HP - 1))
                    m.then_inc(s["scores"], 1)

                for q in range(NQ + 1):
                    n = 4 if q < NQ else 1
                    pe.wait_ge(s["kt0"], 4 * b + q + 1)
                    pe.wait_ge(s["kt1"], 4 * b + q + 1)
                    for p in range(HP):
                        for j in range(n):
                            m = tr(bank[p][:, j * P:(j + 1) * P], K[:, slot, 4 * q + j, p * P:(p + 1) * P], ident[:])
                    m.then_inc(s["K_T"] if q < NQ else s["k_read"], 1)
                    score(q)
                pe.wait_ge(s["zero"], 3)
                pe.wait_ge(s["scaled"], b + 1)
                for j in range(16):
                    o = bank[6 + j // 8][:, (j % 8) * R:(j % 8 + 1) * R]
                    if j < N_OLD:
                        m = tr(o, ex[:, j * P:(j + 1) * P], ident[0:R, 0:R])
                    else:
                        c = N_OLD * P + (j - N_OLD) * NS
                        m = tr(o[0:NS, :], ex[:, c:c + NS], ident[0:R, 0:R])
                    if j % 8 == 7:
                        m.then_inc(s["e_T"], 1)
                pe.wait_ge(s["V"], 48 * (b + 1))
                pe.wait_ge(s["e0"], b + 1)
                pe.wait_ge(s["e1"], b + 1)
                for p in range(HP):
                    for j in range(16):
                        w = V[:, j, p * P:(p + 1) * P] if j < N_OLD else Vn[:, j - N_OLD, p * P:(p + 1) * P]
                        m = mm(bank[4][:, p * 2 * DT:(p + 1) * 2 * DT], w, ET[:, j, 2 * p * DT:2 * (p + 1) * DT],
                               start=(j == 0), stop=(j == 15))
                m.then_inc(s["values"], 1)
                pe.wait_ge(s["out"], 2 * b + 2)
            with pe.Fori(0, DB // 2) as i:
                for slot in range(2):
                    sequence(2 * i + slot, slot, i)
            for p in range(HP):
                m = tr(bank[0][0:NS, p * P:(p + 1) * P], yT[:, p, :], ident[:])
            m.then_inc(s["y_T"], 1)

        def copy_kt(eng, copy, b, j):
            for q in range(NQ + 1):
                width = QW if q < NQ else P
                if q < NQ:
                    eng.wait_ge(s["K_T"], NQ * b + q + 1)
                else:
                    eng.wait_ge(s["k_read"], b + 1)
                eng.wait_ge(s["scores"], 4 * b + q + 1)
                for p in (2 * j, 2 * j + 1):
                    m = copy(KT[:, p, 0:width], bank[p][:, 0:width])
                m.then_inc(s[f"kt{j}"], 1)
                yield q

        @block.vector
        def _(dve):
            v = nc.vector
            ch = Chain(dve, s["dve"], 1)
            dve.wait_ge(s["zero"], 3)
            dve.wait_ge(s["in"], 16 * (2 * NG + 1))
            for g in range(NG):
                dve.wait_ge(s["q_T"], g + 1)
                for e in range(2):
                    for p in range(HP):
                        h = 2 * p + e
                        dst = Qall[HD * e:HD * e + HD].rearrange("p b (g h r) -> p g h b r", g=NG, h=HP)[:, g, p, :, h * DT:(h + 1) * DT]
                        m = v.tensor_copy(dst, bank[g][HD * e:HD * e + HD, p * NS:(p + 1) * NS].rearrange("p (b t) -> p b t", t=DT))
                    m.then_inc(s["q_done"], 1)
            dve.sem_inc(s["kt0"], 1)

            def sequence(b, slot, u):
                ch.start(b)
                copies = copy_kt(dve, v.tensor_copy, b, 0)
                for q in range(NQ + 1):
                    next(copies)
                    dve.wait_ge(s["scores"], 4 * b + q + 2)
                    if q == 0:
                        dve.wait_ge(s[f"nm{slot}"], 16 * (u + 1))
                    v.memset(spare[:], 0.0)
                    width = QW if q < NQ else NEW_W
                    mask = om[:, q * QW:q * QW + QW] if q < NQ else nm[:, slot, :]
                    v.tensor_tensor_reduce(out=sm[:, q * QW:q * QW + width], in0=bank[4 + q % 2][0:R, 0:width], in1=mask,
                                           scale=SCALE, scalar=NEG, op0=ALU.add, op1=ALU.max,
                                           accum_out=mx[:, q:q + 1]).then_inc(s["sm"], 1)
                for _ in copies:
                    pass
                dve.wait_ge(s["sm"], 4 * b + 4)
                v.tensor_reduce(neg[:], mx[:], AX.X, ALU.max, negate=True).then_inc(s["max"], 1)
                dve.wait_ge(s["ex"], b + 1)
                v.reciprocal(rden[:], den[:]).then_inc(s["rden"], 1)
                dve.wait_ge(s["rden"], b + 1)
                v.tensor_scalar(ex[:], ex[:], rden[:], None, ALU.mult).then_inc(s["scaled"], 1)
                dve.wait_ge(s["e_T"], 2 * b + 1)
                v.tensor_copy(ET[:, 0:8, :].rearrange("p a b -> p (a b)"), bank[6][:]).then_inc(s["e0"], 1)
                dve.wait_ge(s["values"], b + 1)
                for e in range(2):
                    src = bank[4][HD * e:HD * e + HD, 0:HP * 2 * DT].rearrange("p (h e t) -> p h e t", h=HP, e=2)[:, :, e, :]
                    v.tensor_copy(yT[HD * e:HD * e + HD, :, bass.ds(b * DT, DT)], src).then_inc(s["out"], 1)
            with dve.Fori(0, DB // 2) as i:
                for slot in range(2):
                    sequence(2 * i + slot, slot, i)
            dve.wait_ge(s["y_T"], 1)
            v.tensor_copy(y[:], bank[0][0:NS, :]).then_inc(s["y"], 1)

        @block.scalar
        def _(act):
            a = nc.scalar
            for g in range(NG):
                act.wait_ge(s["kn_T"], g + 1)
                a.copy(KnT[:, g, :, :].rearrange("p h r -> p (h r)"), bank[4 + g][:, 0:HP * NS]).then_inc(s["kn_done"], 1)
            act.sem_inc(s["kt1"], 1)
            act.wait_ge(s["zero"], 3)

            def sequence(b, slot, u):
                for _ in copy_kt(act, a.copy, b, 1):
                    pass
                act.wait_ge(s["max"], b + 1)
                a.activation(ex[:], sm[:], ACT.Exp, bias=neg[:], scale=1.0, accum_out=den[:]).then_inc(s["ex"], 1)
                act.wait_ge(s["e_T"], 2 * b + 2)
                a.copy(ET[:, 8:13, :].rearrange("p a b -> p (a b)"), bank[7][:, 0:5 * R])
                a.copy(ET[0:NS, 13:16, :].rearrange("p a b -> p (a b)"), bank[7][0:NS, 5 * R:]).then_inc(s["e1"], 1)
            with act.Fori(0, DB // 2) as i:
                for slot in range(2):
                    sequence(2 * i + slot, slot, i)


ARGS = ("x_prompt x_sample state_rwkv state_shift state_conv cache_kv_w128 cache_kv_w512 cache_kv_w2048 "
        "even_w_in even_w_out rwkv_mu rwkv_w0 rwkv_w2 rwkv_a0 rwkv_a2 rwkv_k_k rwkv_k_a rwkv_r_k rwkv_gn_g "
        "rwkv_gn_b conv_w odd_w_in odd_w_out ln_g ln_b").split()
WINDOWS = (128, 512, 2048)
OUTS = {
    "y_prompt": (1, SEQ, D), "y_sample": (DB, DT, D),
    "rwkv_prompt": (1, 1, H, HD, HD), "rwkv_sample": (1, DB, H, HD, HD),
    "shift_prompt": (1, 1, SHIFT_W), "shift_sample": (1, DB, SHIFT_W),
    "conv_prompt": (1, 1, 2, AW), "conv_sample": (1, DB, 2, AW),
}
for _w in WINDOWS:
    OUTS[f"kv{_w}_prompt"] = (1, 1, _w, 2, H, HD)
    OUTS[f"kv{_w}_sample"] = (1, DB, _w, 2, H, HD)


def decoder_step(nc, a, o, c):
    scratch = lambda name, *shape: nc.dram_tensor(f"s_{name}", shape, FP32, kind="Internal").ap()
    p_pad, ps_pad = scratch("p0", PAD + SEQ, EVEN_W), scratch("p0s", DB, PAD + DT, EVEN_W)
    y0, y0s = scratch("y0", SEQ, EVEN_MIX), scratch("y0s", NS, EVEN_MIX)
    scan_in, scan_y = scratch("scan_in", 6, DB, H, DT, HD), scratch("scan_y", DB, H, DT, HD)
    x1, x1s = scratch("x1", SEQ, D), scratch("x1s", NS, D)
    p1, p1s = scratch("p1", SEQ, ODD_W), scratch("p1s", DB, DT, ODD_W)
    stats, o1s = scratch("stats", SEQ, NG, ST_W), scratch("o1s", NS, AW)
    y1, y1s = scratch("y1", SEQ, AW), scratch("y1s", NS, AW)
    caches = [a[f"cache_kv_w{w}"][0] for w in WINDOWS]
    kv_s = [o[f"kv{w}_sample"][0] for w in WINDOWS]
    kv_p = [o[f"kv{w}_prompt"][0, 0] for w in WINDOWS]
    PIECES = 8

    with ExitStack() as ctx:
        ident = ctx.enter_context(nc.sbuf_tensor("ident", [P, P], FP32))
        sw = {n: ctx.enter_context(nc.semaphore(n)) for n in
              "padded ei_w_loaded0 ei_w_loaded1 oi_w_loaded0 oi_w_loaded1 conv_out conv_s_out out_stored0 out_stored1".split()}
        kv_stored = ctx.enter_context(nc.semaphore("kv_stored"))

        def shift_caches(eng, piece):
            for w, cache, out in zip(WINDOWS, caches, kv_s):
                rows = (w - DT) // PIECES
                lo = piece * rows
                eng.dma_start(out[:, bass.ds(lo, rows)].rearrange("b r k h d -> b r (k h d)"),
                                  cache[:, bass.ds(lo + DT, rows)].rearrange("b r k h d -> b r (k h d)"))\
                       .then_inc(kv_stored, 16)

        def new_keys(eng):
            for g, w in enumerate(WINDOWS):
                for kv in range(2):
                    cols = slice(((1 + kv) * NG + g) * AW, ((1 + kv) * NG + g + 1) * AW)
                    eng.dma_start(kv_p[g][:, kv].rearrange("r h d -> r (h d)"), p1[SEQ - w:, cols]).then_inc(kv_stored, 16)
                    eng.dma_start(kv_s[g][:, w - DT:, kv].rearrange("b r h d -> b r (h d)"), p1s[:, :, cols])\
                       .then_inc(kv_stored, 16)

        KV_STORES = NG * PIECES + 4 * NG
        with nc.sbuf_tensor("x_high", [P, KD, NTOK], FP32R) as x_high, nc.sbuf_tensor("x_low", [P, KD, NTOK], FP32R) as x_low:
            transpose_in(nc, a["x_prompt"], a["x_sample"], x_high, x_low, ident, p_pad, ps_pad, a["state_shift"][0], a["state_conv"][0], sw)
            project_in(nc, "ei", x_high, x_low, a["even_w_in"][0], EVEN_W // 16, 16, p_pad[PAD:], ps_pad[:, PAD:], sw, shift_caches)
        rw = [a[f"rwkv_{n}"][0] for n in "mu w0 w2 a0 a2 k_k k_a r_k gn_g gn_b".split()]
        even_mix(nc, ident, p_pad, ps_pad, c["rwkv"], a["state_rwkv"][0], rw, a["conv_w"][0], y0, y0s, scan_in, scan_y,
                 o["rwkv_prompt"][0, 0], o["rwkv_sample"][0], o["shift_prompt"][0], o["shift_sample"][0],
                 o["conv_prompt"][0, 0], o["conv_sample"][0], sw)
        with nc.sbuf_tensor("x1_high", [P, KD, NTOK], FP32R) as x1_high, nc.sbuf_tensor("x1_low", [P, KD, NTOK], FP32R) as x1_low:
            project_out(nc, "eo", ident, y0, y0s, EVEN_MIX, a["even_w_out"][0], a["x_prompt"][0],
                        a["x_sample"].rearrange("b t d -> (b t) d"), a["ln_g"][0], a["ln_b"][0], x1, x1s, (x1_high, x1_low))
            project_in(nc, "oi", x1_high, x1_low, a["odd_w_in"][0], ODD_W // 16, 16, p1, p1s, sw)
        window_attention(nc, ident, p1, c["window"], stats, sw, new_keys)
        sample_attention(nc, ident, p1s, caches, c["sample_old"], c["sample_new"], o1s)
        merge_windows(nc, stats, p1, p1s, o1s, y1, y1s)
        project_out(nc, "oo", ident, y1, y1s, AW, a["odd_w_out"][0], x1, x1s, a["ln_g"][1], a["ln_b"][1],
                    o["y_prompt"][0], o["y_sample"].rearrange("b t d -> (b t) d"))
        with nc.Block() as block:
            @block.sync
            def _(sp):
                sp.wait_ge(kv_stored, 16 * KV_STORES)


EVEN_MIX = 2 * AW


def kernel(**inputs):
    import numpy as np
    import concourse.bacc as bacc
    from concourse.bass_utils import run_bass_kernel_spmd

    nc = bacc.Bacc("TRN2", target_bir_lowering=False, num_devices=1)
    sample_old, sample_new = sample_constants()
    constants = {"rwkv": rwkv_constants(), "window": window_constants(), "sample_old": sample_old, "sample_new": sample_new}
    arrays = {f"in_{n}": np.ascontiguousarray(inputs[n]) for n in ARGS}
    arrays.update({f"const_{n}": v for n, v in constants.items()})
    aps = {n: nc.dram_tensor(n, v.shape, FP32, kind="ExternalInput").ap() for n, v in arrays.items()}
    outs = {n: nc.dram_tensor(f"out_{n}", shape, FP32, kind="ExternalOutput").ap() for n, shape in OUTS.items()}
    decoder_step(nc, {n: aps[f"in_{n}"] for n in ARGS}, outs, {n: aps[f"const_{n}"] for n in constants})
    r = run_bass_kernel_spmd(nc, [arrays], core_ids=[0]).results[0]
    return tuple(r[f"out_{n}"] for n in OUTS)
```

```python
import concourse.bass as bass
from concourse import mybir
from contextlib import ExitStack

FP32 = mybir.dt.float32
FP32R = mybir.dt.float32r
ALU = mybir.AluOpType
ACT = mybir.ActivationFunctionType
AX = mybir.AxisListType

P = 128
D = 1024
KD = D // P
SEQ = 2048
NPT = SEQ // P
DB, DT = 8, 8
NS = DB * DT
NTOK = SEQ + NS
NTILE = NPT + 1
PAIRS = NPT // 2
H, HD = 8, 64
AW = H * HD
SHIFT_W = 3 * AW + 2 * HD
EVEN_W = SHIFT_W + AW + 4 * AW
NG = 3
ODD_W = 3 * NG * AW + AW
PAD = 2
R0, K0, V0, L0, ZA0, B0, C0, HH0, ZB0 = 0, AW, 2 * AW, 3 * AW, SHIFT_W, SHIFT_W + AW, SHIFT_W + 2 * AW, \
    SHIFT_W + 3 * AW, SHIFT_W + 4 * AW
SLOTS = 2


def each_tile(eng, body, tail=True):
    with eng.Fori(0, PAIRS) as i:
        for s in range(SLOTS):
            body(2 * i + s, s, i)
    if tail:
        body(NPT, 0, PAIRS)


class Sems(dict):

    def __init__(self, nc, ctx, phase, names, own={}):
        self.nc, self.own = nc, own
        self.update(own)
        for n in names.split():
            self[n] = ctx.enter_context(nc.semaphore(f"{phase}_{n}"))
        ctx.callback(self.clear)

    def clear(self):
        with self.nc.Block() as block:
            @block.sync
            def _(sp):
                for n, sem in self.items():
                    if n not in self.own:
                        sp.sem_clear(sem)


def transpose_in(nc, x_prompt, x_sample, x_high, x_low, ident, p_pad, ps_pad, state_shift, state_conv, sw):
    with ExitStack() as ctx:
        xin = ctx.enter_context(nc.sbuf_tensor("ti_x", [P, SLOTS, D], FP32))
        tp = [ctx.enter_context(nc.psum_tensor(f"ti_p{i}", [P, 4, P], FP32)) for i in range(2 * SLOTS)]
        zeros = ctx.enter_context(nc.sbuf_tensor("ti_zero", [PAD, SHIFT_W], FP32))
        ones = ctx.enter_context(nc.sbuf_tensor("ti_one", [DB, PAD, AW], FP32))
        s = Sems(nc, ctx, "ti", "ident_zero ident x_loaded0 x_loaded1 transposed high split filled", {"padded": sw["padded"]})
        block = ctx.enter_context(nc.Block())

        @block.gpsimd
        def _(pool):
            nc.gpsimd.memset(ident[:], 0.0).then_inc(s["ident_zero"], 1)
            pool.wait_ge(s["ident_zero"], 1)
            nc.gpsimd.affine_select(out=ident[:], in_=ident[:], compare_op=ALU.not_equal, fill=1.0, base=0,
                                    pattern=[[-1, P]], channel_multiplier=1).then_inc(s["ident"], 1)
            nc.gpsimd.memset(zeros[:], 0.0).then_inc(s["filled"], 1)
            nc.gpsimd.memset(ones[:].rearrange("b a n -> b (a n)"), 1.0).then_inc(s["filled"], 1)
            pool.wait_ge(s["filled"], 2)
            for dst, src in ((p_pad[0:PAD, C0:C0 + 2 * AW], zeros[:, 0:2 * AW]), (p_pad[PAD - 1:PAD, 0:SHIFT_W], zeros[0:1, :]),
                             (ps_pad[:, 0:PAD, HH0:HH0 + AW], ones[:]), (ps_pad[:, 0:PAD, C0:HH0], state_conv),
                             (ps_pad[:, PAD - 1, 0:SHIFT_W], state_shift)):
                pool.dma_start(dst, src).then_inc(s["padded"], 16)
            pool.wait_ge(s["padded"], 16 * 5)

        @block.sync
        def _(sp):
            def load(t, b, u):
                sp.wait_ge(s["transposed"], t + 1)
                src = x_prompt[0, bass.ds(t * P, P), :] if u is not PAIRS else x_sample.rearrange("b t d -> (b t) d")
                rows = P if u is not PAIRS else NS
                sp.dma_start(xin[0:rows, b, :], src).then_inc(s[f"x_loaded{b}"], 16)
            each_tile(sp, load)

        @block.tensor
        def _(pe):
            pe.sem_inc(s["transposed"], SLOTS)
            pe.wait_ge(s["ident"], 1)

            def turn(t, b, u):
                rows = P if u is not PAIRS else NS
                pe.wait_ge(s[f"x_loaded{b}"], 16 * (u + 1))
                pe.wait_ge(s["split"], 2 * t + 2)
                for k in range(KD):
                    mm = nc.tensor.transpose(tp[2 * b + k // 4][:, k % 4, 0:rows], xin[0:rows, b, k * P:(k + 1) * P],
                                             ident[0:rows, 0:rows])
                mm.then_inc(s["transposed"], 1)
            each_tile(pe, turn)

        def halves(t, b, rows):
            at = lambda x, i: x[:, 4 * i:4 * i + 4, bass.ds(t * P, rows)]
            return [(tp[2 * b + i][:, :, 0:rows], at(x_high, i), at(x_low, i)) for i in range(2)]

        @block.vector
        def _(dve):
            dve.sem_inc(s["split"], 2 * SLOTS)

            def low(t, b, u):
                for i, (src, high, dst) in enumerate(halves(t, b, P if u is not PAIRS else NS)):
                    dve.wait_ge(s["high"], 2 * t + i + 1)
                    nc.vector.tensor_tensor(dst, src, high.bitcast(FP32), ALU.subtract).then_inc(s["split"], 1)
            each_tile(dve, low)

        @block.scalar
        def _(act):
            def high(t, b, u):
                act.wait_ge(s["transposed"], t + 1 + SLOTS)
                for src, dst, _ in halves(t, b, P if u is not PAIRS else NS):
                    nc.scalar.copy(dst, src).then_inc(s["high"], 1)
            each_tile(act, high)


def project_in(nc, ph, x_high, x_low, w, cw, n_chunks, p_prompt, p_sample, sw, beside=None):
    NB = 4
    PER = NPT // NB
    with ExitStack() as ctx:
        wc = ctx.enter_context(nc.sbuf_tensor(f"{ph}_w", [P, KD, cw], FP32))
        one = ctx.enter_context(nc.sbuf_tensor(f"{ph}_one", [P, 1], FP32))
        w_high = ctx.enter_context(nc.sbuf_tensor(f"{ph}_w_high", [P, SLOTS, KD, cw], FP32R))
        w_low = ctx.enter_context(nc.sbuf_tensor(f"{ph}_w_low", [P, SLOTS, KD, cw], FP32R))
        stage = ctx.enter_context(nc.sbuf_tensor(f"{ph}_stage", [P, NB + 1, cw], FP32))
        ps = [ctx.enter_context(nc.psum_tensor(f"{ph}_ps{i}", [P, 512], FP32)) for i in range(NB + 1)]
        s = Sems(nc, ctx, ph, "one w_high w_split chunk_done tile_done even_out odd_out "
                              "stored0 stored1 stored2 stored3 stored4",
                 {f"w_loaded{b}": sw[f"{ph}_w_loaded{b}"] for b in range(SLOTS)})
        n_even, n_odd = NPT // 2 + 1, NPT // 2

        def each_chunk(eng, body):
            with eng.Fori(0, n_chunks // 2) as i:
                for b in range(SLOTS):
                    body(2 * i + b, b, i)

        block = ctx.enter_context(nc.Block())

        @block.gpsimd
        def _(pool):
            def load(c, b, u):
                pool.wait_ge(s["w_split"], c + 1)
                pool.wait_ge(s["chunk_done"], c + 1)
                pool.dma_start(wc[:], w[:, bass.ds(c * cw, cw)].rearrange("(k p) n -> p k n", p=P))\
                    .then_inc(s[f"w_loaded{b}"], 16)
                pool.wait_ge(s[f"w_loaded{b}"], 16 * (u + 1))
                nc.gpsimd.tensor_tensor(w_high[:, b, :, :].rearrange("p k n -> p (k n)"), wc[:].rearrange("p k n -> p (k n)"),
                                        one[:].broadcast_to([P, KD * cw]), ALU.mult).then_inc(s["w_high"], 1)
                pool.wait_ge(s["w_high"], c + 1)
                nc.gpsimd.tensor_tensor(w_low[:, b, :, :], wc[:], w_high[:, b, :, :].bitcast(FP32), ALU.subtract)\
                    .then_inc(s["w_split"], 1)
            nc.gpsimd.memset(one[:], 1.0).then_inc(s["one"], 1)
            pool.wait_ge(s["one"], 1)
            pool.sem_inc(s["w_split"], 1)
            each_chunk(pool, load)

        @block.tensor
        def _(pe):
            pe.sem_inc(s["chunk_done"], SLOTS)

            def chunk(c, b, u):
                pe.wait_ge(s["w_split"], c + 2)
                for t in range(NTILE):
                    bank, rows = (t % NB, P) if t < NPT else (NB, NS)
                    if t % 2 == 0:
                        pe.wait_ge(s["even_out"], c * n_even + 1 + (max(t - NB + 2, 0) // 2))
                    else:
                        pe.wait_ge(s["odd_out"], c * n_odd + 1 + (max(t - NB + 1, 0) // 2))
                    for k in range(KD):
                        for i, (x, y) in enumerate(((x_high, w_high), (x_high, w_low), (x_low, w_high))):
                            mm = nc.tensor.matmul(ps[bank][0:rows, 0:cw], x[:, k, t * P:t * P + rows], y[:, b, k, :],
                                                  start=(k == 0 and i == 0), stop=(k == KD - 1 and i == 2))
                    if t < NPT:
                        mm.then_inc(s["tile_done"], 1)
                    else:
                        mm.then_inc(s["chunk_done"], 1)
            each_chunk(pe, chunk)

        def copy_out(eng, copy, parity, out_sem):
            eng.sem_inc(out_sem, 1)

            def chunk(c, b, u):
                if parity and b == 0 and beside:
                    beside(eng, u)
                for t in range(parity, NTILE, 2):
                    bank, rows = (t % NB, P) if t < NPT else (NB, NS)
                    if t < NPT:
                        eng.wait_ge(s["tile_done"], c * NPT + t + 1)
                        eng.wait_ge(s[f"stored{bank}"], 16 * (c * PER + t // NB) + 1)
                    else:
                        eng.wait_ge(s["chunk_done"], c + 1 + SLOTS)
                        eng.wait_ge(s[f"stored{bank}"], 16 * c + 1)
                    copy(stage[0:rows, bank, :], ps[bank][0:rows, 0:cw]).then_inc(out_sem, 1)
            each_chunk(eng, chunk)

        @block.vector
        def _(dve):
            copy_out(dve, nc.vector.tensor_copy, 0, s["even_out"])

        @block.scalar
        def _(act):
            copy_out(act, nc.scalar.copy, 1, s["odd_out"])

        @block.sync
        def _(sp):
            for b in range(NB + 1):
                sp.sem_inc(s[f"stored{b}"], 1)

            def chunk(c, b, u):
                for t in range(NTILE):
                    bank, rows = (t % NB, P) if t < NPT else (NB, NS)
                    if t % 2 == 0:
                        sp.wait_ge(s["even_out"], c * n_even + t // 2 + 2)
                    else:
                        sp.wait_ge(s["odd_out"], c * n_odd + t // 2 + 2)
                    cols = bass.ds(c * cw, cw)
                    dst = p_prompt[t * P:t * P + rows, cols] if t < NPT else p_sample[:, :, cols]
                    sp.dma_start(dst, stage[0:rows, bank, :]).then_inc(s[f"stored{bank}"], 16)
            each_chunk(sp, chunk)
            for b in range(NB):
                sp.wait_ge(s[f"stored{b}"], 16 * n_chunks * PER + 1)
            sp.wait_ge(s[f"stored{NB}"], 16 * n_chunks + 1)


CHUNK = 64
NCH = P // CHUNK
HP = H // 2
LEVELS = 6
LD_SCALE = -0.6065306597126334
GN_EPS = 64e-5
LN_EPS = 1e-5
ALPHA = 4 ** 0.25


def rwkv_constants():
    import numpy as np
    i = np.arange(P)
    same = (i[:, None] // CHUNK) == (i[None, :] // CHUNK)
    upto = same & (i[:, None] <= i[None, :])
    before = same & (i[:, None] < i[None, :])
    off = [(i[:, None] // (2 * m) == i[None, :] // (2 * m)) & (i[:, None] // m > i[None, :] // m)
           for m in (1, 2, 4, 8, 16, 32)]
    eye64 = (i[:, None] % HD) == np.arange(HD)[None, :]
    chunk = (i[:, None] // CHUNK) == np.arange(NCH)[None, :]
    cols = [upto, before, upto, before, upto, off[0].T, *off[1:], eye64, chunk]
    return np.ascontiguousarray(np.concatenate([c.astype(np.float32) for c in cols], axis=1))


CONST_W = 5 * P + LEVELS * P + HD + NCH


class Chain:

    def __init__(self, eng, sem, per_tile):
        self.eng, self.sem, self.per_tile = eng, sem, per_tile

    def start(self, t, n=0):
        self.t, self.n = t, n

    def __call__(self, ins):
        self.n += 1
        ins.then_inc(self.sem, 1)
        self.eng.wait_ge(self.sem, self.t * self.per_tile + self.n)

    def end(self):
        assert self.n == self.per_tile, (self.n, self.per_tile)


def heads(ap):
    return ap.rearrange("p (h d) -> p h d", h=H)


def pairs(bank):
    return bank[:, 0:AW // 2].rearrange("p (h d) -> p h d", d=HD)


def over(ap, n):
    return ap.unsqueeze(2).broadcast_to([ap.shape[0], ap.shape[1], n])


def each(ap, n):
    return ap.unsqueeze(1).broadcast_to([ap.shape[0], n, ap.shape[1]])


def even_mix(nc, ident, p_pad, ps_pad, consts, state_rwkv, rw, conv_w, y_prompt, y_sample, scan_in, scan_y,
             state_p_out, state_s_out, shift_p_out, shift_s_out, conv_p_out, conv_s_out, sw):
    mu, w0, w2, a0, a2, k_k, k_a, r_k, gn_g, gn_b = rw
    with ExitStack() as ctx:
        def sb(name, shape):
            return ctx.enter_context(nc.sbuf_tensor(f"em_{name}", shape, FP32))

        cur = sb("cur", [P, SLOTS, EVEN_W])
        ps = sb("ps", [P, SLOTS, SHIFT_W])
        V = sb("V", [P, SLOTS, AW])
        ch1, ch2 = sb("ch1", [P, 2 * AW]), sb("ch2", [P, 2 * AW])
        cst = sb("cst", [P, CONST_W])
        mu_b = sb("mu", [P, SHIFT_W])
        par = sb("par", [P, 10, AW])
        w2a2 = sb("w2a2", [P, 2, AW])
        W0, A0, KK, KA, RK, GG, GB, CW = 0, 1, 2, 3, 4, 5, 6, 7
        lora = sb("lora", [P, P])
        wa = sb("wa", [P, 2 * AW])
        pc_, pinv, pprev = sb("pc", [P, AW]), sb("pinv", [P, AW]), sb("pprev", [P, AW])
        pend = sb("pend", [P, SLOTS, HP * NCH])
        kk, sq = sb("kk", [P, AW]), sb("sq", [P, AW])
        kn = kk
        bv, kp = sb("bv", [P, AW]), sb("kp", [P, AW])
        rt, bt, kt = sb("rt", [P, AW]), sb("bt", [P, SLOTS, AW]), sb("kt", [P, SLOTS, AW])
        za = sb("za", [P, SLOTS, 2, H, HD])
        ss, rs, bonus = sb("ss", [P, H]), sb("rs", [P, H]), sb("bonus", [P, H])
        half = sb("half", [P, H])
        ZR = sb("ZR", [P, 2, HP, 2, P])
        BT, KT = sb("BT", [P, HP, P]), sb("KT", [P, HP, P])
        AM = sb("AM", [P, H, 4, P])
        T, X = sb("T", [P, H, P]), sb("X", [P, H, P])
        Ym = sb("Ym", [P, H, P])
        WU = sb("WU", [P, H, 2, HD])
        QT = sb("QT", [P, HP, P])
        M1, G = sb("M1", [P, NCH, HP, HD]), sb("G", [P, NCH, HP, HD])
        M_BANK, G_BANK = (2, 7), (4, 0)
        S = sb("S", [P, NCH, HP, HD])
        yl = Ym[:, 0:4, :].rearrange("p h n -> p (h n)")
        y = sb("y", [P, AW])
        mean, var, rstd = sb("mean", [P, H]), sb("var", [P, H]), sb("rstd", [P, H])
        u0 = sb("u0", [P, AW])
        rkv = sb("rkv", [P, SLOTS, AW])
        tz = sb("tz", [P, 2 * AW])
        gate = sb("gate", [P, SLOTS, AW])
        yout = sb("yout", [P, SLOTS, 2 * AW])
        bank = [ctx.enter_context(nc.psum_tensor(f"em_b{i}", [P, 512], FP32)) for i in range(8)]
        sc_z, sc_b, sc_w, sc_k, sc_r = [AM[:, i, :, :].rearrange("p a b -> p (a b)") for i in range(5)]
        sc_v = AM[:, 5, 0:2, :].rearrange("p a b -> p (a b)")
        sc_y = AM[:, 6, 0:2, :].rearrange("p a b -> p (a b)")
        sa = AM[:, 7, 0, 0:32]
        state = cur[:, 1, 0:2048].rearrange("p (i j) -> p i j", j=HD)
        outer = cur[:, 1, 2048:4096].rearrange("p (i j) -> p i j", j=HD)
        outer2 = ps[:, :, :].rearrange("p a b -> p (a b)")[:, 0:2048].rearrange("p (i j) -> p i j", j=HD)
        s_vk = yout[0:HD, 1, 0:H * HD]

        s = Sems(nc, ctx, "em",
                 "cst loaded0 loaded1 ch_loaded half zero shifted conv lora_T lora lora_mm wa_in tanh ld kk sq "
                 "ss rs kp rk bonus cum cprev exps zbk rt zrbk_T0 zrbk_T1 zrbk_T2 zrbk_T3 zrbk_out a_mm masked x1 "
                 "t1_T t1 y_mm ym d_mm t_add x_T x_out av_mm av wu_mm wu q_mm yl_mm m_mm q m1 yl g_mm g_out s_mm "
                 "s_new y_cross y_sum centred ysq var rstd ynorm gates gated stored state_out y_back s_T s_vk rkv "
                 "dve_p dve_c dve_n act pool_s pool_c pool_f scan_out scan_loaded vk vk_free scan_y",
                 {n: sw[n] for n in ("conv_out", "conv_s_out")})
        block = ctx.enter_context(nc.Block())
        c_tri = cst[:, 0:P]
        c_zr = cst[:, P:5 * P]
        c_off = [cst[:, (5 + i) * P:(6 + i) * P] for i in range(LEVELS)]
        c_eye = cst[:, 11 * P:11 * P + HD]
        c_chunk = cst[:, 11 * P + HD:11 * P + HD + NCH]
        LOADS, CSTS = 2, 14
        STATE_OUTS = 2 + 2 + 1
        L = LEVELS - 1

        def rows_of(t):
            return NS if isinstance(t, int) and t == NPT else P

        def walk(eng, step, peeled=1):
            step(0, 0, 0)
            step(1, 1, 0)
            with eng.Fori(1, PAIRS - peeled) as i:
                step(2 * i, 0, i)
                step(2 * i + 1, 1, i)
            for t in range(NPT - 2 * peeled, NPT):
                step(t, t % 2, t // 2)

        def first(t):
            return isinstance(t, int) and t == 0

        def final(t):
            return isinstance(t, int) and t == NPT - 1

        @block.sync
        def _(sp):
            row = lambda a: a.rearrange("(o n) -> o n", o=1)
            sp.wait_ge(s["zero"], 2)

            def load(t, b):
                n = rows_of(t)
                for dst, j, lo, hi in ((cur, 0, 0, EVEN_W), (ps, 1, 0, SHIFT_W)):
                    src = (ps_pad[:, PAD - j:PAD - j + DT, lo:hi] if n == NS else p_pad[bass.ds(t * P + PAD - j, P), lo:hi])
                    sp.dma_start(dst[0:n, b, :], src).then_inc(s[f"loaded{b}"], 16)

            def load_ch(t):
                n = rows_of(t)
                for dst, j in ((ch1, 1), (ch2, 2)):
                    src = ps_pad[:, PAD - j:PAD - j + DT, C0:ZB0] if n == NS else p_pad[bass.ds(t * P + PAD - j, P), C0:ZB0]
                    sp.dma_start(dst[0:n, :], src).then_inc(s["ch_loaded"], 16)

            def store(t, b):
                sp.wait_ge(s["gated"], t + 1)
                n = rows_of(t)
                dst = y_sample if n == NS else y_prompt[bass.ds(t * P, P), :]
                sp.dma_start(dst, yout[0:n, b, :]).then_inc(s["stored"], 16)

            load(0, 0)
            load_ch(0)
            for dst, src in ((mu_b[:], row(mu)), *[(par[:, j, :], row(a)) for j, a in
                             enumerate((w0, a0, k_k, k_a, r_k.rearrange("h d -> (h d)"), gn_g, gn_b,
                                        conv_w[0], conv_w[1], conv_w[2]))]):
                sp.dma_start(dst, src.broadcast_to([P, src.shape[1]])).then_inc(s["cst"], 16)
            sp.dma_start(cst[:], consts).then_inc(s["cst"], 16)
            sp.dma_start(w2a2[0:HD, 0, :], w2).then_inc(s["cst"], 16)
            sp.dma_start(w2a2[HD:P, 1, :], a2).then_inc(s["cst"], 16)
            sp.sem_inc(s["stored"], 32)
            load(1, 1)

            def prepared(t):
                sp.wait_ge(s["conv"], t + 1)
                if not (isinstance(t, int) and t >= NPT):
                    load_ch(t + 1)
                sp.wait_ge(s["rt"], t + 1)
                sp.wait_ge(s["zbk"], t + 1)

            prepared(0)
            load(2, 0)

            def step(t, b, u):
                if not first(t):
                    store(t - 1, 1 - b)
                if final(t):
                    return
                prepared(t + 1)
                if not (isinstance(t, int) and t + 3 > NPT):
                    load(t + 3, 1 - b)
            walk(sp, step, peeled=2)
            store(NPT - 1, 1)
            store(NPT, 0)
            sp.dma_start(shift_p_out, p_pad[PAD + SEQ - 1:PAD + SEQ, 0:SHIFT_W]).then_inc(s["state_out"], 16)
            sp.dma_start(shift_s_out, ps_pad[:, PAD + DT - 1, 0:SHIFT_W]).then_inc(s["state_out"], 16)
            sp.wait_ge(s["stored"], 16 * (NTILE + 2))
            sp.wait_ge(s["state_out"], 16 * STATE_OUTS)

        @block.gpsimd
        def _(pool):
            g = nc.gpsimd
            ch_s, ch_c, ch_f = (Chain(pool, s[f"pool_{c}"], n) for c, n in (("s", 2), ("c", 11), ("f", 2)))
            g.memset(w2a2[:].rearrange("p a n -> p (a n)"), 0.0).then_inc(s["zero"], 1)
            g.memset(ZR[:].rearrange("p a b c d -> p (a b c d)"), 0.0).then_inc(s["zero"], 1)
            g.memset(half[:], -0.5).then_inc(s["half"], 1)
            pool.wait_ge(s["half"], 1)
            pool.wait_ge(s["zero"], 2)
            pool.wait_ge(s["cst"], 16 * CSTS)

            def shift(t, b, u):
                n = rows_of(t)
                ch_s.start(t)
                pool.wait_ge(s[f"loaded{b}"], 16 * LOADS * (u + 1))
                c, x = cur[0:n, b, 0:SHIFT_W], ps[0:n, b, :]
                ch_s(g.tensor_tensor(x, x, c, ALU.subtract))
                ch_s(g.tensor_tensor(x, x, mu_b[0:n, :], ALU.mult))
                if not (isinstance(t, int) and t < SLOTS):
                    pool.wait_ge(s["g_mm"], NCH * (t - 1))
                g.tensor_tensor(V[0:n, b, :], x[:, V0:L0], c[:, V0:L0], ALU.add)
                g.tensor_tensor(x[:, L0:], x[:, L0:], c[:, L0:], ALU.add)
                g.tensor_tensor(x[:, 0:V0], x[:, 0:V0], c[:, 0:V0], ALU.add).then_inc(s["shifted"], 1)
                pool.wait_ge(s["shifted"], t + 1)
                ch_s.end()

            def norm_k(t):
                n = rows_of(t)
                pool.wait_ge(s["ss"], t + 1)
                g.tensor_tensor(rs[0:n], ss[0:n], half[0:n], ALU.pow).then_inc(s["rs"], 1)

            def conv(t, b):
                n = rows_of(t)
                c = cur[0:n, b, :]
                ch_c.start(t)
                pool.wait_ge(s["ch_loaded"], 32 * (t + 1))
                a1, b1, a2_, b2 = ch1[0:n, 0:AW], ch1[0:n, AW:], ch2[0:n, 0:AW], ch2[0:n, AW:]
                ch_c(g.tensor_tensor(u0[0:n], c[:, C0:HH0], c[:, HH0:ZB0], ALU.mult))
                ch_c(g.tensor_tensor(a1, a1, b1, ALU.mult))
                ch_c(g.tensor_tensor(a2_, a2_, b2, ALU.mult))
                ch_c(g.tensor_tensor(a2_, a2_, par[0:n, CW, :], ALU.mult))
                ch_c(g.tensor_tensor(a1, a1, par[0:n, CW + 1, :], ALU.mult))
                ch_c(g.tensor_tensor(b1, u0[0:n], par[0:n, CW + 2, :], ALU.mult))
                ch_c(g.tensor_tensor(a1, a1, a2_, ALU.add))
                ch_c(g.tensor_tensor(a1, a1, b1, ALU.add))
                ch_c(g.tensor_tensor(a1, a1, c[:, B0:C0], ALU.mult))
                pool.wait_ge(s["gates"], t + 1)
                g.tensor_tensor(gate[0:n, b, :], tz[0:n, 0:AW], c[:, ZA0:B0], ALU.mult)
                ch_c(g.tensor_tensor(tz[0:n, AW:], tz[0:n, AW:], c[:, ZB0:], ALU.mult))
                pool.wait_ge(s["stored"], 16 * (t + 1))
                ch_c(g.tensor_tensor(yout[0:n, b, AW:], a1, tz[0:n, AW:], ALU.mult))
                pool.sem_inc(s["conv"], 1)
                ch_c.end()

            def bonus_in(t, b):
                n = rows_of(t)
                r = ps[0:n, b, R0:K0]
                pool.wait_ge(s["kp"], t + 1)
                g.tensor_tensor(sq[0:n], r, kp[0:n], ALU.mult).then_inc(s["rk"], 1)
                pool.wait_ge(s["rk"], 2 * t + 1)
                g.tensor_tensor(sq[0:n], sq[0:n], par[0:n, RK, :], ALU.mult).then_inc(s["rk"], 1)
                if n == P:
                    pool.wait_ge(s["exps"], t + 1)
                    g.tensor_tensor(rt[0:n], r, pc_[0:n], ALU.mult).then_inc(s["rt"], 1)
                pool.wait_ge(s["bonus"], t + 1)
                g.tensor_tensor(heads(rkv[0:n, b, :]), heads(V[0:n, b, :]), over(bonus[0:n], HD), ALU.mult).then_inc(s["rkv"], 1)

            def finish_a(t):
                n = rows_of(t)
                pool.wait_ge(s["var"], t + 1)
                g.tensor_tensor(rstd[0:n], var[0:n], half[0:n], ALU.pow).then_inc(s["rstd"], 1)

            def finish(t, b):
                n = rows_of(t)
                ch_f.start(t)
                finish_a(t)
                pool.wait_ge(s["ynorm"], t + 1)
                ch_f(g.tensor_tensor(y[0:n], y[0:n], par[0:n, GB, :], ALU.add))
                ch_f(g.tensor_tensor(y[0:n], y[0:n], rkv[0:n, b, :], ALU.add))
                g.tensor_tensor(yout[0:n, b, 0:AW], y[0:n], gate[0:n, b, :], ALU.mult).then_inc(s["gated"], 1)
                pool.wait_ge(s["gated"], t + 1)
                ch_f.end()

            shift(0, 0, 0)
            norm_k(0)
            conv(0, 0)
            bonus_in(0, 0)
            shift(1, 1, 0)

            def step(t, b, u):
                if not first(t):
                    finish(t - 1, 1 - b)
                norm_k(t + 1)
                conv(t + 1, 1 - b)
                bonus_in(t + 1, 1 - b)
                if not final(t):
                    shift(t + 2, b, u + 1)
                if isinstance(t, int) and t == NPT - 2:
                    pool.dma_start(conv_p_out, u0[P - 2:P, :]).then_inc(s["conv_out"], 16)
                    pool.wait_ge(s["conv_out"], 16)
            walk(pool, step)
            for q in range(DB):
                pool.dma_start(conv_s_out[q], u0[DT * q + DT - 2:DT * q + DT, :]).then_inc(s["conv_s_out"], 16)
            finish(NPT - 1, 1)
            pool.wait_ge(s["scan_loaded"], 16 * 14)
            for i in range(DT):
                if i:
                    pool.wait_ge(s["vk_free"], i)
                g.tensor_tensor(outer2, over(sc_v[:, 32 * i:32 * i + 32], HD),
                                each(sc_k[:, HD * i:HD * i + HD], 32), ALU.mult).then_inc(s["vk"], 1)
            finish(NPT, 0)
            pool.wait_ge(s["conv_s_out"], 16 * DB)

        @block.vector
        def _(dve):
            v = nc.vector
            ch_p, ch_c, ch_n = (Chain(dve, s[f"dve_{c}"], n) for c, n in (("p", 6), ("c", 3 + NCH), ("n", 4)))
            dve.wait_ge(s["cst"], 16 * CSTS)
            v.memset(S[:, 0, :, :], 0.0).then_inc(s["s_new"], 1)
            dve.wait_ge(s["s_new"], 1)

            def prep_k(t, b):
                n = rows_of(t)
                ch_p.start(t)
                dve.wait_ge(s["shifted"], t + 1)
                v.tensor_tensor(kk[0:n], ps[0:n, b, K0:V0], par[0:n, KK, :], ALU.mult).then_inc(s["kk"], 1)

            def prep_ss(t):
                n = rows_of(t)
                dve.wait_ge(s["sq"], t + 1)
                ch_p(v.tensor_reduce(ss[0:n], heads(sq[0:n]), AX.X, ALU.add))
                v.tensor_scalar(ss[0:n], ss[0:n], 1e-24, None, ALU.max).then_inc(s["ss"], 1)

            def prep_wa(t):
                n = rows_of(t)
                dve.wait_ge(s["lora_mm"], t + 1)
                ch_p(v.tensor_tensor(wa[0:n, 0:AW], bank[7][0:n, :], par[0:n, W0, :], ALU.add))
                v.tensor_tensor(wa[0:n, AW:], bank[6][0:n, :], par[0:n, A0, :], ALU.add).then_inc(s["wa_in"], 1)

            def prep_kp(t, b):
                n = rows_of(t)
                k, a = ps[0:n, b, K0:V0], wa[0:n, AW:]
                dve.wait_ge(s["tanh"], t + 1)
                ch_p(v.tensor_scalar(a, a, 0.5, 0.5, ALU.mult, ALU.add))
                dve.wait_ge(s["rs"], t + 1)
                ch_p(v.tensor_tensor(heads(kn[0:n]), heads(kk[0:n]), over(rs[0:n], HD), ALU.mult))
                ch_p(v.tensor_tensor(bv[0:n], kn[0:n], a, ALU.mult))
                ch_p(v.scalar_tensor_tensor(kp[0:n], a, -1.0, par[0:n, KA, :], ALU.add, ALU.mult))
                v.scalar_tensor_tensor(kp[0:n], kp[0:n], 1.0, k, ALU.add, ALU.mult).then_inc(s["kp"], 1)

            def prep_ld(t):
                n = rows_of(t)
                dve.wait_ge(s["tanh"], t + 1)
                v.tensor_scalar(wa[0:n, 0:AW], wa[0:n, 0:AW], LD_SCALE / 2, LD_SCALE / 2, ALU.mult, ALU.add)\
                    .then_inc(s["ld"], 1)

            def prep_cprev(t):
                dve.wait_ge(s["cum"], t + 1)
                v.tensor_tensor(pprev[:], bank[4][:], wa[:, 0:AW], ALU.subtract).then_inc(s["cprev"], 1)

            def prep_end(t, b):
                n = rows_of(t)
                if n == P:
                    dve.wait_ge(s["exps"], t + 1)
                    v.tensor_tensor(bt[:, b, :], bv[:], pinv[:], ALU.mult)
                    v.tensor_tensor(kt[:, b, :], kp[:], pinv[:], ALU.mult)
                    v.scalar_tensor_tensor(za[:, b, 0, :, :], heads(kn[:]), -1.0, heads(pprev[:]), ALU.mult, ALU.mult)\
                        .then_inc(s["zbk"], 1)
                dve.wait_ge(s["rk"], 2 * t + 2)
                v.tensor_reduce(bonus[0:n], heads(sq[0:n]), AX.X, ALU.add).then_inc(s["bonus"], 1)
                dve.wait_ge(s["bonus"], t + 1)
                ch_p.end()

            def prep_all(t, b):
                prep_k(t, b)
                prep_ss(t)
                prep_wa(t)
                prep_ld(t)
                prep_kp(t, b)
                prep_cprev(t)
                prep_end(t, b)

            def norm_a(t):
                n = rows_of(t)
                yh = heads(y[0:n])
                ch_n.start(t)
                ch_n(v.tensor_reduce(mean[0:n], yh, AX.X, ALU.add))
                ch_n(v.tensor_scalar(mean[0:n], mean[0:n], 1.0 / HD, None, ALU.mult))
                v.tensor_tensor(yh, yh, over(mean[0:n], HD), ALU.subtract).then_inc(s["centred"], 1)

            def norm_b(t):
                n = rows_of(t)
                ch_n.start(t, 2)
                dve.wait_ge(s["ysq"], t + 1)
                ch_n(v.tensor_reduce(var[0:n], heads(sq[0:n]), AX.X, ALU.add))
                v.tensor_scalar(var[0:n], var[0:n], 1.0 / HD, GN_EPS, ALU.mult, ALU.add).then_inc(s["var"], 1)

            def norm_c(t):
                n = rows_of(t)
                yh = heads(y[0:n])
                ch_n.start(t, 3)
                dve.wait_ge(s["rstd"], t + 1)
                ch_n(v.tensor_tensor(yh, yh, over(rstd[0:n], HD), ALU.mult))
                v.tensor_tensor(y[0:n], y[0:n], par[0:n, GG, :], ALU.mult).then_inc(s["ynorm"], 1)

            def step(t, b, u):
                sample_next = final(t)
                ch_c.start(t)
                for h in range(H):
                    dve.wait_ge(s["a_mm"], H * t + h + 1)
                    v.tensor_tensor(AM[:, h, :, :].rearrange("p a b -> p (a b)"), bank[h % 4][:], c_zr, ALU.mult)\
                        .then_inc(s["masked"], 1)
                dve.wait_ge(s["masked"], H * (t + 1))
                for g in range(2):
                    hs = slice(4 * g, 4 * g + 4)
                    ch_c(v.tensor_tensor(X[:, hs, :], AM[:, hs, 0, :], each(c_off[0], 4), ALU.mult))
                    v.tensor_tensor(X[:, hs, :], X[:, hs, :], each(ident[:], 4), ALU.add).then_inc(s["x1"], 1)
                for lv in range(1, LEVELS):
                    for g in range(2):
                        hs = slice(4 * g, 4 * g + 4)
                        dve.wait_ge(s["y_mm"], 2 * (L * t + lv - 1) + g + 1)
                        v.tensor_tensor(Ym[:, hs, :], bank[g][:].rearrange("p (h n) -> p h n", h=4),
                                        each(c_off[lv], 4), ALU.mult).then_inc(s["ym"], 1)
                    for g in range(2):
                        hs = slice(4 * g, 4 * g + 4)
                        dve.wait_ge(s["d_mm"], 2 * (L * t + lv - 1) + g + 1)
                        M = T if lv < LEVELS - 1 else X
                        v.tensor_tensor(M[:, hs, :], M[:, hs, :], bank[2 + g][:].rearrange("p (h n) -> p h n", h=4),
                                        ALU.add).then_inc(s["t_add"], 1)
                    if lv == 1:
                        if not first(t):
                            norm_b(t - 1)
                        prep_k(t + 1, 1 - b)
                    elif lv == 2:
                        if not first(t):
                            norm_c(t - 1)
                        prep_ss(t + 1)
                    elif lv == 3:
                        prep_wa(t + 1)
                    elif lv == 4:
                        prep_ld(t + 1)
                        prep_kp(t + 1, 1 - b)
                if not sample_next:
                    prep_cprev(t + 1)
                dve.wait_ge(s["q_mm"], t + 1)
                for e in range(2):
                    r_ = slice(HD * e, HD * e + HD)
                    m = v.tensor_tensor(QT[r_], bank[0][r_].rearrange("p (h n) -> p h n", h=HP), ZR[r_, e, :, 1, :], ALU.add)
                m.then_inc(s["q"], 1)
                dve.wait_ge(s["m_mm"], t + 1)
                for c in range(NCH):
                    v.tensor_tensor(M1[:, c, :, :], pairs(bank[M_BANK[c]]), each(c_eye, HP), ALU.add)\
                        .then_inc(s["m1"], 1)
                prep_end(t + 1, 1 - b)
                for c in range(NCH):
                    dve.wait_ge(s["s_mm"], NCH * t + c + 1)
                    if c == NCH - 1:
                        dve.wait_ge(s["y_cross"], 2 * t + 1)
                    dve.wait_ge(s["g_out"], NCH * t + c + 1)
                    new = S[:, (c + 1) % NCH, :, :]
                    ch_c(v.tensor_tensor(new, pairs(bank[3]), G[:, c, :, :], ALU.add))
                    v.tensor_tensor(new, new, over(pend[:, b, c::NCH], HD), ALU.mult).then_inc(s["s_new"], 1)
                dve.wait_ge(s["y_cross"], 2 * t + 2)
                dve.wait_ge(s["yl"], t + 1)
                if not first(t):
                    dve.wait_ge(s["gated"], t)
                y4, yl4 = [a.rearrange("p (h e d) -> p h e d", e=2, d=HD) for a in (y[:], yl)]
                ch_c(v.tensor_tensor(y4[:, :, 0, :], yl4[:, :, 0, :], pairs(bank[5]), ALU.add))
                v.tensor_tensor(y4[:, :, 1, :], yl4[:, :, 1, :], pairs(bank[6]), ALU.add).then_inc(s["y_sum"], 1)
                dve.wait_ge(s["y_sum"], t + 1)
                ch_c.end()
                norm_a(t)

            prep_all(0, 0)
            walk(dve, step)
            norm_b(NPT - 1)
            norm_c(NPT - 1)

            steps = Chain(dve, s["dve_c"], 0)
            steps.t, steps.n = 0, NPT * ch_c.per_tile
            dve.wait_ge(s["scan_loaded"], 16 * 14)
            for i in range(DT):
                z, bb, w, rr = [a[:, HD * i:HD * i + HD] for a in (sc_z, sc_b, sc_w, sc_r)]
                steps(v.tensor_tensor(outer, state, each(z, 32), ALU.mult))
                steps(v.tensor_reduce(sa, outer, AX.X, ALU.add))
                steps(v.tensor_tensor(state, state, each(w, 32), ALU.mult))
                steps(v.tensor_tensor(outer, over(sa, HD), each(bb, 32), ALU.mult))
                steps(v.tensor_tensor(state, state, outer, ALU.add))
                dve.wait_ge(s["vk"], i + 1)
                v.tensor_tensor(state, state, outer2, ALU.add).then_inc(s["vk_free"], 1)
                dve.wait_ge(s["vk_free"], i + 1)
                steps(v.tensor_tensor(outer, state, each(rr, 32), ALU.mult))
                last = v.tensor_reduce(sc_y[:, 32 * i:32 * i + 32], outer, AX.X, ALU.add)
                if i < DT - 1:
                    steps(last)
                else:
                    last.then_inc(s["scan_y"], 1)
            dve.wait_ge(s["y_back"], 16 * DB)
            norm_a(NPT)
            norm_b(NPT)
            norm_c(NPT)

        @block.scalar
        def _(act):
            a = nc.scalar
            act.wait_ge(s["zero"], 2)

            def prep_lora(t, b, u):
                n = rows_of(t)
                act.wait_ge(s["lora_T"], t + 1)
                a.activation(lora[0:HD, 0:n], bank[7][0:HD, 0:n], ACT.Tanh).then_inc(s["lora"], 1)
                a.copy(lora[HD:P, 0:n], bank[7][HD:P, 0:n]).then_inc(s["lora"], 1)
                act.wait_ge(s[f"loaded{b}"], 16 * LOADS * (u + 1))
                if not first(t):
                    act.wait_ge(s["conv"], t)
                a.activation(tz[0:n, 0:AW], cur[0:n, b, ZA0:B0], ACT.Tanh, scale=0.5)
                a.activation(tz[0:n, AW:], cur[0:n, b, ZB0:], ACT.Tanh, scale=0.5).then_inc(s["act"], 1)
                act.wait_ge(s["act"], t + 1)
                a.activation(tz[0:n], tz[0:n], ACT.Copy, bias=0.5, scale=0.5).then_inc(s["gates"], 1)

            def prep_sq(t):
                n = rows_of(t)
                act.wait_ge(s["kk"], t + 1)
                a.activation(sq[0:n], kk[0:n], ACT.Square).then_inc(s["sq"], 1)

            def prep_tanh(t):
                n = rows_of(t)
                act.wait_ge(s["wa_in"], t + 1)
                a.activation(wa[0:n], wa[0:n], ACT.Tanh, scale=0.5).then_inc(s["tanh"], 1)

            def prep_exps(t, b):
                act.wait_ge(s["cprev"], t + 1)
                a.activation(pinv[:], bank[4][:], ACT.Exp, scale=-1.0)
                a.activation(pc_[:], bank[4][:], ACT.Exp)
                a.activation(pend[:, b, :], bank[5][:, 0:HP * NCH], ACT.Exp)
                a.activation(pprev[:], pprev[:], ACT.Exp).then_inc(s["exps"], 1)

            def step(t, b, u):
                for j, dst in enumerate((0, 1, BT, KT)):
                    act.wait_ge(s[f"zrbk_T{j}"], t + 1)
                    src = bank[4 + j][:].rearrange("p (h n) -> p h n", h=HP)
                    if j < 2:
                        for e in range(2):
                            r_ = slice(HD * e, HD * e + HD)
                            m = a.copy(ZR[r_, e, :, j, :], src[r_])
                        m.then_inc(s["zrbk_out"], 1)
                    else:
                        a.copy(dst[:], src).then_inc(s["zrbk_out"], 1)
                act.wait_ge(s["av_mm"], t + 1)
                a.copy(za[:, b, 1, :, :], heads(bank[6][:])).then_inc(s["av"], 1)
                act.wait_ge(s["t1_T"], 2 * t + 1)
                a.copy(T[:, 0:4, :], bank[4][:].rearrange("p (h n) -> p h n", h=4)).then_inc(s["t1"], 1)
                act.wait_ge(s["t1_T"], 2 * t + 2)
                a.copy(T[:, 4:8, :], bank[5][:].rearrange("p (h n) -> p h n", h=4)).then_inc(s["t1"], 1)
                for lv in range(1, LEVELS - 1):
                    for g in range(2):
                        act.wait_ge(s["x_T"], 2 * ((L - 1) * t + lv - 1) + g + 1)
                        a.copy(X[:, 4 * g:4 * g + 4, :], bank[4 + g][:].rearrange("p (h n) -> p h n", h=4))\
                            .then_inc(s["x_out"], 1)
                    if lv == 1:
                        prep_lora(t + 1, 1 - b, u + b)
                    elif lv == 2:
                        prep_sq(t + 1)
                    elif lv == 3:
                        prep_tanh(t + 1)
                if not final(t):
                    prep_exps(t + 1, 1 - b)
                for g in range(2):
                    act.wait_ge(s["wu_mm"], 2 * t + g + 1)
                    a.copy(WU[:, 4 * g:4 * g + 4, :, :].rearrange("p h a d -> p (h a d)"), bank[6 + g][:]).then_inc(s["wu"], 1)
                act.wait_ge(s["yl_mm"], t + 1)
                a.copy(yl, bank[1][:]).then_inc(s["yl"], 1)
                for c in range(NCH):
                    act.wait_ge(s["g_mm"], NCH * t + c + 1)
                    a.copy(G[:, c, :, :], pairs(bank[G_BANK[c]])).then_inc(s["g_out"], 1)
                centred_sq(t)

            def centred_sq(t):
                n = rows_of(t)
                act.wait_ge(s["centred"], t + 1)
                a.activation(sq[0:n], y[0:n], ACT.Square).then_inc(s["ysq"], 1)

            prep_lora(0, 0, 0)
            prep_sq(0)
            prep_tanh(0)
            prep_exps(0, 0)
            walk(act, step)

            act.wait_ge(s["bonus"], NPT + 1)
            act.wait_ge(s["rkv"], NPT + 1)
            a.activation(pc_[0:NS], wa[0:NS, 0:AW], ACT.Exp).then_inc(s["act"], 1)
            a.mul(pinv[0:NS], kn[0:NS], -1.0).then_inc(s["act"], 1)
            act.wait_ge(s["act"], NPT + 3)
            act.wait_ge(s["gated"], NPT)
            for j, src in enumerate((pinv[0:NS], bv[0:NS], pc_[0:NS], kp[0:NS], ps[0:NS, 0, R0:K0], V[0:NS, 0, :])):
                for q in range(DB):
                    act.dma_start(scan_in[j, q].rearrange("h t d -> t h d"), heads(src[DT * q:DT * q + DT, :]))\
                        .then_inc(s["scan_out"], 16)
            act.wait_ge(s["scan_out"], 16 * 6 * DB)
            for j, dst in enumerate((sc_z, sc_b, sc_w, sc_k, sc_r)):
                for i in range(2):
                    act.dma_start(dst[64 * i:64 * i + 64, :],
                                  scan_in[j].rearrange("b h t d -> (b h) (t d)")).then_inc(s["scan_loaded"], 16)
            for i in range(2):
                act.dma_start(sc_v[64 * i:64 * i + 64, :].rearrange("p (t d) -> p t d", t=DT),
                              scan_in[5].rearrange("b h t (a d) -> a (b h) t d", a=2)[i])\
                    .then_inc(s["scan_loaded"], 16)
                act.dma_start(state[64 * i:64 * i + 64], state_rwkv.rearrange("b h (a i) j -> a (b h) i j", a=2)[i])\
                    .then_inc(s["scan_loaded"], 16)
            act.wait_ge(s["scan_y"], 1)
            for i in range(2):
                act.dma_start(scan_y.rearrange("b h t (a d) -> a (b h) t d", a=2)[i],
                              sc_y[64 * i:64 * i + 64, :].rearrange("p (t d) -> p t d", t=DT)).then_inc(s["scan_out"], 16)
                act.dma_start(state_s_out.rearrange("b h (a i) j -> a (b h) i j", a=2)[i], state[64 * i:64 * i + 64])\
                    .then_inc(s["state_out"], 16)
            act.wait_ge(s["scan_out"], 16 * (6 * DB + 2))
            for q in range(DB):
                act.dma_start(heads(y[DT * q:DT * q + DT, :]), scan_y[q].rearrange("h t d -> t h d"))\
                    .then_inc(s["y_back"], 16)
            act.wait_ge(s["s_T"], 1)
            act.wait_ge(s["stored"], 16 * (NPT + 2))
            a.copy(s_vk, bank[0][0:HD, :]).then_inc(s["s_vk"], 1)
            act.wait_ge(s["s_vk"], 1)
            act.dma_start(state_p_out.rearrange("h i j -> i h j"), s_vk.rearrange("p (h j) -> p h j", h=H))\
                .then_inc(s["state_out"], 16)
            centred_sq(NPT)

        @block.tensor
        def _(pe):
            mm, tr = nc.tensor.matmul, nc.tensor.transpose
            pe.wait_ge(s["cst"], 16 * CSTS)
            pe.wait_ge(s["zero"], 2)
            cols = [slice(h * HD, (h + 1) * HD) for h in range(H)]

            def prep_lora_T(t, b):
                n = rows_of(t)
                pe.wait_ge(s["shifted"], t + 1)
                tr(bank[7][:, 0:n], ps[0:n, b, L0:], ident[0:n, 0:n]).then_inc(s["lora_T"], 1)

            def prep_lora(t):
                n = rows_of(t)
                pe.wait_ge(s["lora"], 2 * t + 2)
                mm(bank[7][0:n, :], lora[:, 0:n], w2a2[:, 0, :], start=True, stop=True)
                mm(bank[6][0:n, :], lora[:, 0:n], w2a2[:, 1, :], start=True, stop=True).then_inc(s["lora_mm"], 1)

            def prep_cum(t):
                pe.wait_ge(s["ld"], t + 1)
                mm(bank[4][:], c_tri, wa[:, 0:AW], start=True, stop=True)
                for p in range(HP):
                    m = mm(bank[5][:, NCH * p:NCH * (p + 1)], wa[:, p * P:(p + 1) * P], c_chunk, start=True, stop=True)
                m.then_inc(s["cum"], 1)

            def step(t, b, u):
                v = V[:, b, :]
                z = za[:, b, 0, :, :].rearrange("p h d -> p (h d)")
                pe.wait_ge(s["zbk"], t + 1)
                pe.wait_ge(s["rt"], t + 1)
                if not first(t):
                    pe.wait_ge(s["y_sum"], t)
                pair = lambda src, p: src[:, p * P:(p + 1) * P]
                for j, src in enumerate((z, rt[:], bt[:, b, :], kt[:, b, :])):
                    for p in range(HP):
                        m = tr(bank[4 + j][:, p * P:(p + 1) * P], pair(src, p), ident[:])
                    m.then_inc(s[f"zrbk_T{j}"], 1)
                pe.wait_ge(s["zrbk_out"], 4 * t + 4)
                for h in range(H):
                    e, p = h % 2, h // 2
                    if h >= 4:
                        pe.wait_ge(s["masked"], H * t + h - 3)
                    zr = ZR[:, e, p, :, :].rearrange("p a b -> p (a b)")
                    mm(bank[h % 4][:, 0:2 * P], BT[:, p, :], zr, start=True, stop=True)
                    mm(bank[h % 4][:, 2 * P:], KT[:, p, :], zr, start=True, stop=True).then_inc(s["a_mm"], 1)
                pe.wait_ge(s["masked"], H * (t + 1))
                for h in range(H):
                    m = mm(bank[6][:, cols[h]], AM[:, h, 2, :], v[:, cols[h]], start=True, stop=True)
                m.then_inc(s["av_mm"], 1)
                for g in range(2):
                    pe.wait_ge(s["x1"], 2 * t + g + 1)
                    for h in range(4 * g, 4 * g + 4):
                        m = tr(bank[4 + g][:, (h % 4) * P:(h % 4 + 1) * P], X[:, h, :], ident[:])
                    m.then_inc(s["t1_T"], 1)
                for lv in range(1, LEVELS):
                    for g in range(2):
                        if lv == 1:
                            pe.wait_ge(s["t1"], 2 * t + g + 1)
                        else:
                            pe.wait_ge(s["t_add"], 2 * (L * t + lv - 2) + g + 1)
                        for h in range(4 * g, 4 * g + 4):
                            m = mm(bank[g][:, (h % 4) * P:(h % 4 + 1) * P], AM[:, h, 0, :], T[:, h, :], start=True, stop=True)
                        m.then_inc(s["y_mm"], 1)
                    if lv == 1:
                        pe.wait_ge(s["av"], t + 1)
                    for g in range(2):
                        pe.wait_ge(s["ym"], 2 * (L * t + lv - 1) + g + 1)
                        if lv > 1:
                            pe.wait_ge(s["x_out"], 2 * ((L - 1) * t + lv - 2) + g + 1)
                        for h in range(4 * g, 4 * g + 4):
                            o = bank[2 + g][:, (h % 4) * P:(h % 4 + 1) * P]
                            if lv < LEVELS - 1:
                                m = mm(o, X[:, h, :], Ym[:, h, :], start=True, stop=True)
                            else:
                                m = mm(o, Ym[:, h, :], X[:, h, :], start=True, stop=True)
                        m.then_inc(s["d_mm"], 1)
                    if lv < LEVELS - 1:
                        if lv == 1:
                            prep_lora_T(t + 1, 1 - b)
                        elif lv == 2:
                            prep_lora(t + 1)
                        for g in range(2):
                            pe.wait_ge(s["t_add"], 2 * (L * t + lv - 1) + g + 1)
                            for h in range(4 * g, 4 * g + 4):
                                m = tr(bank[4 + g][:, (h % 4) * P:(h % 4 + 1) * P], T[:, h, :], ident[:])
                            m.then_inc(s["x_T"], 1)
                    elif not final(t):
                        prep_cum(t + 1)
                pe.wait_ge(s["t_add"], 2 * L * (t + 1))
                pe.wait_ge(s["wa_in"], t + 2)
                for g in range(2):
                    for h in range(4 * g, 4 * g + 4):
                        m = mm(bank[6 + g][:, (h % 4) * P:(h % 4 + 1) * P], X[:, h, :],
                               za[:, b, :, h, :], start=True, stop=True)
                    m.then_inc(s["wu_mm"], 1)
                pe.wait_ge(s["wu"], 2 * t + 2)
                for h in range(H):
                    e, p = HD * (h % 2), h // 2
                    m = mm(bank[0][e:e + HD, p * P:(p + 1) * P], WU[:, h, 0, :], AM[:, h, 1, :], start=True, stop=True)
                m.then_inc(s["q_mm"], 1)
                for c in range(NCH):
                    cs = slice(c * CHUNK, (c + 1) * CHUNK)
                    for h in range(H):
                        e, p = HD * (h % 2), h // 2
                        m = mm(bank[M_BANK[c]][e:e + HD, p * HD:(p + 1) * HD], WU[cs, h, 0, :], bt[cs, b, cols[h]], start=True, stop=True)
                m.then_inc(s["m_mm"], 1)
                for h in range(H):
                    mm(bank[1][:, cols[h]], AM[:, h, 1, :], WU[:, h, 1, :], start=True, stop=False)
                    m = mm(bank[1][:, cols[h]], AM[:, h, 3, :], v[:, cols[h]], start=False, stop=True)
                m.then_inc(s["yl_mm"], 1)
                pe.wait_ge(s["cst"], 16 * CSTS)
                pe.wait_ge(s["q"], t + 1)
                if not final(t):
                    pe.wait_ge(s["exps"], t + 2)
                for c in range(NCH):
                    cs = slice(c * CHUNK, (c + 1) * CHUNK)
                    for h in range(H):
                        e, p = HD * (h % 2), h // 2
                        o = bank[G_BANK[c]][e:e + HD, p * HD:(p + 1) * HD]
                        mm(o, bt[cs, b, cols[h]], WU[cs, h, 1, :], start=True, stop=False)
                        m = mm(o, kt[cs, b, cols[h]], v[cs, cols[h]], start=False, stop=True)
                    m.then_inc(s["g_mm"], 1)
                for c in range(NCH):
                    cs = slice(c * CHUNK, (c + 1) * CHUNK)
                    pe.wait_ge(s["cst"], 16 * CSTS)
                    pe.wait_ge(s["s_new"], NCH * t + c + 1)
                    pe.wait_ge(s["m1"], NCH * t + c + 1)
                    for h in range(H):
                        e, p = HD * (h % 2), h // 2
                        m = mm(bank[3][e:e + HD, p * HD:(p + 1) * HD], M1[e:e + HD, c, p, :], S[e:e + HD, c, p, :],
                               start=True, stop=True)
                    m.then_inc(s["s_mm"], 1)
                    for h in range(H):
                        e, p = HD * (h % 2), h // 2
                        m = mm(bank[5 + h % 2][cs, p * HD:(p + 1) * HD], QT[e:e + HD, p, cs], S[e:e + HD, c, p, :], start=True, stop=True)
                    m.then_inc(s["y_cross"], 1)

            prep_lora_T(0, 0)
            prep_lora(0)
            prep_cum(0)
            walk(pe, step)
            pe.wait_ge(s["s_new"], NCH * NPT + 1)
            for p in range(HP):
                m = tr(bank[0][0:HD, p * P:(p + 1) * P], S[:, 0, p, :], ident[:])
            m.then_inc(s["s_T"], 1)


def project_out(nc, ph, ident, y_prompt, y_sample, width, w, x_prompt, x_sample, ln_g, ln_b, out_prompt, out_sample, xT=None):
    KW = width // P
    HALF = D // 2
    with ExitStack() as ctx:
        def sb(name, shape):
            return ctx.enter_context(nc.sbuf_tensor(f"{ph}_{name}", shape, FP32))

        ws = sb("w", [P, KW, D])
        g_b, b_b = sb("g", [P, D]), sb("b", [P, D])
        yin = sb("yin", [P, width])
        yT = sb("yT", [P, KW, P])
        res = sb("res", [P, SLOTS, D])
        stats, mv, spare = sb("stats", [P, 2, 6]), sb("mv", [P, 2]), sb("spare", [P, 1])
        rstd, half = sb("rstd", [P, 1]), sb("half", [P, 1])
        bank = [ctx.enter_context(nc.psum_tensor(f"{ph}_b{i}", [P, 512], FP32)) for i in range(8)]
        s = Sems(nc, ctx, ph, "w half y_loaded x_loaded0 x_loaded1 y_T yT0 yT1 products res var rstd scaled normed stored "
                              "x_T x_high x_split dve pool")
        block = ctx.enter_context(nc.Block())
        WS = 3

        def rows(last):
            return NS if last else P

        @block.sync
        def _(sp):
            def load_y(t, last=False):
                sp.wait_ge(s["y_T"], t + 1)
                sp.dma_start(yin[0:rows(last), :], y_sample if last else y_prompt[bass.ds(t * P, P), :])\
                    .then_inc(s["y_loaded"], 16)

            def load_x(t, b, last=False):
                sp.wait_ge(s["stored"], 16 * (t + 1))
                if xT is not None:
                    sp.wait_ge(s["x_T"], t + 1)
                xs = x_sample if last else x_prompt[bass.ds(t * P, P), :]
                sp.dma_start(res[0:rows(last), b, :], xs).then_inc(s[f"x_loaded{b}"], 16)

            def store(t, b, last=False):
                sp.wait_ge(s["normed"], t + 1)
                dst = out_sample if last else out_prompt[bass.ds(t * P, P), :]
                sp.dma_start(dst, res[0:rows(last), b, :]).then_inc(s["stored"], 16)

            sp.sem_inc(s["stored"], 16 * SLOTS)
            load_y(0)
            load_x(0, 0)
            sp.dma_start(ws[:], w.rearrange("(k p) n -> p k n", p=P)).then_inc(s["w"], 16)
            for dst, a in ((g_b, ln_g), (b_b, ln_b)):
                sp.dma_start(dst[:], a.rearrange("(o n) -> o n", o=1).broadcast_to([P, D])).then_inc(s["w"], 16)
            load_y(1)
            load_x(1, 1)

            def ahead(t, b, last=False):
                load_y(t + SLOTS, last)
                store(t, b)
                load_x(t + SLOTS, b, last)

            with sp.Fori(0, PAIRS - 1) as i:
                for b in range(SLOTS):
                    ahead(2 * i + b, b)
            ahead(NPT - 2, 0, last=True)
            store(NPT - 1, 1)
            store(NPT, 0, last=True)
            sp.wait_ge(s["stored"], 16 * (NTILE + 2))

        @block.tensor
        def _(pe):
            mm, tr = nc.tensor.matmul, nc.tensor.transpose
            pe.sem_inc(s["x_T"], SLOTS)
            pe.sem_inc(s["y_T"], 1)
            pe.sem_inc(s["products"], 1)
            pe.wait_ge(s["w"], 16 * WS)

            def products(t, b, u, last=False):
                n = rows(last)
                pe.wait_ge(s["y_loaded"], 16 * (t + 1))
                for k in range(KW):
                    m = tr(bank[k // 4][:, (k % 4) * P:(k % 4) * P + n], yin[0:n, k * P:(k + 1) * P], ident[0:n, 0:n])
                m.then_inc(s["y_T"], 1)
                pe.wait_ge(s["res"], t + 1)
                for j in range(2):
                    for k in range(KW):
                        if j == 0 and k % 4 == 0:
                            pe.wait_ge(s[f"yT{k // 4}"], t + 1)
                        m = mm(bank[2 + 2 * b + j][0:n, :], yT[:, k, 0:n], ws[:, k, j * HALF:(j + 1) * HALF],
                               start=(k == 0), stop=(k == KW - 1))
                m.then_inc(s["products"], 1)

            def transposes(t, b, last=False):
                if xT is None:
                    return
                n = rows(last)
                pe.wait_ge(s["normed"], t + 1)
                pe.wait_ge(s["x_split"], 2 * t + 2)
                for k in range(KD):
                    m = tr(bank[6 + k // 4][:, (k % 4) * P:(k % 4) * P + n], res[0:n, b, k * P:(k + 1) * P], ident[0:n, 0:n])
                m.then_inc(s["x_T"], 1)

            products(0, 0, 0)
            with pe.Fori(0, PAIRS - 1) as i:
                products(2 * i + 1, 1, i)
                transposes(2 * i, 0)
                products(2 * i + 2, 0, i + 1)
                transposes(2 * i + 1, 1)
            products(NPT - 1, 1, PAIRS - 1)
            transposes(NPT - 2, 0)
            products(NPT, 0, PAIRS, last=True)
            transposes(NPT - 1, 1)
            transposes(NPT, 0, last=True)

        def halves(t, n):
            at = lambda x, j: x[:, 4 * j:4 * j + 4, bass.ds(t * P, n)]
            src = lambda j: bank[6 + j][:].rearrange("p (k t) -> p k t", t=P)[:, :, 0:n]
            return [(src(j), at(xT[0], j), at(xT[1], j)) for j in range(2)]

        def in_turn(eng, tile, behind):
            tile(0, 0, 0)
            with eng.Fori(0, PAIRS - 1) as i:
                tile(2 * i + 1, 1, i)
                behind(2 * i, 0)
                tile(2 * i + 2, 0, i + 1)
                behind(2 * i + 1, 1)
            tile(NPT - 1, 1, PAIRS - 1)
            behind(NPT - 2, 0)
            tile(NPT, 0, PAIRS, last=True)
            behind(NPT - 1, 1)
            behind(NPT, 0, last=True)

        @block.vector
        def _(dve):
            v = nc.vector
            ch = Chain(dve, s["dve"], 4)
            dve.sem_inc(s["res"], SLOTS)
            dve.sem_inc(s["x_split"], 2)

            def tile(t, b, u, last=False):
                n = rows(last)
                ch.start(t)
                dve.wait_ge(s["products"], t + 2)
                dve.wait_ge(s[f"x_loaded{b}"], 16 * (u + 1))
                r = res[0:n, b, :]
                for j in range(2):
                    m = v.scalar_tensor_tensor(r[:, j * HALF:(j + 1) * HALF], r[:, j * HALF:(j + 1) * HALF], ALPHA,
                                               bank[2 + 2 * b + j][0:n, :], ALU.mult, ALU.add)
                    if j:
                        m.then_inc(s["res"], 1)
                        dve.wait_ge(s["res"], t + 1 + SLOTS)
                    else:
                        ch(m)
                ch(v.bn_stats(stats[0:n, 0, :], r[:, 0:HALF]))
                ch(v.bn_stats(stats[0:n, 1, :], r[:, HALF:]))
                v.memset(spare[:], 0.0)
                ch(v.bn_aggr(mv[0:n], stats[0:n].rearrange("p a b -> p (a b)")))
                v.tensor_scalar(mv[0:n, 1:2], mv[0:n, 1:2], LN_EPS, None, ALU.add).then_inc(s["var"], 1)
                dve.wait_ge(s["rstd"], t + 1)
                v.tensor_scalar(r, r, mv[0:n, 0:1], rstd[0:n], ALU.subtract, ALU.mult).then_inc(s["scaled"], 1)
                dve.wait_ge(s["scaled"], t + 1)
                ch.end()

            def behind(t, b, last=False):
                if xT is not None:
                    for j, (src, high, low) in enumerate(halves(t, rows(last))):
                        dve.wait_ge(s["x_high"], 2 * t + j + 1)
                        v.tensor_tensor(low, src, high.bitcast(FP32), ALU.subtract).then_inc(s["x_split"], 1)
            in_turn(dve, tile, behind)

        @block.scalar
        def _(act):
            def tile(t, b, u, last=False):
                n = rows(last)
                act.wait_ge(s["y_T"], t + 2)
                act.wait_ge(s["products"], t + 1)
                for j in range(KW // 4):
                    nc.scalar.copy(yT[:, 4 * j:4 * j + 4, 0:n], bank[j][:].rearrange("p (k t) -> p k t", t=P)[:, :, 0:n])\
                        .then_inc(s[f"yT{j}"], 1)

            def behind(t, b, last=False):
                if xT is not None:
                    act.wait_ge(s["x_T"], t + 1 + SLOTS)
                    for src, high, _ in halves(t, rows(last)):
                        nc.scalar.copy(high, src).then_inc(s["x_high"], 1)
            in_turn(act, tile, behind)

        @block.gpsimd
        def _(pool):
            g = nc.gpsimd
            g.memset(half[:], -0.5).then_inc(s["half"], 1)
            pool.wait_ge(s["half"], 1)
            pool.wait_ge(s["w"], 16 * WS)

            def tile(t, b, u, last=False):
                n = rows(last)
                r = res[0:n, b, :]
                pool.wait_ge(s["var"], t + 1)
                g.tensor_tensor(rstd[0:n], mv[0:n, 1:2], half[0:n], ALU.pow).then_inc(s["rstd"], 1)
                pool.wait_ge(s["scaled"], t + 1)
                g.tensor_tensor(r, r, g_b[0:n], ALU.mult).then_inc(s["pool"], 1)
                pool.wait_ge(s["pool"], t + 1)
                g.tensor_tensor(r, r, b_b[0:n], ALU.add).then_inc(s["normed"], 1)
            in_turn(pool, tile, lambda *a, **k: None)


C_QKV = 3 * NG * AW
DIL = (1, 4, 16)
SCALE = HD ** -0.5
NEG = -1e30
ST_W = AW + 2 * H


def window_constants():
    import numpy as np
    q, k = np.arange(P)[:, None], np.arange(2 * P)[None, :]
    dist = q + P - k
    return np.where((dist >= 0) & (dist <= P), 0.0, NEG).astype(np.float32)


def window_attention(nc, ident, p1, mask_in, stats_out, sw, beside):
    VS = 4
    HEADS = ((0, 1), (2, 3), (4, 5), (6, 7))

    with ExitStack() as ctx:
        def sb(name, shape):
            return ctx.enter_context(nc.sbuf_tensor(f"wa_{name}", shape, FP32))

        mask = sb("mask", [P, 2 * P])
        q_in, k_in = sb("q", [P, SLOTS, AW]), sb("k", [P, SLOTS, AW])
        v_in = sb("v", [P, VS, AW])
        qT = sb("qT", [P, SLOTS, 2, HP, P])
        kT = sb("kT", [P, VS, HP, P])
        sm = sb("sm", [P, 2, H, 2 * P])
        ex = sb("ex", [P, 2, H, 2 * P])
        mx, spare = sb("mx", [P, H]), sb("spare", [P, len(HEADS)])
        eT = sb("eT", [P, 2, 2, 2 * P])
        out = sb("out", [P, VS, ST_W])
        b_qk = ctx.enter_context(nc.psum_tensor("wa_qk", [P, 512], FP32))
        b_o = ctx.enter_context(nc.psum_tensor("wa_o", [P, 512], FP32))
        b_s = [ctx.enter_context(nc.psum_tensor(f"wa_s{i}", [P, 512], FP32)) for i in range(4)]
        b_e = [ctx.enter_context(nc.psum_tensor(f"wa_e{i}", [P, 512], FP32)) for i in range(2)]
        s = Sems(nc, ctx, "wa", "mask zero q_T k_T qT0 qT1 kT scores sm negmax ex e_T0 e_T1 eT0 eT1 values out "
                                "dve act loadqk0 loadqk1 loadv0 loadv1 loadv2 loadv3",
                 {f"stored{b}": sw[f"out_stored{b}"] for b in range(VS)})
        block = ctx.enter_context(nc.Block())

        def walk(eng, step, last):
            def four(n0, u, rows, has, before):
                for j in range(4):
                    step(n0 + j, j, u, has[j], before if j == 0 else has[j - 1], *rows(j))
            G0, G1, G2 = NPT // 4, 4, 4
            yes, no = True, False
            four(0, 0, lambda j: (j * P, 1), (no, yes, yes, yes), None)
            with eng.Fori(1, G0) as i:
                four(4 * i, i, lambda j: (i * 4 * P + j * P, 1), (yes,) * 4, yes)
            with eng.Fori(0, G1) as i:
                four(4 * i + NPT, i + G0, lambda j: (i + j * 4 * P, 4), (no, yes, yes, yes), yes)
            four(2 * NPT, G0 + G1, lambda j: (j, 16), (no,) * 4, yes)
            with eng.Fori(1, G2 - 1) as i:
                four(4 * i + 2 * NPT, i + G0 + G1, lambda j: (4 * i + j, 16), (no,) * 4, no)
            four(3 * NPT - 4, G0 + G1 + G2 - 1, lambda j: (4 * (G2 - 1) + j, 16), (no,) * 4, no)
            last(3 * NPT)

        def more(n):
            return not (isinstance(n, int) and n == 3 * NPT - 1)

        @block.sync
        def _(sp):
            sp.dma_start(mask[:], mask_in).then_inc(s["mask"], 16)

            def rows(tensor, j, row, d, c0, c1):
                if d == 4:
                    part = tensor[j * 4 * P:(j + 1) * 4 * P, c0:c1].rearrange("(i d) n -> d i n", d=d)
                    return part[bass.ds(row - j * 4 * P, 1)].rearrange("o i n -> (o i) n")
                if d == 16:
                    return tensor[:, c0:c1].rearrange("(i d) n -> d i n", d=d)[bass.ds(row, 1)].rearrange("o i n -> (o i) n")
                return tensor[bass.ds(row, P), c0:c1]

            def load(n, j, u, has, before, row, d):
                g = DIL.index(d)
                b = j % 2
                if before is not None:
                    if not isinstance(n, int) or n >= 2:
                        sp.wait_ge(s["k_T"], n - 1)
                for a, c in ((q_in, 0), (k_in, NG * AW)):
                    sp.dma_start(a[:, b, :], rows(p1, j, row, d, c + g * AW, c + (g + 1) * AW)).then_inc(s[f"loadqk{b}"], 16)
                if not isinstance(n, int) or n >= VS:
                    sp.wait_ge(s["values"], n - VS + 2)
                sp.dma_start(v_in[:, j, :], rows(p1, j, row, d, 2 * NG * AW + g * AW, 2 * NG * AW + (g + 1) * AW))\
                    .then_inc(s[f"loadv{j}"], 16)
            walk(sp, load, lambda n: None)

        @block.tensor
        def _(pe):
            mm, tr = nc.tensor.matmul, nc.tensor.transpose
            pe.wait_ge(s["mask"], 16)
            pe.wait_ge(s["zero"], 1)

            def turn(src, b, done):
                for p in range(HP):
                    m = tr(b_qk[:, p * P:(p + 1) * P], src[:, b, p * P:(p + 1) * P], ident[:])
                m.then_inc(s[done], 1)

            def turn_q(n, j, u):
                pe.wait_ge(s[f"loadqk{j % 2}"], 32 * (2 * u + j // 2 + 1))
                if not (isinstance(n, int) and n == 0):
                    pe.wait_ge(s["kT"], n)
                turn(q_in, j % 2, "q_T")

            def turn_k(n, j):
                pe.wait_ge(s["qT0"], n + 1)
                pe.wait_ge(s["qT1"], n + 1)
                turn(k_in, j % 2, "k_T")

            def scores(n, j, has, before, i):
                if i == 0:
                    pe.wait_ge(s["qT0"], n + 1)
                    pe.wait_ge(s["qT1"], n + 1)
                    pe.wait_ge(s["kT"], n + 1)
                if before is not None:
                    pe.wait_ge(s["sm"], H * (n - 1) + 2 * i + 2)
                for q, h in enumerate(HEADS[i]):
                    e, p = h % 2, h // 2
                    for c in range(0 if has else 1, 2):
                        m = mm(b_s[i][:, (2 * q + c) * P:(2 * q + c + 1) * P], qT[:, j % 2, e, p, :],
                               kT[:, j if c else (j - 1) % VS, p, :], start=True, stop=True)
                m.then_inc(s["scores"], 1)

            def turn_e(n, j, has, i):
                pe.wait_ge(s["ex"], H * n + 2 * i + 2)
                if not isinstance(n, int) or n:
                    pe.wait_ge(s[f"eT{i % 2}"], 2 * n + i // 2)
                elif i // 2:
                    pe.wait_ge(s[f"eT{i % 2}"], 1)
                for q, h in enumerate(HEADS[i]):
                    for c in range(0 if has else 1, 2):
                        m = tr(b_e[i % 2][:, (2 * q + c) * P:(2 * q + c + 1) * P], ex[:, j % 2, h, c * P:(c + 1) * P], ident[:])
                m.then_inc(s[f"e_T{i % 2}"], 1)

            def product(n, j, has, i):
                pe.wait_ge(s[f"eT{i % 2}"], 2 * n + i // 2 + 1)
                if i == 0 and not (isinstance(n, int) and n == 0):
                    pe.wait_ge(s["out"], n)
                for q, h in enumerate(HEADS[i]):
                    for c in range(0 if has else 1, 2):
                        vb = j if c else (j - 1) % VS
                        m = mm(b_o[:, h * HD:(h + 1) * HD], eT[:, i % 2, q, c * P:(c + 1) * P], v_in[:, vb, h * HD:(h + 1) * HD],
                               start=(c == 0 or not has), stop=(c == 1))
                if i == 3:
                    m.then_inc(s["values"], 1)

            def step(n, j, u, has, before, row, d):
                if before is None:
                    turn_q(0, 0, 0)
                    turn_k(0, 0)
                if more(n):
                    turn_q(n + 1, (j + 1) % 4, u + (j + 1) // 4)
                for i in range(len(HEADS)):
                    if before is not None:
                        turn_e(n - 1, (j - 1) % 4, before, i)
                        if i:
                            product(n - 1, (j - 1) % 4, before, i - 1)
                    scores(n, j, has, before, i)
                    if i == 1 and more(n):
                        turn_k(n + 1, (j + 1) % 4)
                if before is not None:
                    product(n - 1, (j - 1) % 4, before, 3)
                pe.wait_ge(s[f"loadv{j}"], 16 * (u + 1))

            def last(n):
                for i in range(len(HEADS)):
                    turn_e(n - 1, 3, False, i)
                    if i:
                        product(n - 1, 3, False, i - 1)
                product(n - 1, 3, False, 3)
            walk(pe, step, last)

        def copy_qT(eng, copy, n, j, e):
            r = slice(HD * e, HD * e + HD)
            eng.wait_ge(s["q_T"], n + 1)
            copy(qT[r, j % 2, e, :, :].rearrange("p a b -> p (a b)"), b_qk[r]).then_inc(s[f"qT{e}"], 1)

        def copy_eT(eng, copy, n, j, has, i):
            eng.wait_ge(s[f"e_T{i % 2}"], 2 * n + i // 2 + 1)
            if i < 2:
                if not (isinstance(n, int) and n == 0):
                    eng.wait_ge(s["values"], n)
            src = b_e[i % 2][:].rearrange("p (q c t) -> p q c t", q=2, c=2)
            dst = eT[:, i % 2, :, :].rearrange("p q (c t) -> p q c t", c=2)
            lo = 0 if has else 1
            copy(dst[:, :, lo:, :], src[:, :, lo:, :]).then_inc(s[f"eT{i % 2}"], 1)

        @block.vector
        def _(dve):
            v = nc.vector
            dve.wait_ge(s["mask"], 16)
            dve.wait_ge(s["zero"], 1)

            def copy_kT(n, j):
                dve.wait_ge(s["k_T"], n + 1)
                v.tensor_copy(kT[:, j, :, :].rearrange("p a b -> p (a b)"), b_qk[:]).then_inc(s["kT"], 1)

            def scores(n, j, u, has, i):
                lo = 0 if has else P
                dve.wait_ge(s["scores"], 4 * n + i + 1)
                v.memset(spare[:, i:i + 1], 0.0)
                for q, h in enumerate(HEADS[i]):
                    v.tensor_tensor_reduce(out=sm[:, j % 2, h, lo:], in0=b_s[i][:, q * 2 * P + lo:(q + 1) * 2 * P],
                                           in1=mask[:, lo:], scale=SCALE, scalar=NEG, op0=ALU.add, op1=ALU.max,
                                           accum_out=mx[:, h:h + 1]).then_inc(s["sm"], 1)
                dve.wait_ge(s["sm"], H * n + 2 * i + 2)
                if i == 0 and (not isinstance(n, int) or n >= VS):
                    dve.wait_ge(s[f"stored{j}"], 16 * u)
                h = HEADS[i][0]
                v.tensor_scalar(out[:, j, AW + h:AW + h + 2], mx[:, h:h + 2], -1.0, None, ALU.mult).then_inc(s["negmax"], 1)

            def step(n, j, u, has, before, row, d):
                if before is None:
                    copy_qT(dve, v.tensor_copy, 0, 0, 0)
                    copy_kT(0, 0)
                if more(n):
                    copy_qT(dve, v.tensor_copy, n + 1, (j + 1) % 4, 0)
                for i in range(len(HEADS)):
                    if before is not None and i % 2 == 0:
                        copy_eT(dve, v.tensor_copy, n - 1, (j - 1) % 4, before, i)
                    scores(n, j, u, has, i)
                    if i == 1 and more(n):
                        copy_kT(n + 1, (j + 1) % 4)

            def last(n):
                for i in (0, 2):
                    copy_eT(dve, v.tensor_copy, n - 1, 3, False, i)
            walk(dve, step, last)

        @block.scalar
        def _(act):
            a = nc.scalar
            beside(act)
            act.wait_ge(s["zero"], 1)

            def exps(n, j, has, i):
                lo = 0 if has else P
                act.wait_ge(s["negmax"], 4 * n + i + 1)
                for h in HEADS[i]:
                    a.activation(ex[:, j % 2, h, lo:], sm[:, j % 2, h, lo:], ACT.Exp, bias=out[:, j, AW + h:AW + h + 1],
                                 scale=1.0, accum_out=out[:, j, AW + H + h:AW + H + h + 1]).then_inc(s["ex"], 1)

            def copy_out(n, j):
                act.wait_ge(s["values"], n + 1)
                a.copy(out[:, j, 0:AW], b_o[:]).then_inc(s["out"], 1)

            def step(n, j, u, has, before, row, d):
                if before is None:
                    copy_qT(act, a.copy, 0, 0, 1)
                if more(n):
                    copy_qT(act, a.copy, n + 1, (j + 1) % 4, 1)
                for i in range(len(HEADS)):
                    if before is not None and i % 2:
                        copy_eT(act, a.copy, n - 1, (j - 1) % 4, before, i)
                        if i == 3:
                            copy_out(n - 1, (j - 1) % 4)
                    exps(n, j, has, i)

            def last(n):
                for i in (1, 3):
                    copy_eT(act, a.copy, n - 1, 3, False, i)
                copy_out(n - 1, 3)
            walk(act, step, last)

        @block.gpsimd
        def _(pool):
            nc.gpsimd.memset(qT[:].rearrange("p a b c d -> p (a b c d)"), 0.0).then_inc(s["zero"], 1)

            def store(n, j, u, has, before, row, d):
                g = DIL.index(d)
                pool.wait_ge(s["out"], n + 1)
                if d == 1:
                    dst = stats_out[bass.ds(row, P), g, :]
                elif d == 4:
                    dst = stats_out[j * 4 * P:(j + 1) * 4 * P, g, :].rearrange("(i d) n -> d i n", d=d)
                    dst = dst[bass.ds(row - j * 4 * P, 1)].rearrange("o i n -> (o i) n")
                else:
                    dst = stats_out[:, g, :].rearrange("(i d) n -> d i n", d=d)[bass.ds(row, 1)].rearrange("o i n -> (o i) n")
                pool.dma_start(dst, out[:, j, :]).then_inc(s[f"stored{j}"], 16)
            walk(pool, store, lambda n: None)
            for b in range(VS):
                pool.wait_ge(s[f"stored{b}"], 16 * 3 * NPT // VS)


def merge_windows(nc, stats, p1, p1_sample, o_sample, y_prompt, y_sample):
    Z0 = C_QKV
    with ExitStack() as ctx:
        def sb(name, shape):
            return ctx.enter_context(nc.sbuf_tensor(f"mw_{name}", shape, FP32))

        st = sb("st", [P, SLOTS, NG, ST_W])
        z, tz, zh, gate = sb("z", [P, SLOTS, AW]), sb("tz", [P, AW]), sb("zh", [P, AW]), sb("gate", [P, AW])
        low = sb("low", [P, H])
        w, wd = sb("w", [P, NG, H]), sb("wd", [P, NG, H])
        den = sb("den", [P, H])
        part, o = sb("part", [P, AW]), sb("o", [P, SLOTS, AW])
        s = Sems(nc, ctx, "mw", "loaded0 loaded1 tanh gate diff weights merged gated stored read dve pool")
        block = ctx.enter_context(nc.Block())

        @block.sync
        def _(sp):
            def load(t, b, last=False):
                if last:
                    sp.dma_start(o[0:NS, b, :], o_sample).then_inc(s[f"loaded{b}"], 16)
                    sp.dma_start(z[0:NS, b, :], p1_sample[:, :, Z0:].rearrange("b t n -> (b t) n")).then_inc(s[f"loaded{b}"], 16)
                else:
                    sp.dma_start(st[:, b, :, :], stats[bass.ds(t * P, P), :, :]).then_inc(s[f"loaded{b}"], 16)
                    sp.dma_start(z[:, b, :], p1[bass.ds(t * P, P), Z0:]).then_inc(s[f"loaded{b}"], 16)

            def store(t, b, last=False):
                sp.wait_ge(s["gated"], t + 1)
                if last:
                    sp.dma_start(y_sample, o[0:NS, b, :]).then_inc(s["stored"], 16)
                else:
                    sp.dma_start(y_prompt[bass.ds(t * P, P), :], o[:, b, :]).then_inc(s["stored"], 16)

            sp.sem_inc(s["stored"], 32)
            for b in range(SLOTS):
                load(b, b)
            with sp.Fori(0, PAIRS - 1) as i:
                for b in range(SLOTS):
                    sp.wait_ge(s["read"], 2 * i + b + 1)
                    sp.wait_ge(s["tanh"], 2 * i + b + 1)
                    load(2 * i + b + SLOTS, b)
                    sp.wait_ge(s["stored"], 16 * (2 * i + b + 2))
                    store(2 * i + b, b)
            sp.wait_ge(s["stored"], 16 * NPT)
            store(NPT - 2, 0)
            sp.wait_ge(s["stored"], 16 * (NPT - 1 + 2))
            load(NPT, 0, last=True)
            store(NPT - 1, 1)
            store(NPT, 0, last=True)
            sp.wait_ge(s["stored"], 16 * (NTILE + 2))

        @block.scalar
        def _(act):
            def gate_in(t, b, u):
                n = NS if u is PAIRS else P
                act.wait_ge(s[f"loaded{b}"], 32 * (u + 1))
                act.wait_ge(s["gate"], t + 1)
                nc.scalar.mul(zh[0:n], z[0:n, b, :], 0.5)
                nc.scalar.activation(tz[0:n], z[0:n, b, :], ACT.Tanh, scale=0.5).then_inc(s["tanh"], 1)

            def tile(t, b, u):
                gate_in(t, b, u)
                act.wait_ge(s["diff"], t + 1)
                nc.scalar.activation(w[:], w[:], ACT.Exp, scale=-1.0).then_inc(s["weights"], 1)
            each_tile(act, tile, tail=False)
            gate_in(NPT, 0, PAIRS)

        @block.vector
        def _(dve):
            v = nc.vector
            ch = Chain(dve, s["dve"], 10)

            def tile(t, b, u):
                ch.start(t)
                x = st[:, b, :, :]
                nm, dn = x[:, :, AW:AW + H], x[:, :, AW + H:]
                dve.wait_ge(s[f"loaded{b}"], 32 * (u + 1))
                ch(v.tensor_tensor(low[:], nm[:, 0, :], nm[:, 1, :], ALU.min))
                ch(v.tensor_tensor(low[:], low[:], nm[:, 2, :], ALU.min))
                v.tensor_tensor(w[:], nm, each(low[:], NG), ALU.subtract).then_inc(s["diff"], 1)
                dve.wait_ge(s["weights"], t + 1)
                ch(v.tensor_tensor(wd[:], w[:], dn, ALU.mult))
                ch(v.tensor_tensor(den[:], wd[:, 0, :], wd[:, 1, :], ALU.add))
                ch(v.tensor_tensor(den[:], den[:], wd[:, 2, :], ALU.add))
                ch(v.reciprocal(den[:], den[:]))
                ch(v.tensor_tensor(w[:], w[:], each(den[:], NG), ALU.mult))
                dve.wait_ge(s["stored"], 16 * (t + 1))
                for g in range(NG):
                    dst = part if g else o[:, b, :]
                    m = v.tensor_tensor(heads(dst if not g else part[:]), heads(x[:, g, 0:AW]), over(w[:, g, :], HD), ALU.mult)
                    if g < 2:
                        ch(m)
                    else:
                        m.then_inc(s["read"], 1)
                        dve.wait_ge(s["read"], t + 1)
                    if g == 1:
                        ch(v.tensor_tensor(o[:, b, :], o[:, b, :], part[:], ALU.add))
                v.tensor_tensor(o[:, b, :], o[:, b, :], part[:], ALU.add).then_inc(s["merged"], 1)
                dve.wait_ge(s["merged"], t + 1)
                ch.end()
            each_tile(dve, tile, tail=False)

        @block.gpsimd
        def _(pool):
            g = nc.gpsimd
            ch = Chain(pool, s["pool"], 1)
            pool.sem_inc(s["gate"], 1)

            def tile(t, b, u):
                n = NS if u is PAIRS else P
                ch.start(t)
                pool.wait_ge(s[f"loaded{b}"], 32 * (u + 1))
                pool.wait_ge(s["tanh"], t + 1)
                ch(g.tensor_tensor(tz[0:n], tz[0:n], zh[0:n], ALU.mult))
                g.tensor_tensor(gate[0:n], tz[0:n], zh[0:n], ALU.add).then_inc(s["gate"], 1)
                pool.wait_ge(s["gate"], t + 2)
                if u is not PAIRS:
                    pool.wait_ge(s["merged"], t + 1)
                ch.end()
                g.tensor_tensor(o[0:n, b, :], o[0:n, b, :], gate[0:n], ALU.mult).then_inc(s["gated"], 1)
            each_tile(pool, tile)


def sample_constants():
    import numpy as np
    t = np.tile(np.arange(DT), H)[:, None]
    m = np.arange(P)[None, :]
    add = lambda ok: np.where(ok, 0.0, NEG).astype(np.float32)
    old = [add((t % 4 == r) & (r + 4 * m >= t)) for r in range(4)]
    old += [add((t == r) & (m >= 0)) for r in range(8)]
    new = np.zeros((DB, H * DT, P + NG * NS), np.float32)
    col = np.arange(NS)[None, :]
    for b in range(DB):
        parts = [add(m >= t)]
        for d in DIL:
            parts.append(add((col // DT == b) & (col % DT <= t) & ((t - col % DT) % d == 0)))
        new[b] = np.concatenate(parts, axis=1)
    row = np.arange(P)[:, None]
    own = row // DT % H == np.arange(AW)[None, :] // HD
    token = row % DT == np.arange(DT)[None, :]
    return np.concatenate(old, axis=1), new, np.concatenate([own, token], axis=1).astype(np.float32)


def sample_attention(nc, ident, p1s, caches, old_mask, new_mask, own_in, o_out):
    R = H * DT
    NQ = 3
    QW = 4 * P
    NEW_W = P + NG * NS
    COLS = NQ * QW + NEW_W
    N_OLD = 13
    with ExitStack() as ctx:
        def sb(name, shape):
            return ctx.enter_context(nc.sbuf_tensor(f"sa_{name}", shape, FP32))

        K, V = sb("K", [P, SLOTS, N_OLD, AW]), sb("V", [P, SLOTS, N_OLD, AW])
        Vn = sb("Vn", [P, NG, AW])
        kqn = sb("kqn", [NS, NG, AW])
        Qall = sb("Qall", [P, DB, NG * HP * R])
        Q = sb("Q", [P, NG, HP, R])
        KnT = sb("KnT", [P, NG, HP, NS])
        KT = sb("KT", [P, HP, QW])
        om = sb("om", [R, NQ * QW])
        nm = sb("nm", [R, SLOTS, NEW_W])
        sm, ex = sb("sm", [R, COLS]), sb("ex", [R, COLS])
        mx, neg, den, rden = sb("mx", [R, 4]), sb("neg", [R, 1]), sb("den", [R, 1]), sb("rden", [R, 1])
        spare = sb("spare", [R, 1])
        ET = sb("ET", [P, 16, R])
        own = sb("own", [P, AW + DT])
        prod = sb("prod", [P, AW])
        y = sb("y", [DT, SLOTS, AW])
        bank = [ctx.enter_context(nc.psum_tensor(f"sa_b{i}", [P, 512], FP32)) for i in range(8)]
        s = Sems(nc, ctx, "sa", "in zero q_T q_done kn_T kn_done K0 K1 V0 V1 nm0 nm1 K_T kt0 kt1 q_copied scores sm "
                                "max ex rden scaled e_T e0 e1 masked selected out stored0 stored1 act values k_read")
        block = ctx.enter_context(nc.Block())
        c0, c1, c2 = caches

        def walk(eng, step, finish):
            step(0, 0, 0)
            step(1, 1, 0)
            with eng.Fori(1, DB // 2) as i:
                for slot in range(2):
                    step(2 * i + slot, slot, i)
            finish()

        def first(b):
            return isinstance(b, int) and b == 0

        @block.sync
        def _(sp):
            for g in range(NG):
                sp.dma_start(kqn[:, g, :], p1s[:, :, g * AW:(g + 1) * AW].rearrange("b t n -> (b t) n")).then_inc(s["in"], 16)
            sp.dma_start(om[:], old_mask).then_inc(s["in"], 16)
            sp.dma_start(own[:], own_in).then_inc(s["in"], 16)
            sp.wait_ge(s["zero"], 3)
            for g in range(NG):
                c = (2 * NG + g) * AW
                sp.dma_start(Vn[0:NS, g, :], p1s[:, :, c:c + AW].rearrange("b t n -> (b t) n")).then_inc(s["in"], 16)

            def rows(b, which):
                flat = lambda c: c[bass.ds(b, 1), :, which, :, :]
                x1 = flat(c1).rearrange("o (m r) h d -> m (o r) (h d)", r=4)
                x2 = flat(c2).rearrange("o (m r) h d -> m (o r) (h d)", r=16)[:, 0:8, :]
                x0 = flat(c0).rearrange("o m h d -> m o (h d)")
                return x1, x2, x0

            def load(b, slot, u):
                for (lo, hi), src in zip(((0, 4), (4, 12), (12, 13)), rows(b, 0)):
                    sp.dma_start(K[:, slot, lo:hi, :], src).then_inc(s[f"K{slot}"], 16)
                sp.dma_start(nm[:, slot, :], new_mask[bass.ds(b, 1), :, :].rearrange("o r n -> (o r) n")).then_inc(s[f"nm{slot}"], 16)

            def load_v(b, slot):
                for (lo, hi), src in zip(((0, 4), (4, 12), (12, 13)), rows(b, 1)):
                    sp.dma_start(V[:, slot, lo:hi, :], src).then_inc(s[f"V{slot}"], 16)

            sp.wait_ge(s["q_done"], 2 * NG)
            for g in range(NG):
                c = (NG + g) * AW
                sp.dma_start(kqn[:, g, :], p1s[:, :, c:c + AW].rearrange("b t n -> (b t) n")).then_inc(s["in"], 16)
            for b in range(2):
                load(b, b, 0)
                load_v(b, b)
            with sp.Fori(0, DB // 2 - 1) as i:
                for slot in range(2):
                    sp.wait_ge(s["zero"], 3)
                    sp.wait_ge(s["sm"], 4 * (2 * i + slot + 1))
                    load(2 * i + slot + 2, slot, i + 1)
                    sp.wait_ge(s["values"], 2 * i + slot + 1)
                    load_v(2 * i + slot + 2, slot)

        @block.gpsimd
        def _(pool):
            nc.gpsimd.memset(Qall[:].rearrange("p a b -> p (a b)"), 0.0).then_inc(s["zero"], 1)
            nc.gpsimd.memset(Vn[:].rearrange("p a b -> p (a b)"), 0.0).then_inc(s["zero"], 1)
            nc.gpsimd.memset(ET[:].rearrange("p a b -> p (a b)"), 0.0).then_inc(s["zero"], 1)
            pool.wait_ge(s["zero"], 3)

            def own(b, slot, u):
                pool.wait_ge(s["scores"], 4 * b + 1)
                nc.gpsimd.tensor_copy(Q[:].rearrange("p g h r -> p (g h r)"),
                                      Qall[:, bass.ds(b, 1), :].rearrange("p o n -> p (o n)")).then_inc(s["q_copied"], 1)
            pool.wait_ge(s["q_done"], 2 * NG)
            with pool.Fori(0, DB // 2) as i:
                for slot in range(2):
                    own(2 * i + slot, slot, i)

        @block.tensor
        def _(pe):
            mm, tr = nc.tensor.matmul, nc.tensor.transpose
            pe.wait_ge(s["in"], 16 * (2 * NG + 2))
            for g in range(NG):
                for p in range(HP):
                    m = tr(bank[g][:, p * NS:(p + 1) * NS], kqn[:, g, p * P:(p + 1) * P], ident[0:NS, 0:NS])
                m.then_inc(s["q_T"], 1)
            pe.wait_ge(s["in"], 16 * (3 * NG + 2))
            for g in range(NG):
                for p in range(HP):
                    m = tr(bank[4 + g][:, p * NS:(p + 1) * NS], kqn[:, g, p * P:(p + 1) * P], ident[0:NS, 0:NS])
                m.then_inc(s["kn_T"], 1)
            pe.wait_ge(s["q_done"], 2 * NG)
            pe.wait_ge(s["kn_done"], NG)
            pe.sem_inc(s["scores"], 1)

            def turn_e(b, half):
                pe.wait_ge(s["zero"], 3)
                pe.wait_ge(s["scaled"], b + 1)
                if half and not first(b):
                    pe.wait_ge(s["out"], b)
                for j in range(8 * half, 8 * half + 8):
                    o = bank[6 + half][:, (j % 8) * R:(j % 8 + 1) * R]
                    if j < N_OLD:
                        m = tr(o, ex[:, j * P:(j + 1) * P], ident[0:R, 0:R])
                    else:
                        c = N_OLD * P + (j - N_OLD) * NS
                        m = tr(o[0:NS, :], ex[:, c:c + NS], ident[0:R, 0:R])
                m.then_inc(s["e_T"], 1)

            def values(b, slot, u):
                pe.wait_ge(s[f"V{slot}"], 48 * (u + 1))
                pe.wait_ge(s["e0"], b + 1)
                pe.wait_ge(s["e1"], b + 1)
                for j in range(16):
                    e = R * (j % 2)
                    m = mm(bank[4][e:e + R, :], ET[:, j, :], V[:, slot, j, :] if j < N_OLD else Vn[:, j - N_OLD, :],
                           start=(j < 2), stop=(j >= 14))
                m.then_inc(s["values"], 1)

            def select(b):
                pe.wait_ge(s["zero"], 3)
                pe.wait_ge(s["masked"], b + 1)
                mm(bank[7][0:DT, :], own[:, AW:], prod[:], start=True, stop=True).then_inc(s["selected"], 1)

            def finish():
                turn_e(DB - 1, 0)
                select(DB - 2)
                turn_e(DB - 1, 1)
                values(DB - 1, 1, DB // 2 - 1)
                select(DB - 1)

            def sequence(b, slot, u):
                pe.wait_ge(s[f"K{slot}"], 48 * (u + 1))
                pe.wait_ge(s["q_copied"], b + 1)

                def score(q):
                    g = 1 if q == 0 else 2 if q < NQ else 0
                    pe.wait_ge(s["kt0"], 4 * b + q + 2)
                    pe.wait_ge(s["kt1"], 4 * b + q + 2)
                    width = QW if q < NQ else P
                    o = bank[4 + q % 2]
                    if q >= 2:
                        pe.wait_ge(s["sm"], 4 * b + q - 1)
                    elif not first(b):
                        pe.wait_ge(s["sm"], 4 * b)
                        if q == 0 and not (isinstance(b, int) and b == 1):
                            pe.wait_ge(s["masked"], b - 1)
                    for p in range(HP):
                        m = mm(o[0:R, 0:width], Q[:, g, p, :], KT[:, p, 0:width], start=(p == 0), stop=(p == HP - 1))
                    if q == NQ:
                        for g in range(NG):
                            for p in range(HP):
                                m = mm(o[0:R, P + g * NS:P + (g + 1) * NS], Q[:, g, p, :], KnT[:, g, p, :],
                                       start=(p == 0), stop=(p == HP - 1))
                    m.then_inc(s["scores"], 1)

                for q in range(NQ + 1):
                    n = 4 if q < NQ else 1
                    pe.wait_ge(s["kt0"], 4 * b + q + 1)
                    pe.wait_ge(s["kt1"], 4 * b + q + 1)
                    for p in range(HP):
                        for j in range(n):
                            m = tr(bank[p][:, j * P:(j + 1) * P], K[:, slot, 4 * q + j, p * P:(p + 1) * P], ident[:])
                    m.then_inc(s["K_T"] if q < NQ else s["k_read"], 1)
                    if q in (1, 2) and not first(b):
                        turn_e(b - 1, q - 1)
                    score(q)
                    if q == 0 and not (isinstance(b, int) and b < 2):
                        select(b - 2)
                if not first(b):
                    pe.wait_ge(s["sm"], 4 * b + 3)
                    values(b - 1, 1 - slot, u if slot else u - 1)
            walk(pe, sequence, finish)

        def copy_kt(eng, copy, b, j):
            for q in range(NQ + 1):
                width = QW if q < NQ else P
                if q < NQ:
                    eng.wait_ge(s["K_T"], NQ * b + q + 1)
                else:
                    eng.wait_ge(s["k_read"], b + 1)
                eng.wait_ge(s["scores"], 4 * b + q + 1)
                for p in (2 * j, 2 * j + 1):
                    m = copy(KT[:, p, 0:width], bank[p][:, 0:width])
                m.then_inc(s[f"kt{j}"], 1)
                yield q

        @block.vector
        def _(dve):
            v = nc.vector
            dve.wait_ge(s["zero"], 3)
            dve.wait_ge(s["in"], 16 * (2 * NG + 2))
            for g in range(NG):
                dve.wait_ge(s["q_T"], g + 1)
                for e in range(2):
                    for p in range(HP):
                        h = 2 * p + e
                        dst = Qall[HD * e:HD * e + HD].rearrange("p b (g h r) -> p g h b r", g=NG, h=HP)[:, g, p, :, h * DT:(h + 1) * DT]
                        m = v.tensor_copy(dst, bank[g][HD * e:HD * e + HD, p * NS:(p + 1) * NS].rearrange("p (b t) -> p b t", t=DT))
                    m.then_inc(s["q_done"], 1)
            dve.sem_inc(s["kt0"], 1)

            def weights(b):
                dve.wait_ge(s["ex"], b + 1)
                v.reciprocal(rden[:], den[:]).then_inc(s["rden"], 1)
                dve.wait_ge(s["rden"], b + 1)
                v.tensor_scalar(ex[:], ex[:], rden[:], None, ALU.mult).then_inc(s["scaled"], 1)

            def copy_e(b):
                dve.wait_ge(s["e_T"], 2 * b + 1)
                if not first(b):
                    dve.wait_ge(s["values"], b)
                v.tensor_copy(ET[:, 0:8, :].rearrange("p a b -> p (a b)"), bank[6][:]).then_inc(s["e0"], 1)

            def keep_own(b):
                dve.wait_ge(s["values"], b + 1)
                v.tensor_tensor(prod[:], bank[4][:], own[:, 0:AW], ALU.mult).then_inc(s["masked"], 1)

            def out(b, slot, u):
                dve.wait_ge(s["selected"], b + 1)
                dve.wait_ge(s[f"stored{slot}"], 16 * (u + 1))
                v.tensor_copy(y[:, slot, :], bank[7][0:DT, :]).then_inc(s["out"], 1)

            def sequence(b, slot, u):
                copies = copy_kt(dve, v.tensor_copy, b, 0)
                for q in range(NQ + 1):
                    next(copies)
                    if q == 0 and not first(b):
                        weights(b - 1)
                    elif q == 1 and not first(b):
                        copy_e(b - 1)
                    dve.wait_ge(s["scores"], 4 * b + q + 2)
                    if q == 0:
                        dve.wait_ge(s[f"nm{slot}"], 16 * (u + 1))
                    v.memset(spare[:], 0.0)
                    width = QW if q < NQ else NEW_W
                    mask = om[:, q * QW:q * QW + QW] if q < NQ else nm[:, slot, :]
                    v.tensor_tensor_reduce(out=sm[:, q * QW:q * QW + width], in0=bank[4 + q % 2][0:R, 0:width], in1=mask,
                                           scale=SCALE, scalar=NEG, op0=ALU.add, op1=ALU.max,
                                           accum_out=mx[:, q:q + 1]).then_inc(s["sm"], 1)
                    if q == 0 and not (isinstance(b, int) and b < 2):
                        out(b - 2, slot, u - 1)
                dve.wait_ge(s["sm"], 4 * b + 4)
                v.tensor_reduce(neg[:], mx[:], AX.X, ALU.max, negate=True).then_inc(s["max"], 1)
                if not first(b):
                    keep_own(b - 1)

            def finish():
                weights(DB - 1)
                copy_e(DB - 1)
                out(DB - 2, 0, DB // 2 - 1)
                keep_own(DB - 1)
                out(DB - 1, 1, DB // 2 - 1)
            walk(dve, sequence, finish)

        @block.scalar
        def _(act):
            a = nc.scalar
            for g in range(NG):
                act.wait_ge(s["kn_T"], g + 1)
                a.copy(KnT[:, g, :, :].rearrange("p h r -> p (h r)"), bank[4 + g][:, 0:HP * NS]).then_inc(s["kn_done"], 1)
            act.sem_inc(s["kt1"], 1)
            act.wait_ge(s["zero"], 3)

            def copy_e(b):
                act.wait_ge(s["e_T"], 2 * b + 2)
                if not first(b):
                    act.wait_ge(s["values"], b)
                a.copy(ET[:, 8:13, :].rearrange("p a b -> p (a b)"), bank[7][:, 0:5 * R])
                a.copy(ET[0:NS, 13:16, :].rearrange("p a b -> p (a b)"), bank[7][0:NS, 5 * R:]).then_inc(s["e1"], 1)

            def sequence(b, slot, u):
                for q in copy_kt(act, a.copy, b, 1):
                    if q == 1 and not (isinstance(b, int) and b < 2):
                        store(b - 2, slot)
                    if q == 2 and not first(b):
                        copy_e(b - 1)
                act.wait_ge(s["max"], b + 1)
                a.activation(ex[:], sm[:], ACT.Exp, bias=neg[:], scale=1.0, accum_out=den[:]).then_inc(s["ex"], 1)
            def store(b, slot):
                act.wait_ge(s["out"], b + 1)
                act.dma_start(o_out[bass.ds(b * DT, DT), :], y[:, slot, :]).then_inc(s[f"stored{slot}"], 16)

            def finish():
                copy_e(DB - 1)
                store(DB - 2, 0)
                store(DB - 1, 1)
            for slot in range(SLOTS):
                act.sem_inc(s[f"stored{slot}"], 16)
            walk(act, sequence, finish)
            for slot in range(SLOTS):
                act.wait_ge(s[f"stored{slot}"], 16 * (1 + DB // 2))


ARGS = ("x_prompt x_sample state_rwkv state_shift state_conv cache_kv_w128 cache_kv_w512 cache_kv_w2048 "
        "even_w_in even_w_out rwkv_mu rwkv_w0 rwkv_w2 rwkv_a0 rwkv_a2 rwkv_k_k rwkv_k_a rwkv_r_k rwkv_gn_g "
        "rwkv_gn_b conv_w odd_w_in odd_w_out ln_g ln_b").split()
WINDOWS = (128, 512, 2048)
OUTS = {
    "y_prompt": (1, SEQ, D), "y_sample": (DB, DT, D),
    "rwkv_prompt": (1, 1, H, HD, HD), "rwkv_sample": (1, DB, H, HD, HD),
    "shift_prompt": (1, 1, SHIFT_W), "shift_sample": (1, DB, SHIFT_W),
    "conv_prompt": (1, 1, 2, AW), "conv_sample": (1, DB, 2, AW),
}
for _w in WINDOWS:
    OUTS[f"kv{_w}_prompt"] = (1, 1, _w, 2, H, HD)
    OUTS[f"kv{_w}_sample"] = (1, DB, _w, 2, H, HD)


def decoder_step(nc, a, o, c):
    scratch = lambda name, *shape: nc.dram_tensor(f"s_{name}", shape, FP32, kind="Internal").ap()
    p_pad, ps_pad = scratch("p0", PAD + SEQ, EVEN_W), scratch("p0s", DB, PAD + DT, EVEN_W)
    y0, y0s = scratch("y0", SEQ, EVEN_MIX), scratch("y0s", NS, EVEN_MIX)
    scan_in, scan_y = scratch("scan_in", 6, DB, H, DT, HD), scratch("scan_y", DB, H, DT, HD)
    x1, x1s = scratch("x1", SEQ, D), scratch("x1s", NS, D)
    p1, p1s = scratch("p1", SEQ, ODD_W), scratch("p1s", DB, DT, ODD_W)
    stats, o1s = scratch("stats", SEQ, NG, ST_W), scratch("o1s", NS, AW)
    y1, y1s = scratch("y1", SEQ, AW), scratch("y1s", NS, AW)
    caches = [a[f"cache_kv_w{w}"][0] for w in WINDOWS]
    kv_s = [o[f"kv{w}_sample"][0] for w in WINDOWS]
    kv_p = [o[f"kv{w}_prompt"][0, 0] for w in WINDOWS]
    PIECES = 8

    with ExitStack() as ctx:
        ident = ctx.enter_context(nc.sbuf_tensor("ident", [P, P], FP32))
        sw = {n: ctx.enter_context(nc.semaphore(n)) for n in
              "padded ei_w_loaded0 ei_w_loaded1 oi_w_loaded0 oi_w_loaded1 conv_out conv_s_out "
              "out_stored0 out_stored1 out_stored2 out_stored3".split()}
        kv_stored = ctx.enter_context(nc.semaphore("kv_stored"))

        def shift_caches(eng, piece):
            for w, cache, out in zip(WINDOWS, caches, kv_s):
                rows = (w - DT) // PIECES
                lo = piece * rows
                eng.dma_start(out[:, bass.ds(lo, rows)].rearrange("b r k h d -> b r (k h d)"),
                                  cache[:, bass.ds(lo + DT, rows)].rearrange("b r k h d -> b r (k h d)"))\
                       .then_inc(kv_stored, 16)

        def new_keys(eng):
            for g, w in enumerate(WINDOWS):
                for kv in range(2):
                    cols = slice(((1 + kv) * NG + g) * AW, ((1 + kv) * NG + g + 1) * AW)
                    eng.dma_start(kv_p[g][:, kv].rearrange("r h d -> r (h d)"), p1[SEQ - w:, cols]).then_inc(kv_stored, 16)
                    eng.dma_start(kv_s[g][:, w - DT:, kv].rearrange("b r h d -> b r (h d)"), p1s[:, :, cols])\
                       .then_inc(kv_stored, 16)

        KV_STORES = NG * PIECES + 4 * NG
        with nc.sbuf_tensor("x_high", [P, KD, NTOK], FP32R) as x_high, nc.sbuf_tensor("x_low", [P, KD, NTOK], FP32R) as x_low:
            transpose_in(nc, a["x_prompt"], a["x_sample"], x_high, x_low, ident, p_pad, ps_pad, a["state_shift"][0], a["state_conv"][0], sw)
            project_in(nc, "ei", x_high, x_low, a["even_w_in"][0], EVEN_W // 16, 16, p_pad[PAD:], ps_pad[:, PAD:], sw, shift_caches)
        rw = [a[f"rwkv_{n}"][0] for n in "mu w0 w2 a0 a2 k_k k_a r_k gn_g gn_b".split()]
        even_mix(nc, ident, p_pad, ps_pad, c["rwkv"], a["state_rwkv"][0], rw, a["conv_w"][0], y0, y0s, scan_in, scan_y,
                 o["rwkv_prompt"][0, 0], o["rwkv_sample"][0], o["shift_prompt"][0], o["shift_sample"][0],
                 o["conv_prompt"][0, 0], o["conv_sample"][0], sw)
        with nc.sbuf_tensor("x1_high", [P, KD, NTOK], FP32R) as x1_high, nc.sbuf_tensor("x1_low", [P, KD, NTOK], FP32R) as x1_low:
            project_out(nc, "eo", ident, y0, y0s, EVEN_MIX, a["even_w_out"][0], a["x_prompt"][0],
                        a["x_sample"].rearrange("b t d -> (b t) d"), a["ln_g"][0], a["ln_b"][0], x1, x1s, (x1_high, x1_low))
            project_in(nc, "oi", x1_high, x1_low, a["odd_w_in"][0], ODD_W // 16, 16, p1, p1s, sw)
        window_attention(nc, ident, p1, c["window"], stats, sw, new_keys)
        sample_attention(nc, ident, p1s, caches, c["sample_old"], c["sample_new"], c["sample_own"], o1s)
        merge_windows(nc, stats, p1, p1s, o1s, y1, y1s)
        project_out(nc, "oo", ident, y1, y1s, AW, a["odd_w_out"][0], x1, x1s, a["ln_g"][1], a["ln_b"][1],
                    o["y_prompt"][0], o["y_sample"].rearrange("b t d -> (b t) d"))
        with nc.Block() as block:
            @block.sync
            def _(sp):
                sp.wait_ge(kv_stored, 16 * KV_STORES)


EVEN_MIX = 2 * AW


def kernel(**inputs):
    import numpy as np
    import concourse.bacc as bacc
    from concourse.bass_utils import run_bass_kernel_spmd

    nc = bacc.Bacc("TRN2", target_bir_lowering=False, num_devices=1)
    sample_old, sample_new, sample_own = sample_constants()
    constants = {"rwkv": rwkv_constants(), "window": window_constants(), "sample_old": sample_old,
                 "sample_new": sample_new, "sample_own": sample_own}
    arrays = {f"in_{n}": np.ascontiguousarray(inputs[n]) for n in ARGS}
    arrays.update({f"const_{n}": v for n, v in constants.items()})
    aps = {n: nc.dram_tensor(n, v.shape, FP32, kind="ExternalInput").ap() for n, v in arrays.items()}
    outs = {n: nc.dram_tensor(f"out_{n}", shape, FP32, kind="ExternalOutput").ap() for n, shape in OUTS.items()}
    decoder_step(nc, {n: aps[f"in_{n}"] for n in ARGS}, outs, {n: aps[f"const_{n}"] for n in constants})
    r = run_bass_kernel_spmd(nc, [arrays], core_ids=[0]).results[0]
    return tuple(r[f"out_{n}"] for n in OUTS)
```
